# Optimizing a Trainium2 kernel written in Bass

```python
import math
import jax
import jax.numpy as jnp
from jax import lax
import numpy as np

D_MODEL = 1024
BATCH = 1
SEQ = 256
DEPTH = 1
DEC_BATCH = 8
DEC_SEQ = 1
PAST_LEN = 1024
PAGE_SIZE = 128

HEAD_DIM = 64
NSA_HEADS = 8
NSA_GROUPS = 2
NSA_HPG = NSA_HEADS // NSA_GROUPS
CMP_BLK = 32
CMP_STRIDE = 16
SEL_BLK = 64
N_SEL = 16
WINDOW = 512
MOBA_HEADS = 8
MOBA_BLK = 256
MOBA_TOPK = 3
N_BUCKETS = 32
MAX_DISTANCE = 1024
PEER_HEADS = 8
PEER_N_KEYS = 128
PEER_HALF = 128
PEER_TOPK = 16
N_EXPERTS = PEER_N_KEYS * PEER_N_KEYS
NSA_QB = 64
MOBA_QB = 16
PEER_BLK = 256
DN_ALPHA = (2 * DEPTH) ** 0.25
DN_BETA = (8 * DEPTH) ** -0.25
LN_EPS = 1e-5
NEG = -1e30
SPLIT_SIZES = (NSA_HEADS * HEAD_DIM, 4 * NSA_GROUPS * HEAD_DIM, 2 * NSA_GROUPS * HEAD_DIM,
               3 * NSA_HEADS, MOBA_HEADS * HEAD_DIM, 2 * MOBA_HEADS * HEAD_DIM, 2 * D_MODEL)
N_IN = sum(SPLIT_SIZES)

kernel_name = 'hybrid_nsa_moba_peer_step'

def t5_bucket(dist):
    n = jnp.maximum(dist, 0)
    max_exact = N_BUCKETS // 2
    nf = jnp.maximum(n, 1).astype(jnp.float32)
    large = max_exact + (jnp.log(nf / max_exact) / math.log(MAX_DISTANCE / max_exact)
                         * (N_BUCKETS - max_exact)).astype(jnp.int32)
    return jnp.where(n < max_exact, n, jnp.minimum(large, N_BUCKETS - 1)).astype(jnp.int32)

def masked_softmax(s, mask):
    return jax.nn.softmax(jnp.where(mask, s, NEG), axis=-1)

def layer_norm(x, g, b):
    xf = x.astype(jnp.float32)
    mu = xf.mean(-1, keepdims=True)
    var = jnp.square(xf - mu).mean(-1, keepdims=True)
    y = (xf - mu) * lax.rsqrt(var + LN_EPS) * g.astype(jnp.float32) + b.astype(jnp.float32)
    return y.astype(x.dtype)

def query_block(n, qb_max):
    return qb_max if n % qb_max == 0 else n

def gather_blocks(blocks, idx):
    return jax.vmap(jax.vmap(lambda bl, i: bl[i]))(blocks, idx)

def head_bias(table, bucket):
    return jax.vmap(lambda tab, bk: tab[bk], in_axes=(1, 1), out_axes=1)(table, bucket)

def nsa_attention(q, gate_logits, kv_full, win_ctx, q_pos0, win_pos0, cmp_pe, cmp_w, bias_tab):
    B, Tq = q.shape[:2]
    L = kv_full.shape[1]
    dt = q.dtype
    scale = HEAD_DIM ** -0.5
    qg = q.reshape(B, Tq, NSA_GROUPS, NSA_HPG, HEAD_DIM)
    tpos = q_pos0 + jnp.arange(Tq, dtype=jnp.int32)

    r = CMP_BLK // CMP_STRIDE
    n_full = L // CMP_STRIDE
    n_cmp = n_full - r + 1
    seg = kv_full[:, :n_full * CMP_STRIDE, :2].reshape(B, n_full, CMP_STRIDE, 2, NSA_GROUPS, HEAD_DIM)
    pe = cmp_pe.reshape(2, r, CMP_STRIDE, HEAD_DIM)
    w = cmp_w.reshape(2, r, CMP_STRIDE, HEAD_DIM, HEAD_DIM)
    comp = jnp.einsum('bnscgd,csde->bncge',
                      seg[:, 0:n_cmp] + jnp.swapaxes(pe[:, 0], 0, 1)[:, :, None, :], w[:, 0])
    for m in range(1, r):
        comp = comp + jnp.einsum('bnscgd,csde->bncge',
                                 seg[:, m:m + n_cmp] + jnp.swapaxes(pe[:, m], 0, 1)[:, :, None, :], w[:, m])
    kc, vc = comp[:, :, 0], comp[:, :, 1]
    end_pos = jnp.arange(n_cmp, dtype=jnp.int32) * CMP_STRIDE + (CMP_BLK - 1)
    dist_c = tpos[:, None] - end_pos[None, :]
    mask_c = dist_c >= 0
    bias_c = jnp.transpose(bias_tab[t5_bucket(dist_c)], (2, 3, 0, 1))
    s_c = jnp.einsum('btghd,bngd->bghtn', qg, kc).astype(jnp.float32) * scale + bias_c
    p_c = masked_softmax(s_c, mask_c) * mask_c
    o_cmp = jnp.einsum('bghtn,bngd->btghd', p_c.astype(dt), vc)

    imp = p_c.sum(axis=2)
    n_seg = -(-L // CMP_STRIDE)
    seg_score = jnp.pad(imp, ((0, 0), (0, 0), (0, 0), (0, n_seg - n_cmp)))
    for m in range(1, r):
        seg_score = seg_score + jnp.pad(imp, ((0, 0), (0, 0), (0, 0), (m, n_seg - n_cmp - m)))
    spb = SEL_BLK // CMP_STRIDE
    n_sel = -(-L // SEL_BLK)
    blk_score = jnp.pad(seg_score, ((0, 0), (0, 0), (0, 0), (0, n_sel * spb - n_seg)))
    blk_score = blk_score.reshape(B, NSA_GROUPS, Tq, n_sel, spb).sum(-1)
    jblk = jnp.arange(n_sel, dtype=jnp.int32)[None, :]
    cur = (tpos // SEL_BLK)[:, None]
    valid = jblk <= cur
    forced = valid & ((jblk == 0) | (jblk == cur) | (jblk == cur - 1))
    score = jnp.where(forced, jnp.inf, jnp.where(valid, blk_score, -jnp.inf))
    top_s, sel_idx = lax.top_k(score, min(N_SEL, n_sel))
    sel_ok = top_s > -jnp.inf
    n_take = sel_idx.shape[-1]

    kv_s = jnp.pad(kv_full[:, :, 2:], ((0, 0), (0, n_sel * SEL_BLK - L), (0, 0), (0, 0), (0, 0)))
    kv_s = kv_s.reshape(B, n_sel, SEL_BLK, 2, NSA_GROUPS, HEAD_DIM).transpose(0, 4, 1, 2, 3, 5)
    win_pad = jnp.pad(win_ctx, ((0, 0), (WINDOW, 0), (0, 0), (0, 0), (0, 0)))

    qb = query_block(Tq, NSA_QB)
    nqb = Tq // qb
    q_blocks = jnp.moveaxis(qg.reshape(B, nqb, qb, NSA_GROUPS, NSA_HPG, HEAD_DIM), 1, 0)
    idx_blocks = jnp.moveaxis(sel_idx.reshape(B, NSA_GROUPS, nqb, qb, n_take), 2, 0)
    ok_blocks = jnp.moveaxis(sel_ok.reshape(B, NSA_GROUPS, nqb, qb, n_take), 2, 0)
    pos_blocks = tpos.reshape(nqb, qb)
    arange_sel = jnp.arange(SEL_BLK, dtype=jnp.int32)
    arange_win = jnp.arange(WINDOW + qb, dtype=jnp.int32)

    def one_block(args):
        qblk, idx, ok, tp = args
        kvg = gather_blocks(kv_s, idx).reshape(B, NSA_GROUPS, qb, n_take * SEL_BLK, 2, HEAD_DIM)
        kpos = (idx[..., None] * SEL_BLK + arange_sel).reshape(B, NSA_GROUPS, qb, n_take * SEL_BLK)
        dist = tp[None, None, :, None] - kpos
        msk = jnp.repeat(ok, SEL_BLK, axis=-1) & (dist >= 0)
        bias = jnp.moveaxis(head_bias(bias_tab, t5_bucket(dist)), -1, 2)
        s = jnp.einsum('bqghd,bgqkd->bghqk', qblk, kvg[..., 0, :]).astype(jnp.float32) * scale + bias
        p = masked_softmax(s, msk[:, :, None])
        o_sel = jnp.einsum('bghqk,bgqkd->bqghd', p.astype(dt), kvg[..., 1, :])
        wkv = lax.dynamic_slice_in_dim(win_pad, tp[0] - win_pos0, WINDOW + qb, axis=1)
        wpos = tp[0] - WINDOW + arange_win
        wd = tp[:, None] - wpos[None, :]
        wm = (wpos[None, :] >= 0) & (wd >= 0) & (wd <= WINDOW)
        wbias = jnp.transpose(bias_tab[t5_bucket(wd)], (2, 3, 0, 1))
        s = jnp.einsum('bqghd,bkgd->bghqk', qblk, wkv[:, :, 0]).astype(jnp.float32) * scale + wbias
        p = masked_softmax(s, wm)
        o_win = jnp.einsum('bghqk,bkgd->bqghd', p.astype(dt), wkv[:, :, 1])
        return o_sel, o_win

    o_sel, o_win = lax.map(one_block, (q_blocks, idx_blocks, ok_blocks, pos_blocks))
    o_sel = jnp.moveaxis(o_sel, 0, 1).reshape(B, Tq, NSA_GROUPS, NSA_HPG, HEAD_DIM)
    o_win = jnp.moveaxis(o_win, 0, 1).reshape(B, Tq, NSA_GROUPS, NSA_HPG, HEAD_DIM)
    g = jax.nn.sigmoid(gate_logits.astype(jnp.float32)).astype(dt).reshape(B, Tq, NSA_GROUPS, NSA_HPG, 3)
    o = g[..., 0:1] * o_cmp + g[..., 1:2] * o_sel + g[..., 2:3] * o_win
    return o.reshape(B, Tq, NSA_HEADS * HEAD_DIM)

def moba_attention(q, kv_full, q_pos0, bias_tab):
    B, Tq = q.shape[:2]
    L = kv_full.shape[1]
    dt = q.dtype
    scale = HEAD_DIM ** -0.5
    tpos = q_pos0 + jnp.arange(Tq, dtype=jnp.int32)
    nb = -(-L // MOBA_BLK)
    kvp = jnp.pad(kv_full, ((0, 0), (0, nb * MOBA_BLK - L), (0, 0), (0, 0), (0, 0)))
    blocks = kvp.reshape(B, nb, MOBA_BLK, 2, MOBA_HEADS, HEAD_DIM).transpose(0, 4, 1, 2, 3, 5)
    kmean = blocks[..., 0, :].astype(jnp.float32).mean(axis=3)
    own = tpos // MOBA_BLK
    gate = jnp.einsum('bthd,bhnd->bhtn', q.astype(jnp.float32), kmean)
    past = jnp.arange(nb, dtype=jnp.int32)[None, :] < own[:, None]
    top_s, top_i = lax.top_k(jnp.where(past, gate, -jnp.inf), min(MOBA_TOPK, nb))
    own_b = jnp.broadcast_to(own[None, None, :, None], (B, MOBA_HEADS, Tq, 1)).astype(top_i.dtype)
    idx = jnp.concatenate([top_i, own_b], axis=-1)
    ok = jnp.concatenate([top_s > -jnp.inf, jnp.ones((B, MOBA_HEADS, Tq, 1), dtype=bool)], axis=-1)
    n_take = idx.shape[-1]
    qb = query_block(Tq, MOBA_QB)
    nqb = Tq // qb
    q_blocks = jnp.moveaxis(q.reshape(B, nqb, qb, MOBA_HEADS, HEAD_DIM), 1, 0)
    idx_blocks = jnp.moveaxis(idx.reshape(B, MOBA_HEADS, nqb, qb, n_take), 2, 0)
    ok_blocks = jnp.moveaxis(ok.reshape(B, MOBA_HEADS, nqb, qb, n_take), 2, 0)
    pos_blocks = tpos.reshape(nqb, qb)
    arange_blk = jnp.arange(MOBA_BLK, dtype=jnp.int32)

    def one_block(args):
        qblk, ib, okb, tp = args
        kvg = gather_blocks(blocks, ib).reshape(B, MOBA_HEADS, qb, n_take * MOBA_BLK, 2, HEAD_DIM)
        kpos = (ib[..., None] * MOBA_BLK + arange_blk).reshape(B, MOBA_HEADS, qb, n_take * MOBA_BLK)
        dist = tp[None, None, :, None] - kpos
        msk = jnp.repeat(okb, MOBA_BLK, axis=-1) & (dist >= 0)
        s = (jnp.einsum('bqhd,bhqkd->bhqk', qblk, kvg[..., 0, :]).astype(jnp.float32) * scale
             + head_bias(bias_tab, t5_bucket(dist)))
        p = masked_softmax(s, msk)
        return jnp.einsum('bhqk,bhqkd->bqhd', p.astype(dt), kvg[..., 1, :])

    o = lax.map(one_block, (q_blocks, idx_blocks, ok_blocks, pos_blocks))
    return jnp.moveaxis(o, 0, 1).reshape(B, Tq, MOBA_HEADS * HEAD_DIM)

def peer_ffn(x, wq, keys, u_tab, v_tab):
    n, d = x.shape
    blk = min(PEER_BLK, n)
    nblk = -(-n // blk)
    xp = jnp.pad(x, ((0, nblk * blk - n), (0, 0))).reshape(nblk, blk, d)

    def one_block(xb):
        q = jnp.einsum('nd,de->ne', xb, wq).reshape(blk, PEER_HEADS, 2, PEER_HALF)
        s = jnp.einsum('nhcd,hckd->nhck', q, keys).astype(jnp.float32)
        sv, si = lax.top_k(s, PEER_TOPK)
        cand = (sv[:, :, 0, :, None] + sv[:, :, 1, None, :]).reshape(blk, PEER_HEADS, PEER_TOPK * PEER_TOPK)
        cidx = (si[:, :, 0, :, None] * PEER_N_KEYS + si[:, :, 1, None, :]).reshape(blk, PEER_HEADS, PEER_TOPK * PEER_TOPK)
        fs, fpos = lax.top_k(cand, PEER_TOPK)
        eidx = jnp.take_along_axis(cidx, fpos, axis=-1)
        g = jax.nn.softmax(fs, axis=-1)
        act = jax.nn.gelu(jnp.einsum('nd,nhkd->nhk', xb, u_tab[eidx]).astype(jnp.float32), approximate=False)
        return jnp.einsum('nhk,nhkd->nd', (g * act).astype(xb.dtype), v_tab[eidx])

    return lax.map(one_block, xp).reshape(nblk * blk, d)[:n]

def decoder_layer(x, q_pos0, nsa_past, moba_past, win_past, win_keep, w_in, cmp_pe, cmp_w,
                  w_branch_a, w_branch_b, w_out, ln1_g, ln1_b, peer_wq, peer_keys, peer_u, peer_v,
                  ln2_g, ln2_b, rel_bias):
    B, T, _ = x.shape
    proj = jnp.einsum('btd,dn->btn', x, w_in)
    cuts = []
    acc = 0
    for size in SPLIT_SIZES[:-1]:
        acc += size
        cuts.append(acc)
    q_a, kv_nsa, kv_win, gate_a, q_b, kv_b, g_merge = jnp.split(proj, cuts, axis=-1)
    q_a = q_a.reshape(B, T, NSA_HEADS, HEAD_DIM)
    kv_nsa = kv_nsa.reshape(B, T, 4, NSA_GROUPS, HEAD_DIM)
    kv_win = kv_win.reshape(B, T, 2, NSA_GROUPS, HEAD_DIM)
    gate_a = gate_a.reshape(B, T, NSA_HEADS, 3)
    q_b = q_b.reshape(B, T, MOBA_HEADS, HEAD_DIM)
    kv_b = kv_b.reshape(B, T, 2, MOBA_HEADS, HEAD_DIM)
    g_merge = jax.nn.sigmoid(g_merge.astype(jnp.float32)).astype(x.dtype).reshape(B, T, 2, D_MODEL)

    nsa_full = jnp.concatenate([nsa_past, kv_nsa], axis=1)
    moba_full = jnp.concatenate([moba_past, kv_b], axis=1)
    win_ctx = jnp.concatenate([win_past, kv_win], axis=1)
    win_pos0 = q_pos0 - win_past.shape[1]
    bias_a = rel_bias[:, :NSA_HEADS].reshape(N_BUCKETS, NSA_GROUPS, NSA_HPG)
    bias_b = rel_bias[:, NSA_HEADS:]

    o_a = nsa_attention(q_a, gate_a, nsa_full, win_ctx, q_pos0, win_pos0, cmp_pe, cmp_w, bias_a)
    o_b = moba_attention(q_b, moba_full, q_pos0, bias_b)
    y_a = jnp.einsum('btn,nd->btd', o_a, w_branch_a)
    y_b = jnp.einsum('btn,nd->btd', o_b, w_branch_b)
    mix = jnp.einsum('btd,de->bte', g_merge[:, :, 0] * y_a + g_merge[:, :, 1] * y_b, w_out)
    h = layer_norm(DN_ALPHA * x + mix, ln1_g, ln1_b)
    f = peer_ffn(h.reshape(B * T, D_MODEL), peer_wq, peer_keys, peer_u, peer_v).reshape(B, T, D_MODEL)
    y = layer_norm(DN_ALPHA * h + f, ln2_g, ln2_b)
    win_new = win_ctx[:, win_ctx.shape[1] - win_keep:]
    return y, kv_nsa, kv_b, win_new

def setup_inputs(seed: int = 0) -> dict:
    key = jax.random.key(seed)
    ks = jax.random.split(key, 24)
    f32 = jnp.float32
    n_pages = PAST_LEN // PAGE_SIZE
    n_pool = (DEC_BATCH * n_pages * 5) // 4
    win_len = min(WINDOW, PAST_LEN)

    def nrm(k, shape, scale):
        return jax.random.normal(k, shape, f32) * scale

    page_table = jax.random.permutation(ks[5], n_pool)[:DEC_BATCH * n_pages].reshape(DEC_BATCH, n_pages).astype(jnp.int32)
    return {
        'x_prompt': nrm(ks[0], (BATCH, SEQ, D_MODEL), 1.0),
        'x_sample': nrm(ks[1], (DEC_BATCH, DEC_SEQ, D_MODEL), 1.0),
        'cache_nsa': nrm(ks[2], (DEPTH, n_pool, PAGE_SIZE, 4, NSA_GROUPS, HEAD_DIM), 1.0),
        'cache_moba': nrm(ks[3], (DEPTH, n_pool, PAGE_SIZE, 2, MOBA_HEADS, HEAD_DIM), 1.0),
        'state_nsa_win': nrm(ks[4], (DEPTH, DEC_BATCH, win_len, 2, NSA_GROUPS, HEAD_DIM), 1.0),
        'page_table': page_table,
        'w_in': nrm(ks[6], (DEPTH, D_MODEL, N_IN), D_MODEL ** -0.5),
        'nsa_cmp_pe': nrm(ks[7], (DEPTH, 2, CMP_BLK, HEAD_DIM), 0.02),
        'nsa_cmp_w': nrm(ks[8], (DEPTH, 2, CMP_BLK, HEAD_DIM, HEAD_DIM), (CMP_BLK * HEAD_DIM) ** -0.5),
        'w_branch_a': nrm(ks[9], (DEPTH, NSA_HEADS * HEAD_DIM, D_MODEL), (NSA_HEADS * HEAD_DIM) ** -0.5),
        'w_branch_b': nrm(ks[10], (DEPTH, MOBA_HEADS * HEAD_DIM, D_MODEL), (MOBA_HEADS * HEAD_DIM) ** -0.5),
        'w_out': nrm(ks[11], (DEPTH, D_MODEL, D_MODEL), DN_BETA * D_MODEL ** -0.5),
        'ln1_g': 1.0 + nrm(ks[12], (DEPTH, D_MODEL), 0.02),
        'ln1_b': nrm(ks[13], (DEPTH, D_MODEL), 0.02),
        'peer_wq': nrm(ks[14], (DEPTH, D_MODEL, PEER_HEADS * 2 * PEER_HALF), D_MODEL ** -0.5),
        'peer_keys': nrm(ks[15], (DEPTH, PEER_HEADS, 2, PEER_N_KEYS, PEER_HALF), PEER_HALF ** -0.5),
        'peer_u': nrm(ks[16], (DEPTH, N_EXPERTS, D_MODEL), D_MODEL ** -0.5),
        'peer_v': nrm(ks[17], (DEPTH, N_EXPERTS, D_MODEL), DN_BETA),
        'ln2_g': 1.0 + nrm(ks[18], (DEPTH, D_MODEL), 0.02),
        'ln2_b': nrm(ks[19], (DEPTH, D_MODEL), 0.02),
        'rel_bias': nrm(ks[20], (N_BUCKETS, NSA_HEADS + MOBA_HEADS), 0.5),
    }

def reference(x_prompt, x_sample, cache_nsa, cache_moba, state_nsa_win, page_table, w_in, nsa_cmp_pe,
              nsa_cmp_w, w_branch_a, w_branch_b, w_out, ln1_g, ln1_b, peer_wq, peer_keys, peer_u, peer_v,
              ln2_g, ln2_b, rel_bias):
    bp, t_prompt = x_prompt.shape[:2]
    bs = x_sample.shape[0]
    past_len = page_table.shape[1] * cache_nsa.shape[2]
    win_len = state_nsa_win.shape[2]
    xp, xs = x_prompt, x_sample
    p_nsa, p_moba, p_win, s_nsa, s_moba, s_win = [], [], [], [], [], []
    for l in range(DEPTH):
        params = (w_in[l], nsa_cmp_pe[l], nsa_cmp_w[l], w_branch_a[l], w_branch_b[l], w_out[l],
                  ln1_g[l], ln1_b[l], peer_wq[l], peer_keys[l], peer_u[l], peer_v[l], ln2_g[l], ln2_b[l],
                  rel_bias)
        xp, a, b, c = decoder_layer(
            xp, 0,
            jnp.zeros((bp, 0, 4, NSA_GROUPS, HEAD_DIM), xp.dtype),
            jnp.zeros((bp, 0, 2, MOBA_HEADS, HEAD_DIM), xp.dtype),
            jnp.zeros((bp, 0, 2, NSA_GROUPS, HEAD_DIM), xp.dtype),
            min(WINDOW, t_prompt), *params)
        p_nsa.append(a)
        p_moba.append(b)
        p_win.append(c)
        nsa_past = cache_nsa[l][page_table].reshape(bs, past_len, 4, NSA_GROUPS, HEAD_DIM)
        moba_past = cache_moba[l][page_table].reshape(bs, past_len, 2, MOBA_HEADS, HEAD_DIM)
        xs, a, b, c = decoder_layer(xs, past_len, nsa_past, moba_past, state_nsa_win[l], win_len, *params)
        s_nsa.append(a)
        s_moba.append(b)
        s_win.append(c)
    return (xp, xs, jnp.stack(p_nsa), jnp.stack(p_moba), jnp.stack(p_win),
            jnp.stack(s_nsa), jnp.stack(s_moba), jnp.stack(s_win))


_drawn_inputs = setup_inputs


def setup_inputs(seed=0):
    import zlib

    import numpy as np

    out = dict(_drawn_inputs(seed))
    spreads = {}
    factors = {'nsa_cmp_pe': 3.829, 'ln2_g': 2.91, 'ln2_b': 2.842}
    for name, (base, spread) in spreads.items():
        noise = np.random.default_rng([zlib.crc32(name.encode()), seed]).standard_normal(out[name].shape)
        drawn = base * np.exp(spread * noise) if base else spread * noise
        out[name] = jnp.asarray(drawn.astype(out[name].dtype))
    for name, factor in factors.items():
        out[name] = (out[name] * factor).astype(out[name].dtype)
    return out
```

```python
import math
from contextlib import ExitStack

import concourse.bass as bass
from concourse import mybir

F32 = mybir.dt.float32
U32 = mybir.dt.uint32
I32 = mybir.dt.int32
ALU = mybir.AluOpType
ACT = mybir.ActivationFunctionType
AXX = mybir.AxisListType.X

P = 128
D = 1024
KD = D // P
TP = 256
NB = 8
T = TP + NB
HD = 64
NPAIR = 4
PAST = 1024
PAGE = 128
NPG = PAST // PAGE
NCMP_P = TP // 16 - 1
NCMP_D = PAST // 16 - 1
NEG = -1e30
SCALE = HD ** -0.5
ALPHA = 2.0 ** 0.25
EPS = 1e-5
ROWS = NB * 8
TOPK = 16
NH = 8

T_QA, T_QB, T_KC, T_VC, T_KS, T_VS, T_KW, T_VW, T_KB, T_VB, T_GATE, T_MRG = 0, 4, 8, 9, 10, 11, 12, 13, 14, 18, 22, 23
NT_IN = T_MRG + 16
KV0 = T_KC
NKV = T_GATE - T_KC
W_CONV = NT_IN
W_BRANCH = W_CONV + 8
W_OUT = W_BRANCH + 8
W_Q = W_OUT + 8
NW = W_Q + 16
RING = 8
PGW = 640
UNROLL = 4
HALVES = P // UNROLL

C_ID = 0
C_ONE = C_ID + P
C_MASKC = C_ONE + P
C_HM = C_MASKC + 2
C_GSUM = C_HM + 8
C_SELB = C_GSUM + ROWS
C_IDX = C_SELB + 8
C_DIAG = C_IDX + 16
C_MM = C_DIAG + 8
C_MN = C_MM + 512
C_JS = C_MN + P
C_M24 = C_JS + 4
C_B24 = C_M24 + 8
C_KRED = C_B24 + 3
NCONST = C_KRED + 8


class Chain:

    def __init__(self, eng, sem):
        self.eng, self.sem, self.base, self.off = eng, sem, 0, 0

    def __call__(self, ins):
        self.off += 1
        ins.then_inc(self.sem, 1)
        self.eng.wait_ge(self.sem, self.base + self.off)

    def loose(self, ins):
        self.off += 1
        ins.then_inc(self.sem, 1)

    def settle(self):
        self.eng.wait_ge(self.sem, self.base + self.off)

    def enter(self, i, per):
        self.start, self.per = self.base + self.off, per
        self.base, self.off = i * per + self.start, 0

    def leave(self, turns):
        assert self.off == self.per, (self.off, self.per)
        self.base, self.off = 0, self.start + turns * self.per


def hybrid_layer(nc, a):
    ctx = ExitStack()
    with ctx:
        def sb(name, shape, dt=F32):
            return ctx.enter_context(nc.sbuf_tensor(name, shape, dt))

        def sem(name):
            return ctx.enter_context(nc.semaphore(name))

        cst = sb("cst", [P, NCONST])
        x_n = sb("x_n", [P, 3, D])
        xT_r = sb("xT_r", [P, KD * T])
        feat_r = sb("feat_r", [P, NT_IN * T])
        kv_n = sb("kv_n", [P, 2, NKV, P])
        ring = sb("ring", [P, RING, D])
        big = sb("big", [P, 16384])
        pg_r = sb("pg_r", [P, NPG * PGW])
        ps = ctx.enter_context(nc.psum_tensor("ps", [P, 8, 512], F32))
        tabx = sb("tabx", [33, 16])
        tabd = sb("tabd", [32, 2, ROWS])
        kc_p = sb("kc_p", [P, 2, 17])
        vc_pn = sb("vc_pn", [NCMP_P, P])
        gate_n = sb("gate_n", [P, 2, 24])
        ptab = sb("ptab", [1, NB * NPG], I32)
        small = sb("small", [P, 128])

        ident = cst[:, C_ID:C_ID + P]
        feat = feat_r[:, :].rearrange("p (n t) -> p n t", t=T)
        xT = xT_r[:, :].rearrange("p (k t) -> p k t", t=T)
        ct = big[:, :].rearrange("p (c b n s) -> p c b n s", c=2, b=NB, s=16)
        bias_p = pg_r[:, 0:4096].rearrange("p (h k) -> p h k", h=16)
        pages = pg_r[:, :].rearrange("p (g c) -> p g c", g=NPG)

        o_n = big[:, 0:2048].rearrange("p (t h d) -> p t h d", t=2, h=16)
        qz = big[:, 2048:3072].rearrange("p (m r t) -> p m r t", m=2, r=2)
        s_p = big[:, 3072:4608].rearrange("p (r c) -> p r c", r=2)
        pT = big[:, 4608:5376]
        biasd = big[0:ROWS, 5376:7426].rearrange("p (m k) -> p m k", m=2)
        win_k = big[:, 7426:11522].rearrange("p (b k) -> p b k", b=NB)
        win_v = big[:, 11522:15618].rearrange("p (b c d) -> p b c d", b=NB, c=4)
        pm = big[0:ROWS, 0:1025]
        psl = big[0:ROWS, 1025:2050]
        pw = big[0:ROWS, 2050:2563]
        pc = big[0:ROWS, 2563:2626]
        pTm = big[:, 2626:3138].rearrange("p (g r) -> p g r", r=ROWS)
        pTs = big[:, 3138:3650].rearrange("p (g r) -> p g r", r=ROWS)
        pTw = big[:, 3650:3906].rearrange("p (g r) -> p g r", r=ROWS)
        pTc = big[0:NCMP_D, 3906:3970]
        sel_m = big[0:NB, 3970:4994].rearrange("p (r c) -> p r c", r=2)
        sel_n = big[0:NB, 4994:5250].rearrange("p (r c) -> p r c", r=2)
        mT = big[:, 0:KD * T].rearrange("p (k t) -> p k t", t=T)
        qT2 = big[:, 2112:2112 + 2 * T].rearrange("p (r t) -> p r t", r=2)
        oT = feat_r[:, 0:KD * T].rearrange("p (k t) -> p k t", t=T)
        kc_dk = sb("kc_dk", [P, NB * NCMP_D])
        bc_keep = sb("bc_keep", [P, 240])
        x_flat = x_n[:, :, :].rearrange("p t d -> p (t d)")
        brev = x_flat[0:16, 0:384]
        smp_n = x_flat[0:NB, 0:NKV * P].rearrange("p (n c) -> p n c", c=P)
        vc_dn = x_flat[0:NCMP_D, NKV * P:NKV * P + NB * P].rearrange("p (b c) -> p b c", b=NB)
        o_part = big[:, 15618:15874]
        imp, seg, blk = big[0:ROWS, 15874:15937], big[0:ROWS, 15937:15993], big[0:ROWS, 15993:16041]
        mtmp = big[:, 2112:2112 + T]
        stats = sb("stats", [P, 16])
        vc_dT = xT_r[:, 0:NB * NCMP_D]
        kcx = xT_r[:, 576:1152].rearrange("p (c k) -> p c k", c=2)
        qbd_m = xT_r[:, 0:2048].rearrange("p (b j r) -> p b j r", b=NB, j=NPAIR)
        qa_r = sb("qa_r", [P, NB * ROWS])
        qbd_a = qa_r[:, :].rearrange("p (b r) -> p b r", b=NB)
        ez = sb("ez", [P, 3, ROWS])
        gz = sb("gz", [24, ROWS])
        pnz = sb("pnz", [NB, NB, 24])

        sc = feat_r[:, 0:6144].rearrange("p (t n k) -> p t n k", t=3, n=16)
        keysT = feat_r[:, 6144:8192].rearrange("p (n k) -> p n k", n=16)
        h_rep = feat_r[:, 8192:9216]
        rr = ring[:, :, :].rearrange("p a b -> p (a b)")
        val = rr[:, 0:256].rearrange("p (n k) -> p n k", n=16)
        idf = rr[:, 256:512].rearrange("p (n k) -> p n k", n=16)
        cand = rr[:, 512:2560]
        oneh = rr[:, 2560:4608]
        idu = rr[:, 4608:4864].bitcast(U32).rearrange("p (n k) -> p n k", n=16)
        fpos = rr[:, 4864:4992].bitcast(U32)
        fi = rr[:, 4992:5120].bitcast(U32)
        fif = rr[:, 5120:5248]
        ea = rr[:, 5248:5376]
        eb = rr[:, 5376:5504]
        acc = [rr[:, 5504:6528], rr[:, 6528:7552], pg_r[:, 4096:5120]]
        gsum = rr[:, 7552:7560]
        ghi = rr[:, 7560:7568]
        ln_rows = pg_r[:, 0:4096].rearrange("p (n d) -> p n d", n=4)
        gk = sb("gk", [P, 3, P])
        eidx = sb("eidx", [P, 3, P], U32)
        idx_s = sb("idx_s", [P, 2, UNROLL], U32)
        dots = sb("dots", [P, 2, UNROLL])
        gel = sb("gel", [P, 2, UNROLL])
        wts = sb("wts", [P, 2, UNROLL])
        gk_s = sb("gk_s", [P, 8])
        eidx_s = sb("eidx_s", [P, 8], U32)
        u_rows = big[:, 0:8192].rearrange("p (s d) -> p s d", s=8)
        v_rows = big[:, 8192:16384].rearrange("p (s d) -> p s d", s=8)

        bias_scr = nc.dram_tensor("bias_scr", (16, P, 384), F32).ap()
        h_scr = nc.dram_tensor("h_scr", (NB, D), F32).ap()
        g_scr = nc.dram_tensor("g_scr", (NB, P), F32).ap()
        e_scr = nc.dram_tensor("e_scr", (NB, P), U32).ap()

        cst_in, tab_in, oh_in, pt_in, xT_in, x_in = (sem(n) for n in ("cst_in", "tab_in", "oh_in", "pt_in", "xT_in", "x_in"))
        pe_in = sem("pe_in")
        w_in = [sem(f"w_in{i}") for i in range(RING)]
        w_used = sem("w_used")
        brev_mm, brev_sb, bscr_out, bias_in, biasc_mm, biasc_sb = (
            sem(n) for n in ("brev_mm", "brev_sb", "bscr_out", "bias_in", "biasc_mm", "biasc_sb"))
        proj_sb, gates_sb = sem("proj_sb"), sem("gates_sb")
        kvt_mm, kvt_v, kvt_a = sem("kvt_mm"), sem("kvt_v"), sem("kvt_a")
        ct_in, kcx_sb, comp_sb, vct_mm, vct_sb = (
            sem(n) for n in ("ct_in", "kcx_sb", "comp_sb", "vct_mm", "vct_sb"))
        qza_sb, qzb_sb, qk_mm, s_sb_, mx_sb, exp_sb, tp_mm, pt_v, pt_a, pv_mm, o_sb = (
            sem(n) for n in ("qza_sb", "qzb_sb", "qk_mm", "s_sb", "mx_sb", "exp_sb", "tp_mm", "pt_v", "pt_a", "pv_mm", "o_sb"))
        qz_zero = sem("qz_zero")
        oT_mm, oT_v = sem("oT_mm"), sem("oT_v")
        winpg_in = sem("winpg_in")
        kv_in = [sem("kv_in0"), sem("kv_in1")]
        kv_used = [sem("kv_used0"), sem("kv_used1")]
        biasd_mm, biasd_sb, qbd_sb, ez_sb, sd_mm, small_mm = (
            sem(n) for n in ("biasd_mm", "biasd_sb", "qbd_sb", "ez_sb", "sd_mm", "small_mm"))
        dmax_sb, dexp_sb, imp_rd, imp_mm, pd_sb, pdt_mm, pdt_sb, pnew_mm, pnz_sb = (
            sem(n) for n in ("dmax_sb", "dexp_sb", "imp_rd", "imp_mm", "pd_sb", "pdt_mm", "pdt_sb", "pnew_mm", "pnz_sb"))
        od_mm, od_sb, oc_mm, oTd_sb = (sem(n) for n in ("od_mm", "od_sb", "oc_mm", "oTd_sb"))
        m_sb, mix_sb, ln_in, h_sb, hT_mm, hT_sb = (
            sem(n) for n in ("m_sb", "mix_sb", "ln_in", "h_sb", "hT_mm", "hT_sb"))
        keys_in, q_sb, sc_mm, sc_sb = (sem(n) for n in ("keys_in", "q_sb", "sc_mm", "sc_sb"))
        fsub_sb, gexp_sb, e_sb, hs_out, gs_out, es_out, hrep_in, gks_in, eis_in = (
            sem(n) for n in ("fsub_sb", "gexp_sb", "e_sb", "hs_out", "gs_out", "es_out", "hrep_in", "gks_in", "eis_in"))
        idx_st, idx_go = sem("idx_st"), sem("idx_go")
        u_in = [sem(f"u_in{i}") for i in range(8)]
        v_in = [sem(f"v_in{i}") for i in range(8)]
        u_used, v_used, gel_sb = sem("u_used"), sem("v_used"), sem("gel_sb")
        sum_mm, y_sb = sem("sum_mm"), sem("y_sb")
        var_sb, std_sb = sem("var_sb"), sem("std_sb")
        out_w, out_kv, out_y = sem("out_w"), sem("out_kv"), sem("out_y")
        dve_own, pool_own, act_own = sem("dve_own"), sem("pool_own"), sem("act_own")

        oh_r = feat_r[0:33, 0:30 * P + 384]
        oh_rev = oh_r[:, 0:384]
        oh_c = oh_r[:, 384:384 + 30 * P].rearrange("p (m t) -> p m t", m=30)
        oh_d = pg_r[0:32, 4096:4096 + PAST]
        block = ctx.enter_context(nc.Block())

        def kind_of(s):
            return ("cmp", "sel", "win", "moba")[s]

        @block.sync
        def _(sp):
            sp.dma_start(tabx[:, :], a["tab_ext"]).then_inc(tab_in, 16)
            sp.dma_start(tabd[:, :, :], a["tab_dec"]).then_inc(tab_in, 16)
            sp.dma_start(oh_r, a["onehot"][:, 0:384 + 30 * P]).then_inc(oh_in, 16)
            sp.dma_start(oh_d, a["onehot"][0:32, 384 + 30 * P:384 + 30 * P + PAST]).then_inc(oh_in, 16)
            sp.dma_start(xT_r[:, :], a["xT"]).then_inc(xT_in, 16)
            sp.dma_start(cst[:, :], a["consts"]).then_inc(cst_in, 16)

            def weight(n, slot):
                if not (isinstance(n, int) and n < RING):
                    sp.wait_ge(w_used, n + (1 - RING))
                sp.dma_start(ring[:, slot:slot + 1, :], a["wall"][bass.ds(n, 1), :, :].rearrange("a p c -> p a c")
                             ).then_inc(w_in[slot], 16)

            for n in range(RING):
                weight(n, n)
            sp.dma_start(a["win_sample"][:, 0:511, :], a["win_state"][:, 1:512, :]).then_inc(out_w, 16)
            with sp.Fori(1, 5) as it:
                for j in range(RING):
                    weight(it * RING + j, j)
            for n in range(5 * RING, W_OUT):
                weight(n, n % RING)
            sp.wait_ge(pt_in, 16)
            sp.wait_ge(s_sb_, 4 * NPAIR)

            def load_pages(which, b, first):
                for g in range(NPG):
                    half = g // 4
                    if g % 4 == 0 and not first:
                        sp.wait_ge(kv_used[half], b + which * NB)
                    page = sp.value_load(ptab[0:1, bass.ds(b * NPG + g, 1)], min_val=0, max_val=79)
                    sp.dma_start(pages[:, g:g + 1, :], a["pack_kv"][which, bass.ds(page, 1), :, :].rearrange("a p c -> p a c")
                                 ).then_inc(kv_in[half], 16)

            load_pages(0, 0, True)
            with sp.Fori(1, NB) as b:
                load_pages(0, b, False)
            with sp.Fori(0, NB) as b:
                load_pages(1, b, False)
            sp.wait_ge(od_mm, NB)
            sp.wait_ge(out_kv, 16 * 9)
            sp.dma_start(x_n[:, 0:2, :], a["x_prompt"].rearrange("(t p) d -> p t d", p=P)).then_inc(x_in, 16)
            sp.dma_start(x_n[0:NB, 2, :], a["x_sample"]).then_inc(x_in, 16)
            for i, nm in enumerate(("ln1_g", "ln1_b", "ln2_g", "ln2_b")):
                sp.dma_start(ln_rows[:, i, :], a[nm].broadcast_to([P, D])).then_inc(ln_in, 16)
            for n in range(W_OUT, W_Q):
                weight(n, n % RING)
            sp.wait_ge(m_sb, 8)
            sp.dma_start(keysT, a["keysT"]).then_inc(keys_in, 16)
            with sp.Fori(0, 2) as it:
                for j in range(RING):
                    weight(it * RING + (W_Q + j), (W_Q + j) % RING)
            sp.wait_ge(h_sb, 3)
            sp.dma_start(h_scr, x_n[0:NB, 2, :]).then_inc(hs_out, 16)
            sp.wait_ge(hs_out, 16)
            sp.dma_start(h_rep, h_scr.unsqueeze(1).broadcast_to([NB, TOPK, D])).then_inc(hrep_in, 16)
            sp.wait_ge(e_sb, 3)
            sp.dma_start(g_scr, gk[0:NB, 2, :]).then_inc(gs_out, 16)
            sp.dma_start(e_scr, eidx[0:NB, 2, :]).then_inc(es_out, 16)
            sp.wait_ge(gs_out, 16)
            sp.wait_ge(es_out, 16)
            with nc.allow_non_contiguous_dma(reason="a small re-layout"):
                for h in range(NH):
                    sp.dma_start(gk_s[:, h:h + 1], g_scr.rearrange("n (h k) -> n k h", h=NH)[:, :, h:h + 1]).then_inc(gks_in, 16)
                    sp.dma_start(eidx_s[:, h:h + 1], e_scr.rearrange("n (h k) -> n k h", h=NH)[:, :, h:h + 1]).then_inc(eis_in, 16)
            for tt in range(3):
                sp.wait_ge(y_sb, tt + 1)
                if tt < 2:
                    sp.dma_start(a["y_prompt"][tt * P:(tt + 1) * P, :], x_n[:, tt, :]).then_inc(out_y, 16)
                else:
                    sp.dma_start(a["y_sample"], x_n[0:NB, 2, :]).then_inc(out_y, 16)
            sp.wait_ge(out_y, 48)
            sp.wait_ge(out_w, 16)
            sp.wait_ge(out_kv, 16 * 9)

        @block.gpsimd
        def _(pool):
            own = Chain(pool, pool_own)
            pool.dma_start(ptab[:, :], a["page_table"]).then_inc(pt_in, 16)
            pool.wait_ge(pt_in, 16)
            with pool.Fori(0, NB * NPG) as g:
                page = pool.value_load(ptab[0:1, bass.ds(g, 1)], min_val=0, max_val=79)
                pool.dma_start(big[:, :].rearrange("p (c g k) -> p c g k", c=2, k=PAGE)[:, :, bass.ds(g, 1), :],
                               a["pack_cmp"][bass.ds(page, 1), :, :, :].rearrange("a p c k -> p c a k")).then_inc(ct_in, 16)
            pool.wait_ge(brev_sb, 1)
            pool.dma_start(bias_scr, brev[:, :].unsqueeze(1).broadcast_to([16, P, 384])).then_inc(bscr_out, 16)
            pool.wait_ge(bscr_out, 16)
            pool.dma_start(bias_p, bass.AP(tensor=bias_scr.tensor, offset=127, ap=[[383, P], [P * 384, 16], [1, TP]])
                           ).then_inc(bias_in, 16)
            pool.wait_ge(w_used, NT_IN)
            pool.dma_start(kcx[:, :, TP:TP + 32], a["peT"]).then_inc(pe_in, 16)
            pool.wait_ge(w_used, W_BRANCH)
            pool.memset(qz[:, :, :, :], 0.0).then_inc(qz_zero, 1)
            pool.dma_start(win_k, a["win_kT"].rearrange("b p k -> p b k")).then_inc(winpg_in, 16)
            pool.dma_start(win_v, a["win_vr"].rearrange("b p c -> p b c")).then_inc(winpg_in, 16)
            pool.wait_ge(qz_zero, 1)

            def stage_q(j, first):
                for m, tile in ((0, T_QA), (1, T_QB)):
                    done = (qza_sb, qzb_sb)[m]
                    if not first:
                        pool.wait_ge(qk_mm, j * 4 - 1 if m == 0 else j * 4)
                    for r in range(2):
                        pool.tensor_copy(qz[r * HD:(r + 1) * HD, m:m + 1, r, :],
                                         feat[r * HD:(r + 1) * HD, bass.ds(j + tile, 1), 0:TP]).then_inc(done, 1)

            pool.wait_ge(proj_sb, NT_IN)
            stage_q(0, True)
            with pool.Fori(1, NPAIR) as j:
                stage_q(j, False)
            pool.wait_ge(vct_sb, 1)
            pool.wait_ge(qza_sb, 2 * NPAIR)
            pool.wait_ge(qzb_sb, 2 * NPAIR)
            own(pool.memset(xT_r[:, :], 0.0))
            own(pool.memset(qa_r[:, :], 0.0))
            qm = xT_r[:, 0:2048]
            for r in range(2):
                rows = slice(r * HD, (r + 1) * HD)
                for j in range(NPAIR):
                    st = j * 66 + r
                    own(pool.tensor_scalar(qm[rows, st:st + 264 * 7 + 1:264], feat[rows, T_QB + j, TP:T], SCALE, None, ALU.mult))
                    st = j + 4 * r
                    own(pool.tensor_scalar(qa_r[rows, st:st + 72 * 7 + 1:72], feat[rows, T_QA + j, TP:T], SCALE, None, ALU.mult))
            own.settle()
            pool.engine_nop().then_inc(qbd_sb, 1)

            def gather_half(half, idx_ap, group):
                if group is not None:
                    pool.wait_ge(u_used, group * 8 + (4 * half - 4))
                    pool.wait_ge(v_used, group * 8 + (4 * half - 4))
                pool.tensor_copy(idx_s[:, half, :], idx_ap).then_inc(idx_st, 1)
                pool.wait_ge(idx_st, (group * 2 + (half + 1)) if group is not None else half + 1)
                pool.sem_inc(idx_go, 1)
                for s in range(UNROLL):
                    slot = half * UNROLL + s
                    off = bass.IndirectOffsetOnAxis(ap=idx_s[:, half, s:s + 1], axis=0)
                    pool.indirect_dma_start(u_rows[:, slot, :], None, a["peer_u"], off).then_inc(u_in[slot], 16)
                for s in range(UNROLL):
                    slot = half * UNROLL + s
                    off = bass.IndirectOffsetOnAxis(ap=idx_s[:, half, s:s + 1], axis=0)
                    pool.indirect_dma_start(v_rows[:, slot, :], None, a["peer_v"], off).then_inc(v_in[slot], 16)

            pool.wait_ge(sc_mm, 16)
            for tt in range(2):
                pool.wait_ge(e_sb, tt + 1)
                if tt == 0:
                    for half in range(2):
                        gather_half(half, eidx[:, 0, half * UNROLL:(half + 1) * UNROLL], None)
                with pool.Fori(1 if tt == 0 else 0, 16) as i:
                    for half in range(2):
                        gather_half(half, eidx[:, tt, bass.ds(i * 8 + half * UNROLL, UNROLL)], i + 16 * tt)
            pool.wait_ge(eis_in, 16 * NH)
            for half in range(2):
                gather_half(half, eidx_s[:, half * UNROLL:(half + 1) * UNROLL], 32)

        @block.scalar
        def _(act):
            act.wait_ge(brev_mm, 1)
            nc.scalar.copy(brev[:, :], ps[0:16, 0, 0:384]).then_inc(brev_sb, 1)
            with act.Fori(0, NT_IN // 2) as i:
                for j in range(2):
                    act.wait_ge(w_used, i * 2 + (j + 1))
                    nc.scalar.copy(feat[:, bass.ds(i * 2 + j, 1), :], ps[:, j:j + 1, 0:T]).then_inc(proj_sb, 1)
            act.wait_ge(w_used, NT_IN)
            nc.scalar.copy(feat[:, NT_IN - 1, :], ps[:, 0, 0:T]).then_inc(proj_sb, 1)
            for c in range(2):
                act.wait_ge(proj_sb, NT_IN)
                nc.scalar.copy(kcx[:, c, 0:TP], feat[:, T_KC + c, 0:TP]).then_inc(kcx_sb, 1)
            act.wait_ge(proj_sb, NT_IN)
            nc.scalar.activation(feat[:, T_GATE:NT_IN, :], feat[:, T_GATE:NT_IN, :], ACT.Sigmoid).then_inc(gates_sb, 1)
            act.wait_ge(bscr_out, 16)
            for g in range(1, 12, 2):
                act.wait_ge(kvt_mm, g + 1)
                n = 4 if g % 4 < 3 else 2
                src = ps[:, 2 + g % 2, 0:n * P].rearrange("p (n c) -> p n c", c=P)
                dst = (kv_n[:, g // 4, (g % 4) * 4:(g % 4) * 4 + n, :] if g < 8
                       else smp_n[:, (g % 4) * 4:(g % 4) * 4 + n, :])
                nc.scalar.copy(dst, src if g < 8 else src[0:NB]).then_inc(kvt_a, 1)
            act.wait_ge(kvt_a, 6)
            act.wait_ge(kvt_v, 6)
            for tt in range(2):
                r = slice(tt * P, (tt + 1) * P)
                for nm, lo, hi in (("nsa_prompt", 0, 4), ("win_prompt", 4, 6), ("moba_prompt", 6, 14)):
                    act.dma_start(a[nm][r, :].rearrange("p (n c) -> p n c", c=P), kv_n[:, tt, lo:hi, :]).then_inc(out_kv, 16)
            act.dma_start(a["nsa_sample"].rearrange("p (n c) -> p n c", c=P), smp_n[:, 0:4, :]).then_inc(out_kv, 16)
            act.dma_start(a["moba_sample"].rearrange("p (n c) -> p n c", c=P), smp_n[:, 6:14, :]).then_inc(out_kv, 16)
            act.dma_start(a["win_sample"][:, 511, :].rearrange("p (n c) -> p n c", c=P), smp_n[:, 4:6, :]).then_inc(out_kv, 16)

            own = Chain(act, act_own)

            def exps(u, s):
                act.wait_ge(mx_sb, u + 1)
                w = NCMP_P if s == 0 else None
                for t in range(2):
                    for r in range(2):
                        i = t * 2 + r
                        if s == 0:
                            v = s_p[:, 0, i * NCMP_P:(i + 1) * NCMP_P]
                        else:
                            lo = 2 * TP + r * P if t == 0 else r * TP
                            v = s_p[:, s % 2, lo:lo + (P if t == 0 else TP)]
                        nc.scalar.activation(v, v, ACT.Exp, bias=small[:, 8 * (s % 2) + i:8 * (s % 2) + i + 1],
                                             accum_out=small[:, 8 * (s % 2) + 4 + i:8 * (s % 2) + 5 + i]).then_inc(exp_sb, 1)

            def turn(u, s):
                act.wait_ge(tp_mm, u + 1)
                n = 384 if s else 256
                rows = P if s else NCMP_P
                nc.scalar.copy(pT[0:rows, 0:n], ps[0:rows, 4, 0:n]).then_inc(pt_a, 1)

            def body(j, last):
                for s in range(4):
                    if not (last and s == 3):
                        exps(j * 4 + (s + 1), (s + 1) % 4)
                    turn(j * 4 + s, s)

            exps(0, 0)
            with act.Fori(0, NPAIR - 1) as j:
                body(j, False)
            body(NPAIR - 1, True)

            for i, v in enumerate((pc, pm, psl, pw)):
                act.wait_ge(dmax_sb, i + 1)
                nc.scalar.activation(v, v, ACT.Exp, bias=small[0:ROWS, 32 + i:33 + i],
                                     accum_out=small[0:ROWS, 36 + i:37 + i]).then_inc(dexp_sb, 1)

            def deviations(first):
                for tt in range(3):
                    r = P if tt < 2 else NB
                    act.wait_ge(var_sb, first + tt + 1)
                    nc.scalar.sqrt(stats[0:r, 15:16], stats[0:r, 14:15]).then_inc(std_sb, 1)

            deviations(0)
            for n in range(16):
                act.wait_ge(w_used, W_Q + n + 1)
                if n >= 2:
                    act.wait_ge(sc_mm, n - 1)
                nc.scalar.copy(qT2[:, n % 2, :], ps[:, n % 2, 0:T]).then_inc(q_sb, 1)
            for tt in range(3):
                r = P if tt < 2 else NB
                act.wait_ge(fsub_sb, tt + 1)
                nc.scalar.activation(gk[0:r, tt, :], gk[0:r, tt, :], ACT.Exp).then_inc(gexp_sb, 1)
            def gelu(q, half):
                act.wait_ge(u_used, (q + 1) * UNROLL)
                nc.scalar.activation(gel[:, half, :], dots[:, half, :], ACT.Gelu).then_inc(gel_sb, 1)

            with act.Fori(0, HALVES + 1) as i:
                for half in range(2):
                    gelu(i * 2 + half, half)
            deviations(3)

        @block.tensor
        def _(pe):
            mm, tp = nc.tensor.matmul, nc.tensor.transpose
            pe.wait_ge(tab_in, 32)
            pe.wait_ge(oh_in, 32)
            mm(ps[0:16, 0, 0:384], tabx[:, :], oh_rev, start=True, stop=True).then_inc(brev_mm, 1)
            for i in range(30):
                last = mm(ps[:, 7, i * 8:(i + 1) * 8], oh_c[:, i, :], tabx[:, 0:8], start=True, stop=True)
            last.then_inc(biasc_mm, 1)

            pe.wait_ge(xT_in, 16)
            pe.wait_ge(brev_sb, 1)

            def proj_body(it, tiles, first):
                for j in range(tiles):
                    pe.wait_ge(w_in[j], it * 16 + 16)
                    if not (first and j < 2):
                        pe.wait_ge(proj_sb, it * RING + (j - 1))
                    for k in range(KD):
                        last = mm(ps[:, j % 2, 0:T], ring[:, j, k * P:(k + 1) * P], xT[:, k, :], start=(k == 0), stop=(k == KD - 1))
                    last.then_inc(w_used, 1)

            proj_body(0, RING, True)
            with pe.Fori(1, 4) as it:
                proj_body(it, RING, False)
            proj_body(4, 7, False)
            pe.wait_ge(proj_sb, NT_IN)
            pe.wait_ge(cst_in, 16)
            for g in range(12):
                if g >= 2:
                    pe.wait_ge(kvt_v if g % 2 == 0 else kvt_a, g // 2)
                n = 4 if g % 4 < 3 else 2
                for i in range(n):
                    t = KV0 + (g % 4) * 4 + i
                    if g < 8:
                        last = tp(ps[:, 2 + g % 2, i * P:(i + 1) * P], feat[:, t, (g // 4) * P:(g // 4 + 1) * P], ident)
                    else:
                        last = tp(ps[0:NB, 2 + g % 2, i * P:(i + 1) * P], feat[:, t, TP:T], ident)
                last.then_inc(kvt_mm, 1)
            pe.wait_ge(gates_sb, 1)
            for tt in range(2):
                last = tp(ps[:, 0, tt * P:(tt + 1) * P], feat[:, T_GATE, tt * P:(tt + 1) * P], ident)
            last.then_inc(kvt_mm, 1)
            pe.wait_ge(ct_in, 16 * NB * NPG)
            pe.wait_ge(kcx_sb, 2)
            pe.wait_ge(pe_in, 16)
            pe.wait_ge(biasc_sb, 1)
            for c in range(2):
                kv = kcx[:, c, :].rearrange("p (n s) -> p n s", s=16)
                for q in range(4):
                    n = W_CONV + c * 4 + q
                    pe.wait_ge(w_in[n % RING], 16 * (n // RING + 1))
                    for i in range(8):
                        w = ring[:, n % RING, i * P:(i + 1) * P]
                        m, s = divmod(q * 8 + i, 16)
                        f, l = (q == 0 and i == 0), (q == 3 and i == 7)
                        mm(ps[:, 4 + c, 0:NB * NCMP_D].rearrange("p (b n) -> p b n", b=NB), w, ct[:, c, :, m:m + NCMP_D, s], start=f, stop=l)
                        last = mm(ps[:, 6 + c, 0:17], w, kv[:, m:m + 17, s], start=f, stop=l)
                    last.then_inc(w_used, 1)
            pe.wait_ge(comp_sb, 4)
            pe.wait_ge(kvt_v, 6)
            pe.wait_ge(kvt_a, 6)
            tp(ps[0:NCMP_P, 1, 0:P], kc_p[:, 1, 0:NCMP_P], ident)
            for b in range(NB):
                last = tp(ps[0:NCMP_D, 2 + b // 4, (b % 4) * P:(b % 4 + 1) * P], vc_dT[:, b * NCMP_D:(b + 1) * NCMP_D], ident)
            last.then_inc(vct_mm, 1)
            for m in range(2):
                for c in range(2):
                    mm(ps[0:ROWS, 4 + 2 * m + c, :], tabd[:, m, :], oh_d[:, c * 512:(c + 1) * 512], start=True, stop=True)
            for m in range(2):
                last = mm(ps[0:ROWS, 0, 256 + m:257 + m], tabd[:, m, :], cst[0:32, C_ID:C_ID + 1], start=True, stop=True)
            last.then_inc(biasd_mm, 1)
            pe.wait_ge(vct_sb, 1)
            pe.wait_ge(biasd_sb, 1)

            def keys(s, j):
                if s == 0:
                    return kc_p[:, 0, 0:NCMP_P]
                return feat[:, {1: T_KS, 2: T_KW}[s], 0:TP] if s < 3 else feat[:, bass.ds(j + T_KB, 1), 0:TP].rearrange("p a t -> p (a t)")

            def scores(u, j, s, early):
                if s == 0:
                    pe.wait_ge(qza_sb, j * 2 + 2)
                if s == 3:
                    pe.wait_ge(qzb_sb, j * 2 + 2)
                if not early:
                    pe.wait_ge(s_sb_, u + (-1))
                k = keys(s, j)
                bank = 2 * (s % 2)
                for r in range(2):
                    q = qz[:, 1 if s == 3 else 0, r, :]
                    if s == 0:
                        for t in range(2):
                            i = t * 2 + r
                            last = mm(ps[:, bank, i * NCMP_P:(i + 1) * NCMP_P], q[:, t * P:(t + 1) * P], k, start=True, stop=True)
                    else:
                        mm(ps[:, bank, r * TP:(r + 1) * TP], q[:, P:TP], k, start=True, stop=True)
                        last = mm(ps[:, bank + 1, r * P:(r + 1) * P], q[:, 0:P], k[:, 0:P], start=True, stop=True)
                last.then_inc(qk_mm, 1)

            def values(u, j, s, early, unit0):
                pe.wait_ge(exp_sb, u * 4 + 4)
                if not unit0:
                    pe.wait_ge(pt_a, u)
                    pe.wait_ge(pt_v, u)
                buf = s_p[:, s % 2, :]
                if s == 0:
                    for t in range(2):
                        for r in range(2):
                            i = t * 2 + r
                            last = tp(ps[0:NCMP_P, 4 + r, t * P:(t + 1) * P], buf[:, i * NCMP_P:(i + 1) * NCMP_P], ident)
                else:
                    for r in range(2):
                        for c in range(2):
                            tp(ps[:, 4 + r, c * P:(c + 1) * P], buf[:, r * TP + c * P:r * TP + (c + 1) * P], ident)
                        last = tp(ps[:, 4 + r, 2 * P:3 * P], buf[:, 2 * TP + r * P:2 * TP + (r + 1) * P], ident)
                last.then_inc(tp_mm, 1)
                pe.wait_ge(pt_a, u + 1)
                pe.wait_ge(pt_v, u + 1)
                if not early:
                    pe.wait_ge(o_sb, u + (-1))
                out = ps[:, 6 + s % 2, :]
                for r in range(2):
                    hs = slice(r * HD, (r + 1) * HD)
                    if s == 0:
                        for t in range(2):
                            last = mm(out[:, (t * 2 + r) * HD:(t * 2 + r + 1) * HD], pT[0:NCMP_P, r * 256 + t * P:r * 256 + (t + 1) * P],
                                      vc_pn[:, hs], start=True, stop=True)
                        continue
                    def v(c):
                        if s < 3:
                            return kv_n[:, c, {1: T_VS, 2: T_VW}[s] - KV0, hs]
                        return kv_n[:, c, bass.ds(j + (T_VB - KV0), 1), hs].rearrange("p a d -> p (a d)")
                    o1 = out[:, (2 + r) * HD:(3 + r) * HD]
                    mm(o1, pT[:, r * 384:r * 384 + P], v(0), start=True, stop=False)
                    mm(o1, pT[:, r * 384 + P:r * 384 + 2 * P], v(1), start=False, stop=True)
                    last = mm(out[:, r * HD:(r + 1) * HD], pT[:, r * 384 + 2 * P:r * 384 + 3 * P], v(0), start=True, stop=True)
                last.then_inc(pv_mm, 1)

            def att_body(j, first, last):
                for s in range(4):
                    if not (last and s == 3):
                        nj = j if s < 3 else j + 1
                        scores(j * 4 + (s + 1), nj, (s + 1) % 4, first and s == 0)
                    values(j * 4 + s, j, s, first and s < 2, first and s == 0)

            scores(0, 0, 0, True)
            att_body(0, True, False)
            with pe.Fori(1, NPAIR - 1) as j:
                att_body(j, False, False)
            att_body(NPAIR - 1, False, True)
            pe.wait_ge(o_sb, 4 * NPAIR)
            for g in range(4):
                tt, c0 = divmod(g * 4, 8)
                for i in range(4):
                    last = tp(ps[:, g, i * P:(i + 1) * P],
                              o_n[:, tt, 2 * (c0 + i):2 * (c0 + i) + 2, :].rearrange("p h d -> p (h d)"), ident)
            last.then_inc(oT_mm, 1)
            pe.wait_ge(oT_v, 1)

            pe.wait_ge(qbd_sb, 1)
            pe.wait_ge(winpg_in, 32)
            for b in range(NB):
                f, l = b == 0, b == NB - 1
                for half in range(2):
                    pe.wait_ge(kv_in[half], 64 * (b + 1))
                    for j in range(NPAIR):
                        mm(ps[0:ROWS, half, :], qbd_m[:, b, j, :], pages[:, half * 4:half * 4 + 4, j * P:(j + 1) * P],
                           start=f and j == 0, stop=l and j == NPAIR - 1)
                    mm(ps[0:ROWS, 2 + half, :], qbd_a[:, b, :], pages[:, half * 4:half * 4 + 4, 512:640],
                       start=f, stop=l).then_inc(kv_used[half], 1)
                mm(ps[0:ROWS, 4, :], qbd_a[:, b, :], win_k[:, b, :], start=f, stop=l)
                last = mm(ps[0:ROWS, 5, 0:NCMP_D], qbd_a[:, b, :], kc_dk[:, b * NCMP_D:(b + 1) * NCMP_D], start=f, stop=l)
            last.then_inc(sd_mm, 1)
            pe.wait_ge(ez_sb, 1)
            for i in range(3):
                mm(ps[0:ROWS, 6, i:i + 1], ez[:, i, :], cst[:, C_ONE:C_ONE + 1], start=True, stop=True)
            mm(ps[0:ROWS, 6, 8:11], gz[:, :], cst[0:24, C_B24:C_B24 + 3], start=True, stop=True).then_inc(small_mm, 1)
            pe.wait_ge(imp_rd, 1)
            mm(ps[0:ROWS, 7, 0:NCMP_D], cst[0:ROWS, C_GSUM:C_GSUM + ROWS], pc, start=True, stop=True).then_inc(imp_mm, 1)
            pe.wait_ge(pd_sb, 1)
            for g in range(NPG):
                tp(ps[:, 0, g * ROWS:(g + 1) * ROWS], pm[:, g * P:(g + 1) * P], cst[0:ROWS, 0:ROWS])
                tp(ps[:, 1, g * ROWS:(g + 1) * ROWS], psl[:, g * P:(g + 1) * P], cst[0:ROWS, 0:ROWS])
            for g in range(4):
                tp(ps[:, 2, g * ROWS:(g + 1) * ROWS], pw[:, g * P:(g + 1) * P], cst[0:ROWS, 0:ROWS])
            tp(ps[0:NCMP_D, 2, 256:320], pc, cst[0:ROWS, 0:ROWS]).then_inc(pdt_mm, 1)
            mm(ps[0:NB, 6, 16:40], cst[0:ROWS, C_SELB:C_SELB + 8], small[0:ROWS, 64:88], start=True, stop=True).then_inc(pnew_mm, 1)
            pe.wait_ge(pdt_sb, 1)
            pe.wait_ge(pnz_sb, 1)

            def columns(b):
                pe.wait_ge(od_sb, b + 1)
                mm(ps[:, 3, b * 8:b * 8 + 4], sel_n[:, b % 2, :], cst[0:NB, C_JS:C_JS + 4], start=True, stop=True)
                for j in range(NPAIR):
                    last = mm(ps[:, 3, b * 8 + 4 + j:b * 8 + 5 + j], sel_m[:, b % 2, j * P:(j + 1) * P], cst[0:NB, C_ONE:C_ONE + 1],
                              start=True, stop=True)
                last.then_inc(oc_mm, 1)

            for b in range(NB):
                rb = slice(b * 8, (b + 1) * 8)
                om, on = ps[0:NB, 4 + 2 * (b % 2), :], ps[0:NB, 5 + 2 * (b % 2), 0:P]
                if b >= 2:
                    pe.wait_ge(od_sb, b - 1)
                for g in range(NPG):
                    if g % 4 == 0:
                        pe.wait_ge(kv_in[g // 4], 64 * (NB + b + 1))
                    mm(om, pTm[:, g, rb], pages[:, g, 0:512], start=(g == 0), stop=False)
                    x = mm(on, pTs[:, g, rb], pages[:, g, 512:640], start=(g == 0), stop=False)
                    if g % 4 == 3:
                        x.then_inc(kv_used[g // 4], 1)
                for g in range(4):
                    mm(on, pTw[:, g, rb], win_v[:, b, g, :], start=False, stop=False)
                mm(on, pTc[:, rb], vc_dn[:, b, :], start=False, stop=False)
                mm(on, pnz[:, b, 8:16], smp_n[:, T_VS - KV0, :], start=False, stop=False)
                mm(on, pnz[:, b, 16:24], smp_n[:, T_VW - KV0, :], start=False, stop=True)
                mm(om, pnz[:, b, 0:8], smp_n[:, T_VB - KV0:T_VB - KV0 + 4, :].rearrange("p n c -> p (n c)"),
                   start=False, stop=True).then_inc(od_mm, 1)
                if b:
                    columns(b - 1)
            columns(NB - 1)

            pe.wait_ge(oTd_sb, 1)
            for n in range(8):
                w = W_BRANCH + n
                pe.wait_ge(w_in[w % RING], 16 * (w // RING + 1))
                if n >= 2:
                    pe.wait_ge(m_sb, n - 1)
                for m in range(2):
                    for k in range(4):
                        last = mm(ps[:, 4 + 2 * (n % 2) + m, 0:T], ring[:, w % RING, (m * 4 + k) * P:(m * 4 + k + 1) * P], oT[:, m * 4 + k, :],
                                  start=(k == 0), stop=(k == 3))
                last.then_inc(w_used, 1)
            pe.wait_ge(m_sb, 8)
            for n in range(8):
                w = W_OUT + n
                pe.wait_ge(w_in[w % RING], 16 * (w // RING + 1))
                if n >= 2:
                    pe.wait_ge(mix_sb, n - 1)
                for tt in range(3):
                    r = P if tt < 2 else NB
                    for k in range(KD):
                        last = mm(ps[0:r, n % 2, tt * P:(tt + 1) * P], mT[:, k, tt * P:tt * P + r], ring[:, w % RING, k * P:(k + 1) * P],
                                  start=(k == 0), stop=(k == KD - 1))
                last.then_inc(w_used, 1)
            for tt in range(3):
                r = P if tt < 2 else NB
                pe.wait_ge(h_sb, tt + 1)
                for half in range(2):
                    for i in range(4):
                        k = half * 4 + i
                        last = tp(ps[:, 2 + 2 * tt + half if tt < 2 else 6 + half, i * P:i * P + r], x_n[0:r, tt, k * P:(k + 1) * P], ident[0:r, 0:r])
                last.then_inc(hT_mm, 1)
            pe.wait_ge(hT_sb, 3)
            pe.wait_ge(keys_in, 16)

            def key_scores(n):
                pe.wait_ge(q_sb, n + 1)
                if n >= 2:
                    pe.wait_ge(sc_sb, n - 1)
                for tt in range(3):
                    r = P if tt < 2 else NB
                    last = mm(ps[0:r, 2 + n % 2, tt * P:(tt + 1) * P], qT2[:, n % 2, tt * P:tt * P + r], keysT[:, n, :], start=True, stop=True)
                last.then_inc(sc_mm, 1)

            pe.wait_ge(mix_sb, 8)
            for n in range(16):
                w = W_Q + n
                pe.wait_ge(w_in[w % RING], 16 * (w // RING + 1))
                if n >= 2:
                    pe.wait_ge(q_sb, n - 1)
                for k in range(KD):
                    last = mm(ps[:, n % 2, 0:T], ring[:, w % RING, k * P:(k + 1) * P], xT[:, k, :], start=(k == 0), stop=(k == KD - 1))
                last.then_inc(w_used, 1)
                if n:
                    key_scores(n - 1)
            key_scores(15)
            pe.wait_ge(v_used, 8 * 33)
            for c in range(2):
                last = mm(ps[0:NB, c, :], cst[:, C_KRED:C_KRED + 8], acc[2][:, c * 512:(c + 1) * 512], start=True, stop=True)
            last.then_inc(sum_mm, 1)

        @block.vector
        def _(dve):
            own = Chain(dve, dve_own)
            v = nc.vector
            TT, TS, STT = v.tensor_tensor, v.tensor_scalar, v.scalar_tensor_tensor
            dve.wait_ge(biasc_mm, 1)
            v.tensor_copy(bc_keep[:, :], ps[:, 7, 0:240]).then_inc(biasc_sb, 1)
            own.loose(v.memset(ez[:, :, :], 0.0))
            dve.wait_ge(bscr_out, 16)
            for g in range(0, 12, 2):
                dve.wait_ge(kvt_mm, g + 1)
                n = 4
                src = ps[:, 2 + g % 2, 0:n * P].rearrange("p (n c) -> p n c", c=P)
                dst = (kv_n[:, g // 4, (g % 4) * 4:(g % 4) * 4 + n, :] if g < 8 else smp_n[:, (g % 4) * 4:(g % 4) * 4 + n, :])
                v.tensor_copy(dst, src if g < 8 else src[0:NB]).then_inc(kvt_v, 1)
            dve.wait_ge(kvt_mm, 13)
            own(v.tensor_copy(gate_n[:, :, :], ps[:, 0, 0:2 * P].rearrange("p (t c) -> p t c", t=2)[:, :, 0:24]))
            dve.wait_ge(w_used, W_BRANCH)
            own.loose(v.tensor_copy(kc_p[:, 0, :], ps[:, 6, 0:17]))
            own(v.tensor_copy(kc_p[:, 1, :], ps[:, 7, 0:17]))
            for c in range(2):
                TS(kc_p[:, c, 0:NCMP_P], kc_p[:, c, 0:NCMP_P], kc_p[:, c, 16:17], None, ALU.add).then_inc(comp_sb, 1)
                TS((kc_dk[:, :], vc_dT)[c], ps[:, 4 + c, 0:NB * NCMP_D], kc_p[:, c, 16:17], None, ALU.add).then_inc(comp_sb, 1)
            dve.wait_ge(vct_mm, 1)
            own.loose(v.tensor_copy(vc_pn[:, :], ps[0:NCMP_P, 1, 0:P]))
            for i in range(2):
                own.loose(v.tensor_copy(vc_dn[:, 4 * i:4 * i + 4, :].rearrange("p b c -> p (b c)"), ps[0:NCMP_D, 2 + i, :]))
            own.settle()
            v.engine_nop().then_inc(vct_sb, 1)
            dve.wait_ge(biasd_mm, 1)
            for m in range(2):
                own.loose(v.tensor_copy(biasd[:, m, 0:1024], ps[0:ROWS, 4 + 2 * m:6 + 2 * m, :].rearrange("p a b -> p (a b)")))
                own.loose(v.tensor_copy(biasd[:, m, 1024:1025], ps[0:ROWS, 0, 256 + m:257 + m]))
            own.settle()
            v.engine_nop().then_inc(biasd_sb, 1)

            dve.wait_ge(bias_in, 16)

            def add_bias(u, j, s, early):
                dve.wait_ge(qk_mm, u + 1)
                if not early:
                    dve.wait_ge(tp_mm, u + (-1))
                bank, b = 2 * (s % 2), s % 2
                buf, mx = s_p[:, b, :], small[:, 8 * b:8 * b + 4]
                if s == 0:
                    for t in range(2):
                        own.loose(STT(buf[:, t * 30:(t + 1) * 30].rearrange("p (r n) -> p r n", r=2),
                            ps[:, bank, t * 30:(t + 1) * 30].rearrange("p (r n) -> p r n", r=2), SCALE,
                            bc_keep[:, :].rearrange("p (t n h) -> p t h n", t=2, h=8)[:, t, bass.ds(j * 2, 2), :], ALU.mult, ALU.add))
                    own.settle()
                    v.tensor_reduce(mx, buf[:, 0:60].rearrange("p (i n) -> p i n", i=4), AXX, ALU.max, negate=True).then_inc(mx_sb, 1)
                    v.engine_nop().then_inc(s_sb_, 1)
                else:
                    h0 = j * 2 + (8 if s == 3 else 0)
                    bias = bias_p[:, bass.ds(h0, 2), :]
                    own.loose(STT(buf[:, 0:512].rearrange("p (r k) -> p r k", r=2), ps[:, bank, :].rearrange("p (r k) -> p r k", r=2), SCALE,
                        bias, ALU.mult, ALU.add))
                    own.loose(STT(buf[:, 512:768].rearrange("p (r k) -> p r k", r=2), ps[:, bank + 1, 0:256].rearrange("p (r k) -> p r k", r=2), SCALE,
                        bias_p[:, bass.ds(h0, 2), P:TP], ALU.mult, ALU.add))
                    own.settle()
                    own(v.tensor_reduce(mx[:, 2:4], buf[:, 0:512].rearrange("p (i n) -> p i n", i=2), AXX, ALU.max, negate=True))
                    v.tensor_reduce(mx[:, 0:2], buf[:, 512:768].rearrange("p (i n) -> p i n", i=2), AXX, ALU.max, negate=True).then_inc(mx_sb, 1)
                    v.engine_nop().then_inc(s_sb_, 1)

            def weigh(u, j, s, first):
                b = s % 2
                dve.wait_ge(exp_sb, u * 4 + 4)
                if not (first and s == 0):
                    dve.wait_ge(o_sb, u)
                sums, wt = small[:, 8 * b + 4:8 * b + 8], small[:, 16:20]
                if s == 0:
                    own(v.reciprocal(wt, sums))
                    own(TT(wt.rearrange("p (t r) -> p t r", t=2), wt.rearrange("p (t r) -> p t r", t=2),
                           cst[:, C_MASKC:C_MASKC + 2].unsqueeze(2).broadcast_to([P, 2, 2]), ALU.mult))
                else:
                    own(v.reciprocal(wt, sums))
                if s < 3:
                    own(TT(wt.rearrange("p (t r) -> p t r", t=2), wt.rearrange("p (t r) -> p t r", t=2),
                           gate_n[:, :, bass.ds(j * 6 + s, 4)][:, :, 0:4:3], ALU.mult))
                dve.wait_ge(tp_mm, u + 1)
                n = 384 if s else 256
                rows = P if s else NCMP_P
                v.tensor_copy(pT[0:rows, n:2 * n], ps[0:rows, 5, 0:n]).then_inc(pt_v, 1)
                dve.wait_ge(pv_mm, u + 1)
                out = o_n[:, :, bass.ds(j * 2 + (8 if s == 3 else 0), 2), :]
                src = ps[:, 6 + b, 0:256].rearrange("p (t r d) -> p t r d", t=2, r=2)
                wb = wt.rearrange("p (t r) -> p t r", t=2).unsqueeze(3).broadcast_to([P, 2, 2, HD])
                if s in (0, 3):
                    TT(out, src, wb, ALU.mult).then_inc(o_sb, 1)
                else:
                    own(TT(o_part[:, :].rearrange("p (t r d) -> p t r d", t=2, r=2), src, wb, ALU.mult))
                    TT(out, out, o_part[:, :].rearrange("p (t r d) -> p t r d", t=2, r=2), ALU.add).then_inc(o_sb, 1)

            def body(j, first, last):
                for s in range(4):
                    if not (last and s == 3):
                        nj = j if s < 3 else j + 1
                        add_bias(j * 4 + (s + 1), nj, (s + 1) % 4, first and s == 0)
                    weigh(j * 4 + s, j, s, first)

            add_bias(0, 0, 0, True)
            before = own.off
            body(0, True, False)
            per = own.off - before
            turns = NPAIR - 2
            with dve.Fori(0, turns) as i:
                own.enter(i, per)
                body(i + 1, False, False)
            own.leave(turns)
            body(NPAIR - 1, False, True)

            for r in range(2):
                rows = slice(r * HD, (r + 1) * HD)
                def put(i):
                    return ez[rows, i, :].rearrange("p (b h) -> p h b", h=8)
                q = lambda t: feat[rows, t:t + 4, TP:T]
                own.loose(STT(put(0)[:, r:8:2, :], q(T_QB), SCALE, feat[rows, T_KB:T_KB + 4, TP:T], ALU.mult, ALU.mult))
                for i, t in ((1, T_KS), (2, T_KW)):
                    own.loose(STT(put(i)[:, 4 * r:4 * r + 4, :], q(T_QA), SCALE,
                        feat[rows, t:t + 1, TP:T].broadcast_to([HD, 4, NB]), ALU.mult, ALU.mult))
            own.loose(TT(gz[:, :].rearrange("p (b h) -> p b h", h=8), feat[0:24, T_GATE, TP:T].unsqueeze(2).broadcast_to([24, NB, 8]),
                   cst[0:24, C_M24:C_M24 + 8].unsqueeze(1).broadcast_to([24, NB, 8]), ALU.mult))
            own.settle()
            v.engine_nop().then_inc(ez_sb, 1)

            dve.wait_ge(oT_mm, 1)
            dve.wait_ge(qbd_sb, 1)
            for g in range(4):
                tt, c0 = divmod(g * 4, 8)
                own.loose(v.tensor_copy(oT[:, c0:c0 + 4, tt * P:(tt + 1) * P], ps[:, g, :].rearrange("p (k t) -> p k t", k=4)))
            own.settle()
            v.engine_nop().then_inc(oT_v, 1)

            R = ROWS
            sm = small[0:R, :]
            dve.wait_ge(small_mm, 1)
            own.loose(v.tensor_copy(sm[:, 20:23], ps[0:R, 6, 0:3]))
            own(v.tensor_copy(sm[:, 28:31], ps[0:R, 6, 8:11]))
            dve.wait_ge(sd_mm, 1)

            def drop_one(score, n, mask, tmp):
                own(v.tensor_reduce(sm[:, 44:45], score, AXX, ALU.min))
                own(TS(tmp, score, sm[:, 44:45], None, ALU.is_equal))
                own(TT(tmp, tmp, cst[0:R, C_IDX + 1:C_IDX + 1 + n], ALU.mult))
                own(v.tensor_reduce(sm[:, 45:46], tmp, AXX, ALU.max))
                own(TS(mask, cst[0:R, C_IDX + 1:C_IDX + 1 + n], sm[:, 45:46], NEG, ALU.is_equal, ALU.mult))

            own(TT(pc, ps[0:R, 5, 0:NCMP_D], biasd[:, 0, 31:1024:16], ALU.add))
            v.tensor_reduce(sm[:, 32:33], pc, AXX, ALU.max, negate=True).then_inc(dmax_sb, 1)
            own(v.tensor_reduce(sm[:, 48:52], ps[0:R, 0:2, :].rearrange("p a (n k) -> p (a n) k", k=256), AXX, ALU.add))
            drop_one(sm[:, 48:52], 4, sm[:, 52:56], sm[:, 56:60])
            for n in range(4):
                own.loose(STT(pm[:, n * 256:(n + 1) * 256], ps[0:R, n // 2, (n % 2) * 256:(n % 2 + 1) * 256], sm[:, 52 + n:53 + n],
                    biasd[:, 1, n * 256:(n + 1) * 256], ALU.add, ALU.add))
            own.loose(TT(pm[:, 1024:1025], sm[:, 20:21], biasd[:, 1, 1024:1025], ALU.add))
            own.settle()
            dve.wait_ge(dmax_sb, 1)
            v.tensor_reduce(sm[:, 33:34], pm, AXX, ALU.max, negate=True).then_inc(dmax_sb, 1)
            dve.wait_ge(dexp_sb, 1)
            own(v.reciprocal(sm[:, 40:41], sm[:, 36:37]))
            own(TS(pc, pc, sm[:, 40:41], None, ALU.mult))
            v.engine_nop().then_inc(imp_rd, 1)
            dve.wait_ge(imp_mm, 1)
            own(v.tensor_copy(imp[:, :], ps[0:R, 7, 0:NCMP_D]))
            own(TT(seg[:, :], imp[:, 4:60], imp[:, 3:59], ALU.add))
            own(v.tensor_reduce(blk[:, 0:14], seg[:, :].rearrange("p (n k) -> p n k", k=4), AXX, ALU.add))
            own(v.memset(blk[:, 16:32], 0.0))
            drop_one(blk[:, 0:14], 14, blk[:, 17:31], blk[:, 32:46])
            own(TT(psl[:, 0:1024], ps[0:R, 2:4, :].rearrange("p a b -> p (a b)"), biasd[:, 0, 0:1024], ALU.add))
            own.loose(TT(psl[:, 0:1024].rearrange("p (n k) -> p n k", k=64), psl[:, 0:1024].rearrange("p (n k) -> p n k", k=64),
                   blk[:, 16:32].unsqueeze(2).broadcast_to([R, 16, 64]), ALU.add))
            own.loose(TT(psl[:, 1024:1025], sm[:, 21:22], biasd[:, 0, 1024:1025], ALU.add))
            own.settle()
            v.tensor_reduce(sm[:, 34:35], psl, AXX, ALU.max, negate=True).then_inc(dmax_sb, 1)
            own.loose(TT(pw[:, 0:512], ps[0:R, 4, :], biasd[:, 0, 512:1024], ALU.add))
            own.loose(TT(pw[:, 512:513], sm[:, 22:23], biasd[:, 0, 1024:1025], ALU.add))
            own.settle()
            v.tensor_reduce(sm[:, 35:36], pw, AXX, ALU.max, negate=True).then_inc(dmax_sb, 1)
            dve.wait_ge(dexp_sb, 4)
            own(v.reciprocal(sm[:, 41:44], sm[:, 37:40]))
            own(TT(sm[:, 42:44], sm[:, 42:44], sm[:, 29:31], ALU.mult))
            own.loose(TS(pc, pc, sm[:, 28:29], None, ALU.mult))
            own.loose(TS(pm, pm, sm[:, 41:42], None, ALU.mult))
            own.loose(TS(psl, psl, sm[:, 42:43], None, ALU.mult))
            own.loose(TS(pw, pw, sm[:, 43:44], None, ALU.mult))
            own.settle()
            for i, p_new in enumerate((pm[:, 1024:1025], psl[:, 1024:1025], pw[:, 512:513])):
                own.loose(TS(sm[:, 64 + 8 * i:72 + 8 * i], cst[0:R, C_HM:C_HM + 8], p_new, None, ALU.mult))
            own.settle()
            v.engine_nop().then_inc(pd_sb, 1)
            dve.wait_ge(pdt_mm, 1)
            own.loose(v.tensor_copy(pTm, ps[:, 0, :].rearrange("p (g r) -> p g r", r=ROWS)))
            own.loose(v.tensor_copy(pTs, ps[:, 1, :].rearrange("p (g r) -> p g r", r=ROWS)))
            own.loose(v.tensor_copy(pTw, ps[:, 2, 0:256].rearrange("p (g r) -> p g r", r=ROWS)))
            own.loose(v.tensor_copy(pTc, ps[0:NCMP_D, 2, 256:320]))
            own.settle()
            v.engine_nop().then_inc(pdt_sb, 1)
            dve.wait_ge(pnew_mm, 1)
            own(v.tensor_copy(sm[0:NB, 96:120], ps[0:NB, 6, 16:40]))
            TT(pnz[:, :, :], sm[0:NB, 96:120].unsqueeze(1).broadcast_to([NB, NB, 24]),
               cst[0:NB, C_DIAG:C_DIAG + 8].unsqueeze(2).broadcast_to([NB, NB, 24]), ALU.mult).then_inc(pnz_sb, 1)
            for b in range(NB):
                dve.wait_ge(od_mm, b + 1)
                if b >= 2:
                    dve.wait_ge(oc_mm, b - 1)
                own(TT(sel_n[:, b % 2, :], ps[0:NB, 5 + 2 * (b % 2), 0:P], cst[0:NB, C_MN:C_MN + P], ALU.mult))
                TT(sel_m[:, b % 2, :], ps[0:NB, 4 + 2 * (b % 2), :], cst[0:NB, C_MM:C_MM + 512], ALU.mult).then_inc(od_sb, 1)
            dve.wait_ge(oc_mm, NB)
            v.tensor_copy(oT[:, :, TP:T], ps[:, 3, 0:64].rearrange("p (b k) -> p k b", k=8)).then_inc(oTd_sb, 1)

            for n in range(8):
                dve.wait_ge(w_used, W_BRANCH + n + 1)
                bank = 4 + 2 * (n % 2)
                own.loose(TT(mT[:, n, :], ps[:, bank, 0:T], feat[:, T_MRG + n, :], ALU.mult))
                own.loose(TT(mtmp[:, 0:T], ps[:, bank + 1, 0:T], feat[:, T_MRG + 8 + n, :], ALU.mult))
                own.settle()
                TT(mT[:, n, :], mT[:, n, :], mtmp[:, 0:T], ALU.add).then_inc(m_sb, 1)
                dve.wait_ge(m_sb, n + 1)
            dve.wait_ge(x_in, 32)
            for n in range(8):
                dve.wait_ge(w_used, W_OUT + n + 1)
                cols = slice(n * P, (n + 1) * P)
                own(STT(x_n[:, 0:2, cols], x_n[:, 0:2, cols], ALPHA, ps[:, n % 2, 0:2 * P].rearrange("p (t c) -> p t c", t=2), ALU.mult, ALU.add))
                STT(x_n[0:NB, 2, cols], x_n[0:NB, 2, cols], ALPHA, ps[0:NB, n % 2, 2 * P:3 * P], ALU.mult, ALU.add).then_inc(mix_sb, 1)
            dve.wait_ge(mix_sb, 8)
            dve.wait_ge(ln_in, 64)

            norms = [0]

            def layer_norm(tt, g, done):
                r = P if tt < 2 else NB
                xr = x_n[0:r, tt, :]
                own.loose(v.bn_stats(stats[0:r, 0:6], xr[:, 0:512]))
                own.loose(v.bn_stats(stats[0:r, 6:12], xr[:, 512:1024]))
                own.settle()
                own(v.bn_aggr(stats[0:r, 12:14], stats[0:r, 0:12].rearrange("p (a b) -> p a b", a=2)))
                TS(stats[0:r, 14:15], stats[0:r, 13:14], EPS, None, ALU.add).then_inc(var_sb, 1)
                dve.wait_ge(std_sb, norms[0] + 1)
                norms[0] += 1
                own(v.reciprocal(stats[0:r, 14:15], stats[0:r, 15:16]))
                own(TS(xr, xr, stats[0:r, 12:13], stats[0:r, 14:15], ALU.subtract, ALU.mult))
                own(TT(xr, xr, ln_rows[0:r, g, :], ALU.mult))
                TT(xr, xr, ln_rows[0:r, g + 1, :], ALU.add).then_inc(done, 1)

            for tt in range(3):
                layer_norm(tt, 0, h_sb)
            for tt in range(3):
                r = P if tt < 2 else NB
                dve.wait_ge(hT_mm, tt + 1)
                bk = 2 + 2 * tt if tt < 2 else 6
                for half in range(2):
                    own.loose(v.tensor_copy(xT[:, half * 4:half * 4 + 4, tt * P:tt * P + r],
                        ps[:, bk + half, :].rearrange("p (k t) -> p k t", k=4)[:, :, 0:r]))
                own.settle()
                v.engine_nop().then_inc(hT_sb, 1)
            dve.wait_ge(m_sb, 8)
            for n in range(16):
                dve.wait_ge(sc_mm, n + 1)
                own(v.tensor_copy(sc[:, 0:2, n, :], ps[:, 2 + n % 2, 0:2 * P].rearrange("p (t k) -> p t k", t=2)))
                v.tensor_copy(sc[0:NB, 2, n, :], ps[0:NB, 2 + n % 2, 2 * P:3 * P]).then_inc(sc_sb, 1)
            dve.wait_ge(sc_sb, 16)

            def top16(rows, n, width, get, vals, idxs):
                r = rows
                for i in range(n):
                    own.loose(v.max(vals[0:r, i, 0:8], get(i)))
                own.settle()
                for i in range(n):
                    own.loose(v.max_index(idxs[0:r, i, 0:8], vals[0:r, i, 0:8], get(i)))
                own.settle()
                for i in range(n):
                    own.loose(v.match_replace(get(i), vals[0:r, i, 0:8], get(i), -3.0e38))
                own.settle()
                for i in range(n):
                    own.loose(v.max(vals[0:r, i, 8:16], get(i)))
                own.settle()
                for i in range(n):
                    own.loose(v.max_index(idxs[0:r, i, 8:16], vals[0:r, i, 8:16], get(i)))
                own.settle()

            for tt in range(3):
                r = P if tt < 2 else NB
                top16(r, 16, 128, lambda i: sc[0:r, tt, i, :], val, idu)
                own(v.tensor_copy(idf[0:r], idu[0:r]))
                c4 = cand[0:r].rearrange("p (h i j) -> p h i j", h=8, i=16)
                own(TT(c4, val[0:r, 0:16:2, :].unsqueeze(3).broadcast_to([r, 8, 16, 16]),
                       val[0:r, 1:16:2, :].unsqueeze(2).broadcast_to([r, 8, 16, 16]), ALU.add))
                gv = gk[:, tt, :].rearrange("p (h k) -> p h k", h=8)
                fp = fpos.rearrange("p (h k) -> p h k", h=8)
                top16(r, 8, 256, lambda i: cand[0:r, i * 256:(i + 1) * 256], gv, fp)
                own(v.tensor_copy(ghi[0:r], gv[0:r, :, 0]))
                TT(gv[0:r], gv[0:r], ghi[0:r].unsqueeze(2).broadcast_to([r, 8, 16]), ALU.subtract).then_inc(fsub_sb, 1)
                io = cst[0:r, C_IDX:C_IDX + 16].unsqueeze(1).broadcast_to([r, P, 16])
                oh3 = oneh[0:r].rearrange("p (q i) -> p q i", i=16)
                oh4 = oneh[0:r].rearrange("p (h k i) -> p h k i", h=8, k=16)
                for half, dst in ((0, ea), (1, eb)):
                    if half == 0:
                        own(TS(fi[0:r], fpos[0:r], 4, None, ALU.logical_shift_right))
                    else:
                        own(TS(fi[0:r], fpos[0:r], 15, None, ALU.bitwise_and))
                    own(v.tensor_copy(fif[0:r], fi[0:r]))
                    own(TT(oh3, fif[0:r].unsqueeze(2).broadcast_to([r, P, 16]), io, ALU.is_equal))
                    own(TT(oh4, oh4, idf[0:r, half:16:2, :].unsqueeze(2).broadcast_to([r, 8, 16, 16]), ALU.mult))
                    own(v.tensor_reduce(dst[0:r], oh3, AXX, ALU.add))
                own(STT(ea[0:r], ea[0:r], 128.0, eb[0:r], ALU.mult, ALU.add))
                own(v.tensor_copy(eidx[0:r, tt, :], ea[0:r]))
                dve.wait_ge(gexp_sb, tt + 1)
                own(v.tensor_reduce(gsum[0:r], gv[0:r], AXX, ALU.add))
                own(v.reciprocal(gsum[0:r], gsum[0:r]))
                own(TT(gv[0:r], gv[0:r], gsum[0:r].unsqueeze(2).broadcast_to([r, 8, 16]), ALU.mult))
                v.engine_nop().then_inc(e_sb, 1)

            for tt in range(3):
                own.loose(v.memset(acc[tt], 0.0))
            own.settle()

            def dot(q, half, hrow, group):
                for s in range(UNROLL):
                    slot = half * UNROLL + s
                    dve.wait_ge(u_in[slot], group * 16 + 16)
                    v.tensor_tensor_reduce(out=u_rows[:, slot, :], in0=u_rows[:, slot, :], in1=hrow, scale=1.0, scalar=0.0,
                                           op0=ALU.mult, op1=ALU.add, accum_out=dots[:, half, s:s + 1]).then_inc(u_used, 1)

            def weighted(q, half, weights, tt, group):
                dve.wait_ge(gel_sb, q + 1)
                own(TT(wts[:, half, :], gel[:, half, :], weights, ALU.mult))
                for s in range(UNROLL):
                    slot = half * UNROLL + s
                    dve.wait_ge(v_in[slot], group * 16 + 16)
                    STT(acc[tt], v_rows[:, slot, :], wts[:, half, s:s + 1], acc[tt], ALU.mult, ALU.add).then_inc(v_used, 1)
                    dve.wait_ge(v_used, q * UNROLL + (s + 1))

            for tt in range(2):
                hrow = x_n[:, tt, :]
                q0, g0 = tt * HALVES, tt * 16
                dot(q0, 0, hrow, g0)
                with dve.Fori(0, 15) as i:
                    own.enter(i, 2)
                    dot(None, 1, hrow, i + g0)
                    weighted(i * 2 + q0, 0, gk[:, tt, bass.ds(i * 8, UNROLL)], tt, i + g0)
                    dot(None, 0, hrow, i + (g0 + 1))
                    weighted(i * 2 + (q0 + 1), 1, gk[:, tt, bass.ds(i * 8 + UNROLL, UNROLL)], tt, i + g0)
                own.leave(15)
                dot(None, 1, hrow, g0 + 15)
                weighted(q0 + 30, 0, gk[:, tt, 120:124], tt, g0 + 15)
                weighted(q0 + 31, 1, gk[:, tt, 124:128], tt, g0 + 15)
            dve.wait_ge(hrep_in, 16)
            dve.wait_ge(gks_in, 16 * NH)
            dot(None, 0, h_rep, 32)
            dot(None, 1, h_rep, 32)
            weighted(64, 0, gk_s[:, 0:4], 2, 32)
            weighted(65, 1, gk_s[:, 4:8], 2, 32)
            for tt in range(2):
                own(STT(x_n[:, tt, :], x_n[:, tt, :], ALPHA, acc[tt], ALU.mult, ALU.add))
                layer_norm(tt, 2, y_sb)
            dve.wait_ge(sum_mm, 1)
            own(STT(x_n[0:NB, 2, :], x_n[0:NB, 2, :], ALPHA, ps[0:NB, 0:2, :].rearrange("p a b -> p (a b)"), ALU.mult, ALU.add))
            layer_norm(2, 2, y_sb)


OUT_SHAPES = {
    "y_prompt": (TP, D), "y_sample": (NB, D), "nsa_prompt": (TP, 512), "moba_prompt": (TP, 1024),
    "win_prompt": (TP, 256), "nsa_sample": (NB, 512), "moba_sample": (NB, 1024), "win_sample": (NB, 512, 256),
}
OUT_NAMES = list(OUT_SHAPES)


def bucket(np, n):
    n = np.asarray(n)
    nf = np.maximum(n, 1).astype(np.float32)
    large = 16 + (np.log(nf / np.float32(16)) / math.log(1024 / 16) * 16).astype(np.int32)
    return np.where(n < 16, n, np.minimum(large, 31))


def shape_constants(np):
    def one_hot(dist):
        flat = np.asarray(dist).reshape(-1)
        oh = np.zeros((33, flat.size), np.float32)
        rows = np.where(flat < 0, 32, bucket(np, np.maximum(flat, 0)))
        oh[rows, np.arange(flat.size)] = 1.0
        return oh

    t = np.arange(P)
    rev = one_hot(255 - np.arange(384))
    ends = 16 * np.arange(NCMP_P) + 31
    dist_c = np.stack([[(tt * P + t) - e for e in ends] for tt in range(2)])
    onehot = np.concatenate([rev, one_hot(dist_c), one_hot(PAST - np.arange(PAST))], axis=1)
    c = np.zeros((P, NCONST), np.float32)
    r = np.arange(ROWS)
    c[:, C_ID:C_ID + P] = np.eye(P)
    c[:, C_ONE:C_ONE + P] = 1
    c[:, C_MASKC:C_MASKC + 2] = (dist_c[:, 0] >= 0).T
    c[:ROWS, C_HM:C_HM + 8] = (r % 8)[:, None] == np.arange(8)
    c[:ROWS, C_GSUM:C_GSUM + ROWS] = (r // 4)[:, None] == (r // 4)
    c[:ROWS, C_SELB:C_SELB + 8] = (r // 8)[:, None] == np.arange(8)
    c[:, C_IDX:C_IDX + 16] = np.arange(16)
    c[:8, C_DIAG:C_DIAG + 8] = np.eye(8)
    c[:8, C_MM:C_MM + 512] = np.arange(8)[:, None] == np.arange(512) // 64
    c[:8, C_MN:C_MN + P] = (np.arange(8) // 4)[:, None] == np.arange(P) // 64
    c[:8, C_JS:C_JS + 4] = (np.arange(8) % 4)[:, None] == np.arange(4)
    q = np.arange(24)
    c[:24, C_M24:C_M24 + 8] = (q // 6 + 4 * (q // 3 % 2))[:, None] == np.arange(8)
    c[:24, C_B24:C_B24 + 3] = (q % 3)[:, None] == np.arange(3)
    c[:, C_KRED:C_KRED + 8] = (np.arange(P) // 16)[:, None] == np.arange(8)
    return onehot, c


def kernel(**inputs):
    import numpy as np
    import concourse.bacc as bacc
    from concourse.bass_utils import run_bass_kernel_spmd as run

    i = {k: np.asarray(v) for k, v in inputs.items()}
    pair = [h for j in range(4) for h in (j, j + 4)]
    w = i["w_in"][0]
    cols = lambda lo, n: w[:, lo:lo + n]
    wq_a = cols(0, 512).reshape(D, 8, 64)[:, pair].reshape(D, 512)
    gate = cols(1280, 24).reshape(D, 8, 3)[:, pair].reshape(D, 24)
    gate = np.concatenate([gate, np.zeros((D, P - 24), np.float32)], axis=1)
    w_feat = np.concatenate([wq_a, cols(1304, 512), cols(512, 512), cols(1024, 256), cols(1816, 1024), gate, cols(2840, 2048)], axis=1)

    def tiles(m):
        k, n = m.shape
        return m.reshape(k // P, P, n // P, P).transpose(2, 1, 0, 3).reshape(n // P, P, k)

    cw = i["nsa_cmp_w"][0]
    conv = np.zeros((2, 4, P, 8, P), np.float32)
    cw8 = cw.reshape(2, 4, 8, 64, 64)
    for g in range(2):
        conv[:, :, g * 64:(g + 1) * 64, :, g * 64:(g + 1) * 64] = cw8.transpose(0, 1, 3, 2, 4)
    wa = i["w_branch_a"][0].reshape(8, 64, D)[pair].reshape(512, D)
    branch = np.concatenate([wa, i["w_branch_b"][0]], axis=0)
    wall = np.concatenate([tiles(w_feat), conv.reshape(8, P, D), tiles(branch), tiles(i["w_out"][0]), tiles(i["peer_wq"][0])], axis=0)

    x_all = np.concatenate([i["x_prompt"][0], i["x_sample"][:, 0]], axis=0)
    nsa = i["cache_nsa"][0]
    moba = i["cache_moba"][0]
    pool = nsa.shape[0]
    col = lambda m: m.reshape(pool, PAGE, P).transpose(0, 2, 1)
    pack_cmp = np.stack([col(nsa[:, :, 0]), col(nsa[:, :, 1])], axis=2)
    k_m = moba[:, :, 0].reshape(pool, PAGE, 4, P).transpose(0, 3, 2, 1).reshape(pool, P, 512)
    pack_k = np.concatenate([k_m, col(nsa[:, :, 2])], axis=2)
    pack_v = np.concatenate([moba[:, :, 1].reshape(pool, PAGE, 512), nsa[:, :, 3].reshape(pool, PAGE, P)], axis=2)
    win = i["state_nsa_win"][0]
    win_kT = win[:, :, 0].reshape(NB, 512, P).transpose(0, 2, 1)
    win_vr = win[:, :, 1].reshape(NB, 4, P, P).transpose(0, 2, 1, 3).reshape(NB, P, 512)
    pe = i["nsa_cmp_pe"][0].transpose(2, 0, 1)
    rb = i["rel_bias"]
    rb_p = rb[:, pair + list(range(8, 16))]
    tab_ext = np.concatenate([rb_p, np.full((1, 16), NEG, np.float32)], axis=0)
    tab_dec = np.stack([np.tile(rb[:, 0:8], (1, NB)), np.tile(rb[:, 8:16], (1, NB))], axis=1)
    onehot, consts = shape_constants(np)
    keysT = i["peer_keys"][0].reshape(16, P, P).transpose(2, 0, 1)
    arrays = {
        "tab_ext": tab_ext, "tab_dec": tab_dec, "onehot": onehot, "consts": consts,
        "xT": x_all.T.reshape(KD, P, T).transpose(1, 0, 2).reshape(P, KD * T),
        "x_prompt": i["x_prompt"][0], "x_sample": i["x_sample"][:, 0], "wall": wall,
        "win_state": win.reshape(NB, 512, 256), "page_table": i["page_table"].reshape(1, NB * NPG),
        "pack_cmp": pack_cmp, "pack_kv": np.stack([pack_k, pack_v]), "win_kT": win_kT, "win_vr": win_vr,
        "peT": np.concatenate([pe, pe], axis=0), "keysT": keysT,
        "ln1_g": i["ln1_g"], "ln1_b": i["ln1_b"], "ln2_g": i["ln2_g"], "ln2_b": i["ln2_b"],
        "peer_u": i["peer_u"][0], "peer_v": i["peer_v"][0],
    }
    nc = bacc.Bacc("TRN2", target_bir_lowering=False, num_devices=1)
    feeds, aps = {}, {}
    for name, v in arrays.items():
        v = np.ascontiguousarray(v)
        feeds[name] = v
        aps[name] = nc.dram_tensor(name, v.shape, mybir.dt.from_np(v.dtype), kind="ExternalInput").ap()
    for name, shape in OUT_SHAPES.items():
        aps[name] = nc.dram_tensor(name, shape, F32, kind="ExternalOutput").ap()
    hybrid_layer(nc, aps)
    r = run(nc, [feeds], core_ids=[0]).results[0]
    return (
        r["y_prompt"].reshape(1, TP, D), r["y_sample"].reshape(NB, 1, D),
        r["nsa_prompt"].reshape(1, 1, TP, 4, 2, 64), r["moba_prompt"].reshape(1, 1, TP, 2, 8, 64),
        r["win_prompt"].reshape(1, 1, TP, 2, 2, 64), r["nsa_sample"].reshape(1, NB, 1, 4, 2, 64),
        r["moba_sample"].reshape(1, NB, 1, 2, 8, 64), r["win_sample"].reshape(1, NB, 512, 2, 2, 64),
    )
```

```python
import math
from contextlib import ExitStack

import concourse.bass as bass
from concourse import mybir

F32 = mybir.dt.float32
U32 = mybir.dt.uint32
I32 = mybir.dt.int32
ALU = mybir.AluOpType
ACT = mybir.ActivationFunctionType
AXX = mybir.AxisListType.X

P = 128
D = 1024
KD = D // P
TP = 256
NB = 8
T = TP + NB
HD = 64
NPAIR = 4
PAST = 1024
PAGE = 128
NPG = PAST // PAGE
NCMP_P = TP // 16 - 1
NCMP_D = PAST // 16 - 1
NEG = -1e30
SCALE = HD ** -0.5
ALPHA = 2.0 ** 0.25
EPS = 1e-5
ROWS = NB * 8
TOPK = 16
NH = 8

T_QA, T_QB, T_KC, T_VC, T_KS, T_VS, T_KW, T_VW, T_KB, T_VB, T_GATE, T_MRG = 0, 4, 8, 9, 10, 11, 12, 13, 14, 18, 22, 23
NT_IN = T_MRG + 16
KV0 = T_KC
NKV = T_GATE - T_KC
W_CONV = T_MRG
W_MRG = W_CONV + 8
W_BRANCH = W_MRG + 16
W_OUT = W_BRANCH + 8
W_Q = W_OUT + 8
NW = W_Q + 16
RING = 8
PGRING = 3
PGW = 640
UNROLL = 4
GROUPS = 4
HEAD_T = 2
TURN0 = (0, P // 8, P // 4)
TURNS = P // 4 + 1
AHEAD = 6

C_ID = 0
C_ONE = C_ID + P
C_MASKC = C_ONE + P
C_HM = C_MASKC + 2
C_GSUM = C_HM + 8
C_SELB = C_GSUM + ROWS
C_IDX = C_SELB + 8
C_DIAG = C_IDX + 16
C_MM = C_DIAG + 8
C_MN = C_MM + 512
C_JS = C_MN + P
C_M24 = C_JS + 4
C_B24 = C_M24 + 8
C_KRED = C_B24 + 3
NCONST = C_KRED + 8


def ring_slots():
    slots, before, loads, last, count = [], [], [], {}, {}
    for n in range(NW):
        slot = n % RING if n < W_MRG else (n - W_MRG) % PGRING if n < W_BRANCH else (n - W_BRANCH) % RING
        if n >= W_BRANCH and n - W_BRANCH < RING and slot >= PGRING:
            last[slot] = None
        slots.append(slot)
        before.append(last.get(slot))
        last[slot] = n
        count[slot] = count.get(slot, 0) + 1
        loads.append(count[slot])
    return slots, before, loads


W_SLOT, W_BEFORE, W_LOADS = ring_slots()


def found(tt, h):
    return h + 1 if tt == 0 else h * 2 + (NH + 1)


class Chain:

    def __init__(self, eng, sem):
        self.eng, self.sem, self.base, self.off = eng, sem, 0, 0

    def __call__(self, ins):
        self.off += 1
        ins.then_inc(self.sem, 1)
        self.eng.wait_ge(self.sem, self.base + self.off)

    def loose(self, ins):
        self.off += 1
        ins.then_inc(self.sem, 1)

    def settle(self):
        self.eng.wait_ge(self.sem, self.base + self.off)

    def enter(self, i, per, first=0):
        self.start, self.per = self.base + self.off, per
        self.base, self.off = i * per + (self.start - first * per), 0

    def leave(self, turns):
        assert self.off == self.per, (self.off, self.per)
        self.base, self.off = 0, self.start + turns * self.per


def hybrid_layer(nc, a):
    ctx = ExitStack()
    with ctx:
        def sb(name, shape, dt=F32):
            return ctx.enter_context(nc.sbuf_tensor(name, shape, dt))

        def sem(name):
            return ctx.enter_context(nc.semaphore(name))

        cst = sb("cst", [P, NCONST])
        x_n = sb("x_n", [P, 3, D])
        xT_r = sb("xT_r", [P, KD * T])
        feat_r = sb("feat_r", [P, NT_IN * T])
        kv_n = sb("kv_n", [P, 2, NKV, P])
        ring = sb("ring", [P, RING, D])
        big = sb("big", [P, 16384])
        pg_r = sb("pg_r", [P, NPG * PGW])
        ps = ctx.enter_context(nc.psum_tensor("ps", [P, 8, 512], F32))
        tabx = sb("tabx", [33, 16])
        tabd = sb("tabd", [32, 2, ROWS])
        kc_p = sb("kc_p", [P, 2, 17])
        vc_pn = sb("vc_pn", [NCMP_P, P])
        gate_n = sb("gate_n", [P, 2, 24])
        ptab = sb("ptab", [1, NB * NPG], I32)
        small = sb("small", [P, 128])

        ident = cst[:, C_ID:C_ID + P]
        feat = feat_r[:, :].rearrange("p (n t) -> p n t", t=T)
        xT = xT_r[:, :].rearrange("p (k t) -> p k t", t=T)
        ct = big[:, :].rearrange("p (c b n s) -> p c b n s", c=2, b=NB, s=16)
        bias_p = pg_r[:, 0:4096].rearrange("p (h k) -> p h k", h=16)
        pages = ring[:, PGRING:RING, :].rearrange("p a b -> p (a b)").rearrange("p (g c) -> p g c", g=NPG)
        xT2 = pg_r[:, 0:KD * T].rearrange("p (k t) -> p k t", t=T)

        o_n = big[:, 0:2048].rearrange("p (t h d) -> p t h d", t=2, h=16)
        qz = big[:, 2048:3072].rearrange("p (m r t) -> p m r t", m=2, r=2)
        s_p = big[:, 3072:4608].rearrange("p (r c) -> p r c", r=2)
        pT = big[:, 4608:5376]
        biasd = big[0:ROWS, 5376:7426].rearrange("p (m k) -> p m k", m=2)
        win_k = big[:, 7426:11522].rearrange("p (b k) -> p b k", b=NB)
        win_v = big[:, 11522:15618].rearrange("p (b c d) -> p b c d", b=NB, c=4)
        pm = big[0:ROWS, 0:1025]
        psl = big[0:ROWS, 1025:2050]
        half0 = pg_r[0:ROWS, 4096:5120].rearrange("p (n k) -> p n k", k=512)
        pw = big[0:ROWS, 2050:2563]
        pc = big[0:ROWS, 2563:2626]
        pTm = big[:, 2626:3138].rearrange("p (g r) -> p g r", r=ROWS)
        pTs = big[:, 3138:3650].rearrange("p (g r) -> p g r", r=ROWS)
        pTw = big[:, 3650:3906].rearrange("p (g r) -> p g r", r=ROWS)
        pTc = big[0:NCMP_D, 3906:3970]
        sel_m = big[0:NB, 3970:4994].rearrange("p (r c) -> p r c", r=2)
        sel_n = big[0:NB, 4994:5250].rearrange("p (r c) -> p r c", r=2)
        mT = big[:, 0:KD * T].rearrange("p (k t) -> p k t", t=T)
        mixT = big[:, 2640:2640 + 2 * T].rearrange("p (r t) -> p r t", r=2)
        oT = feat_r[:, 0:KD * T].rearrange("p (k t) -> p k t", t=T)
        kc_dk = sb("kc_dk", [P, NB * NCMP_D])
        bc_keep = sb("bc_keep", [P, 240])
        x_flat = x_n[:, :, :].rearrange("p t d -> p (t d)")
        brev = x_flat[0:16, 0:384]
        smp_n = x_flat[0:NB, 0:NKV * P].rearrange("p (n c) -> p n c", c=P)
        vc_dn = x_flat[0:NCMP_D, NKV * P:NKV * P + NB * P].rearrange("p (b c) -> p b c", b=NB)
        o_part = big[:, 15618:15874]
        imp, seg, blk = big[0:ROWS, 15874:15937], big[0:ROWS, 15937:15993], big[0:ROWS, 15993:16041]
        mtmp = big[:, 2112:2112 + T]
        stats = sb("stats", [P, 16])
        vc_dT = xT_r[:, 0:NB * NCMP_D]
        kcx = xT_r[:, 576:1152].rearrange("p (c k) -> p c k", c=2)
        qbd_m = xT_r[:, 0:2048].rearrange("p (b j r) -> p b j r", b=NB, j=NPAIR)
        qa_r = sb("qa_r", [P, NB * ROWS])
        qbd_a = qa_r[:, :].rearrange("p (b r) -> p b r", b=NB)
        ez = sb("ez", [P, 3, ROWS])
        gz = sb("gz", [24, ROWS])
        pnz = sb("pnz", [NB, NB, 24])

        scores = feat_r[:, 0:6144]
        keysT = feat_r[:, 6144:8192].rearrange("p (n k) -> p n k", n=16)
        h_rep = feat_r[:, 8192:9216]
        kv_flat = kv_n[:, :, :, :].rearrange("p t n c -> p (t n c)")
        diag = kv_flat[:, 0:2048].rearrange("p (g s k) -> p g s k", g=GROUPS, s=UNROLL)
        qT2 = kv_flat[:, 2048:2048 + 2 * T].rearrange("p (r t) -> p r t", r=2)
        rest = kv_flat[:, 2576:2832].rearrange("p (c k) -> p c k", c=2)
        cand = kv_flat[:, 2832:3088]
        oneh = kv_flat[:, 3088:3344]
        val = kv_flat[:, 3344:3376].rearrange("p (c k) -> p c k", c=2)
        idu = kv_flat[:, 3376:3408].bitcast(U32).rearrange("p (c k) -> p c k", c=2)
        idf = kv_flat[:, 3408:3440].rearrange("p (c k) -> p c k", c=2)
        fpos = kv_flat[:, 3440:3456].bitcast(U32)
        fi = kv_flat[:, 3456:3472].bitcast(U32)
        fif = kv_flat[:, 3472:3488]
        ea = kv_flat[:, 3488:3504]
        eb = kv_flat[:, 3504:3520]
        best = kv_flat[:, 3520:3552].rearrange("p (c k) -> p c k", c=2)
        bexp = kv_flat[:, 3552:3584].rearrange("p (c k) -> p c k", c=2)
        gsum = sb("gsum", [P, 2])
        nbest = sb("nbest", [P, 2])
        alpha_id = qa_r[:, 0:P]
        ln_rows = pg_r[:, 0:4096].rearrange("p (n d) -> p n d", n=4)
        gk = sb("gk", [P, 3, P])
        eidx = sb("eidx", [P, 3, P], U32)
        idx_u = sb("idx_u", [P, 2, UNROLL], U32)
        idx_v = sb("idx_v", [P, 2, UNROLL], U32)
        dots = sb("dots", [P, GROUPS, UNROLL])
        gel = sb("gel", [P, GROUPS, UNROLL])
        wts = sb("wts", [P, GROUPS, UNROLL])
        gk_s = sb("gk_s", [P, 8])
        eidx_s = sb("eidx_s", [P, 8], U32)
        u_rows = big[:, 0:8192].rearrange("p (s d) -> p s d", s=8)
        v_rows = big[:, 8192:16384].rearrange("p (s d) -> p s d", s=8)

        bias_scr = nc.dram_tensor("bias_scr", (16, P, 384), F32).ap()
        h_scr = nc.dram_tensor("h_scr", (NB, D), F32).ap()
        g_scr = nc.dram_tensor("g_scr", (NB, P), F32).ap()
        e_scr = nc.dram_tensor("e_scr", (NB, P), U32).ap()

        cst_in, tab_in, oh_in, pt_in, xT_in, x_in = (sem(n) for n in ("cst_in", "tab_in", "oh_in", "pt_in", "xT_in", "x_in"))
        pe_in = sem("pe_in")
        w_in = [sem(f"w_in{i}") for i in range(RING)]
        w_used = sem("w_used")
        brev_mm, brev_sb, bscr_out, bias_in, biasc_mm, biasc_sb = (
            sem(n) for n in ("brev_mm", "brev_sb", "bscr_out", "bias_in", "biasc_mm", "biasc_sb"))
        proj_sb, gates_sb = sem("proj_sb"), sem("gates_sb")
        kvt_mm, kvt_v, kvt_a = sem("kvt_mm"), sem("kvt_v"), sem("kvt_a")
        ct_in, kcx_sb, comp_sb, vct_mm, vct_sb = (
            sem(n) for n in ("ct_in", "kcx_sb", "comp_sb", "vct_mm", "vct_sb"))
        qza_sb, qzb_sb, qk_mm, s_sb_, mx_sb, exp_sb, tp_mm, pt_v, pt_a, pv_mm, o_sb = (
            sem(n) for n in ("qza_sb", "qzb_sb", "qk_mm", "s_sb", "mx_sb", "exp_sb", "tp_mm", "pt_v", "pt_a", "pv_mm", "o_sb"))
        qz_zero = sem("qz_zero")
        oT_mm, oT_v = sem("oT_mm"), sem("oT_v")
        winpg_in = sem("winpg_in")
        kv_in = [sem("kv_in0"), sem("kv_in1")]
        kv_used = [sem("kv_used0"), sem("kv_used1")]
        biasd_mm, biasd_sb, qbd_sb, ez_sb, sd_mm, small_mm = (
            sem(n) for n in ("biasd_mm", "biasd_sb", "qbd_sb", "ez_sb", "sd_mm", "small_mm"))
        dmax_sb, dexp_sb, imp_rd, imp_mm, pd_sb, pdt_mm, pdt_sb, pnew_mm, pnz_sb = (
            sem(n) for n in ("dmax_sb", "dexp_sb", "imp_rd", "imp_mm", "pd_sb", "pdt_mm", "pdt_sb", "pnew_mm", "pnz_sb"))
        od_mm, od_sb, oc_mm, oTd_sb = (sem(n) for n in ("od_mm", "od_sb", "oc_mm", "oTd_sb"))
        m_sb, mix_sb, ln_in, h_sb, hT_mm, hT_sb = (
            sem(n) for n in ("m_sb", "mix_sb", "ln_in", "h_sb", "hT_mm", "hT_sb"))
        keys_in, q_sb, sc_mm, sc_sb = (sem(n) for n in ("keys_in", "q_sb", "sc_mm", "sc_sb"))
        fsub_sb, gexp_sb, e_sb, hs_out, gs_out, es_out, hrep_in, gks_in, eis_in = (
            sem(n) for n in ("fsub_sb", "gexp_sb", "e_sb", "hs_out", "gs_out", "es_out", "hrep_in", "gks_in", "eis_in"))
        idx_st, idx_go = sem("idx_st"), sem("idx_go")
        u_in = [sem(f"u_in{i}") for i in range(8)]
        v_in = [sem(f"v_in{i}") for i in range(8)]
        u_used, v_used, gel_sb = sem("u_used"), sem("v_used"), sem("gel_sb")
        diag_sb, nm_sb, y_sb, dve_go = sem("diag_sb"), sem("nm_sb"), sem("y_sb"), sem("dve_go")
        var_sb, std_sb = sem("var_sb"), sem("std_sb")
        mgate_sb, mixt_mm, mixt_sb, k_mm, kev_sb, cmp_mm = (sem(n) for n in ("mgate_sb", "mixt_mm", "mixt_sb", "k_mm", "kev_sb", "cmp_mm"))
        MRG_BANK = [(3, 4)[i % 2] for i in range(16)]
        EXP_AFTER = (1, 2, 2, 2)
        out_w, out_kv, out_y = sem("out_w"), sem("out_kv"), sem("out_y")
        dve_own, pool_own, act_own = sem("dve_own"), sem("pool_own"), sem("act_own")

        oh_r = feat_r[0:33, 0:30 * P + 384]
        oh_rev = oh_r[:, 0:384]
        oh_c = oh_r[:, 384:384 + 30 * P].rearrange("p (m t) -> p m t", m=30)
        oh_d = pg_r[0:32, 4096:4096 + PAST]
        block = ctx.enter_context(nc.Block())

        def kind_of(s):
            return ("cmp", "sel", "win", "moba")[s]

        @block.sync
        def _(sp):
            sp.dma_start(tabx[:, :], a["tab_ext"]).then_inc(tab_in, 16)
            sp.dma_start(tabd[:, :, :], a["tab_dec"]).then_inc(tab_in, 16)
            sp.dma_start(oh_r, a["onehot"][:, 0:384 + 30 * P]).then_inc(oh_in, 16)
            sp.dma_start(oh_d, a["onehot"][0:32, 384 + 30 * P:384 + 30 * P + PAST]).then_inc(oh_in, 16)
            sp.dma_start(xT_r[:, :], a["xT"]).then_inc(xT_in, 16)
            sp.dma_start(cst[:, :], a["consts"]).then_inc(cst_in, 16)

            def weight(n):
                if W_BEFORE[n] is not None:
                    sp.wait_ge(w_used, W_BEFORE[n] + 1)
                sp.dma_start(ring[:, W_SLOT[n], :], a["wall"][n]).then_inc(w_in[W_SLOT[n]], 16)

            for n in range(RING):
                weight(n)
            sp.dma_start(a["win_sample"][:, 0:511, :], a["win_state"][:, 1:512, :]).then_inc(out_w, 16)
            turns = W_MRG // RING
            with sp.Fori(1, turns) as it:
                for j in range(RING):
                    sp.wait_ge(w_used, it * RING + (j + 1 - RING))
                    sp.dma_start(ring[:, j:j + 1, :], a["wall"][bass.ds(it * RING + j, 1), :, :].rearrange("a p c -> p a c")
                                 ).then_inc(w_in[j], 16)
            for n in range(turns * RING, W_MRG + PGRING):
                weight(n)
            sp.wait_ge(pt_in, 16)
            sp.wait_ge(w_used, W_MRG)

            def load_chunk(which, b, first_page, buf, uses):
                if uses is not None:
                    sp.wait_ge(kv_used[buf], uses)
                for g in range(4):
                    page = sp.value_load(ptab[0:1, bass.ds(b * NPG + (first_page + g), 1)], min_val=0, max_val=79)
                    sp.dma_start(pages[:, buf * 4 + g:buf * 4 + g + 1, :],
                                 a["pack_kv"][which, bass.ds(page, 1), :, :].rearrange("a p c -> p a c")).then_inc(kv_in[buf], 16)

            for half in range(2):
                if half == 0:
                    for b in range(2):
                        load_chunk(0, b, 0, b, None)
                with sp.Fori(1 - half, NB // 2) as i:
                    for r in range(2):
                        load_chunk(0, i * 2 + r, 4 * half, r, i + NB // 2 * half)
            sp.wait_ge(s_sb_, 4 * NPAIR)
            sp.dma_start(pg_r[:, 0:KD * T], a["xT"]).then_inc(xT_in, 16)
            for n in range(W_MRG + PGRING, W_MRG + 8):
                weight(n)
            with sp.Fori(0, NB) as b:
                for half in range(2):
                    load_chunk(1, b, 4 * half, half, b + NB)
            for n in range(W_MRG + 8, W_BRANCH):
                weight(n)
            sp.wait_ge(od_mm, NB)
            for n in range(W_BRANCH, W_OUT):
                weight(n)
            sp.wait_ge(out_kv, 16 * 9)
            sp.dma_start(x_n[:, 0:2, :], a["x_prompt"].rearrange("(t p) d -> p t d", p=P)).then_inc(x_in, 16)
            sp.dma_start(x_n[0:NB, 2, :], a["x_sample"]).then_inc(x_in, 16)
            for i, nm in enumerate(("ln1_g", "ln1_b", "ln2_g", "ln2_b")):
                sp.wait_ge(w_used, W_BRANCH)
                sp.dma_start(ln_rows[:, i, :], a[nm].broadcast_to([P, D])).then_inc(ln_in, 16)
            for n in range(W_OUT, W_Q):
                weight(n)
            sp.wait_ge(m_sb, 8)
            sp.dma_start(keysT, a["keysT"]).then_inc(keys_in, 16)
            for n in range(W_Q, NW):
                weight(n)
            sp.wait_ge(h_sb, 3)
            sp.dma_start(h_scr, x_n[0:NB, 2, :]).then_inc(hs_out, 16)
            sp.wait_ge(hs_out, 16)
            sp.dma_start(h_rep, h_scr.unsqueeze(1).broadcast_to([NB, TOPK, D])).then_inc(hrep_in, 16)
            sp.wait_ge(y_sb, 1)
            sp.dma_start(a["y_prompt"][0:P, :], x_n[:, 0, :]).then_inc(out_y, 16)
            sp.wait_ge(nm_sb, 3 * NH)
            sp.dma_start(g_scr, gk[0:NB, 2, :]).then_inc(gs_out, 16)
            sp.dma_start(e_scr, eidx[0:NB, 2, :]).then_inc(es_out, 16)
            sp.wait_ge(gs_out, 16)
            sp.wait_ge(es_out, 16)
            with nc.allow_non_contiguous_dma(reason="a small re-layout"):
                for h in range(NH):
                    sp.dma_start(gk_s[:, h:h + 1], g_scr.rearrange("n (h k) -> n k h", h=NH)[:, :, h:h + 1]).then_inc(gks_in, 16)
                    sp.dma_start(eidx_s[:, h:h + 1], e_scr.rearrange("n (h k) -> n k h", h=NH)[:, :, h:h + 1]).then_inc(eis_in, 16)
            sp.wait_ge(y_sb, 2)
            sp.dma_start(a["y_prompt"][P:TP, :], x_n[:, 1, :]).then_inc(out_y, 16)
            sp.wait_ge(y_sb, 3)
            sp.dma_start(a["y_sample"], x_n[0:NB, 2, :]).then_inc(out_y, 16)
            sp.wait_ge(out_y, 48)
            sp.wait_ge(out_w, 16)
            sp.wait_ge(out_kv, 16 * 9)

        @block.gpsimd
        def _(pool):
            own = Chain(pool, pool_own)
            pool.dma_start(ptab[:, :], a["page_table"]).then_inc(pt_in, 16)
            pool.wait_ge(pt_in, 16)
            with pool.Fori(0, NB * NPG) as g:
                page = pool.value_load(ptab[0:1, bass.ds(g, 1)], min_val=0, max_val=79)
                pool.dma_start(big[:, :].rearrange("p (c g k) -> p c g k", c=2, k=PAGE)[:, :, bass.ds(g, 1), :],
                               a["pack_cmp"][bass.ds(page, 1), :, :, :].rearrange("a p c k -> p c a k")).then_inc(ct_in, 16)
            pool.wait_ge(brev_sb, 1)
            pool.dma_start(bias_scr, brev[:, :].unsqueeze(1).broadcast_to([16, P, 384])).then_inc(bscr_out, 16)
            pool.wait_ge(bscr_out, 16)
            pool.dma_start(bias_p, bass.AP(tensor=bias_scr.tensor, offset=127, ap=[[383, P], [P * 384, 16], [1, TP]])
                           ).then_inc(bias_in, 16)
            pool.wait_ge(w_used, T_MRG)
            pool.dma_start(kcx[:, :, TP:TP + 32], a["peT"]).then_inc(pe_in, 16)
            pool.wait_ge(w_used, W_MRG)
            pool.memset(qz[:, :, :, :], 0.0).then_inc(qz_zero, 1)
            pool.dma_start(win_k, a["win_kT"].rearrange("b p k -> p b k")).then_inc(winpg_in, 16)
            pool.dma_start(win_v, a["win_vr"].rearrange("b p c -> p b c")).then_inc(winpg_in, 16)
            pool.wait_ge(qz_zero, 1)

            def stage_q(j, first):
                for m, tile in ((0, T_QA), (1, T_QB)):
                    done = (qza_sb, qzb_sb)[m]
                    if not first:
                        pool.wait_ge(qk_mm, j * 4 + (m - 1))
                    for r in range(2):
                        pool.tensor_copy(qz[r * HD:(r + 1) * HD, m:m + 1, r, :],
                                         feat[r * HD:(r + 1) * HD, bass.ds(j + tile, 1), 0:TP]).then_inc(done, 1)

            pool.wait_ge(proj_sb, T_MRG + 2)
            stage_q(0, True)
            pool.wait_ge(vct_sb, 1)
            pool.wait_ge(qza_sb, 2)
            pool.wait_ge(qzb_sb, 2)
            own(pool.memset(xT_r[:, :], 0.0))
            own(pool.memset(qa_r[:, :], 0.0))
            qm = xT_r[:, 0:2048]
            for r in range(2):
                rows = slice(r * HD, (r + 1) * HD)
                for j in range(NPAIR):
                    st = j * 66 + r
                    own(pool.tensor_scalar(qm[rows, st:st + 264 * 7 + 1:264], feat[rows, T_QB + j, TP:T], SCALE, None, ALU.mult))
                    st = j + 4 * r
                    own(pool.tensor_scalar(qa_r[rows, st:st + 72 * 7 + 1:72], feat[rows, T_QA + j, TP:T], SCALE, None, ALU.mult))
            own.settle()
            pool.engine_nop().then_inc(qbd_sb, 1)
            with pool.Fori(1, NPAIR) as j:
                stage_q(j, False)

            def fetch(kind, half, turn, idx_ap, count):
                if not (isinstance(turn, int) and turn == 0):
                    pool.wait_ge((u_used, v_used)[kind], turn * 8 + (4 * half - 4))
                    pool.sem_inc(idx_go, 1)
                staged = (idx_u, idx_v)[kind]
                pool.tensor_copy(staged[:, half, :], idx_ap).then_inc(idx_st, 1)
                pool.wait_ge(idx_st, count)
                pool.sem_inc(idx_go, 1)
                table, slots, landed = ((a["peer_u"], u_rows, u_in), (a["peer_v"], v_rows, v_in))[kind]
                for s in range(UNROLL):
                    slot = half * UNROLL + s
                    off = bass.IndirectOffsetOnAxis(ap=staged[:, half, s:s + 1], axis=0)
                    pool.indirect_dma_start(slots[:, slot, :], None, table, off).then_inc(landed[slot], 16)

            def fetch_turn(turn, at, src, before):
                zero = isinstance(turn, int) and turn == 0
                c = 1 if zero else turn * 4
                fetch(0, 0, turn, src(at), c)
                if not zero:
                    fetch(1, 1, turn + (-1), before, c + 1)
                fetch(0, 1, turn, src(at + UNROLL), 2 if zero else c + 2)
                fetch(1, 0, turn, src(at), 3 if zero else c + 3)

            before = None
            for tt in range(2):
                src = lambda at, tt=tt: eidx[:, tt, bass.ds(at, UNROLL)]

                def rows_of_head(h, peeled):
                    pool.wait_ge(e_sb, found(tt, h))
                    pool.sem_inc(idx_go, 1)
                    for i in range(HEAD_T):
                        at = h * TOPK + i * 8
                        fetch_turn(h * HEAD_T + (TURN0[tt] + i), at, src, before if peeled and i == 0 else src(at + (-UNROLL)))

                rows_of_head(0, True)
                with pool.Fori(1, NH) as h:
                    rows_of_head(h, False)
                before = src(P - UNROLL)
            pool.wait_ge(eis_in, 16 * NH)
            fetch_turn(TURN0[2], 0, lambda at: eidx_s[:, bass.ds(at, UNROLL)], before)
            before = eidx_s[:, UNROLL:2 * UNROLL]
            fetch(1, 1, TURNS - 1, before, 4 * TURNS)

        @block.scalar
        def _(act):
            act.wait_ge(brev_mm, 1)
            nc.scalar.copy(brev[:, :], ps[0:16, 0, 0:384]).then_inc(brev_sb, 1)
            act.sem_inc(proj_sb, 2)
            with act.Fori(0, T_MRG // 2) as i:
                for j in range(2):
                    act.wait_ge(w_used, i * 2 + (j + 1))
                    nc.scalar.copy(feat[:, bass.ds(i * 2 + j, 1), :], ps[:, j:j + 1, 0:T]).then_inc(proj_sb, 1)
            act.wait_ge(w_used, T_MRG)
            nc.scalar.copy(feat[:, T_GATE, :], ps[:, 0, 0:T]).then_inc(proj_sb, 1)
            act.wait_ge(proj_sb, T_MRG + 2)
            for c in range(2):
                nc.scalar.copy(kcx[:, c, 0:TP], feat[:, T_KC + c, 0:TP]).then_inc(kcx_sb, 1)
            nc.scalar.activation(feat[:, T_GATE, :], feat[:, T_GATE, :], ACT.Sigmoid).then_inc(gates_sb, 1)
            act.wait_ge(bscr_out, 16)
            for g in range(1, 12, 2):
                act.wait_ge(kvt_mm, g + 1)
                n = 4 if g % 4 < 3 else 2
                src = ps[:, 2 + g % 2, 0:n * P].rearrange("p (n c) -> p n c", c=P)
                dst = (kv_n[:, g // 4, (g % 4) * 4:(g % 4) * 4 + n, :] if g < 8
                       else smp_n[:, (g % 4) * 4:(g % 4) * 4 + n, :])
                nc.scalar.copy(dst, src if g < 8 else src[0:NB]).then_inc(kvt_a, 1)
            act.wait_ge(kvt_a, 6)
            act.wait_ge(kvt_v, 6)
            for tt in range(2):
                r = slice(tt * P, (tt + 1) * P)
                for nm, lo, hi in (("nsa_prompt", 0, 4), ("win_prompt", 4, 6), ("moba_prompt", 6, 14)):
                    act.dma_start(a[nm][r, :].rearrange("p (n c) -> p n c", c=P), kv_n[:, tt, lo:hi, :]).then_inc(out_kv, 16)
            act.dma_start(a["nsa_sample"].rearrange("p (n c) -> p n c", c=P), smp_n[:, 0:4, :]).then_inc(out_kv, 16)
            act.dma_start(a["moba_sample"].rearrange("p (n c) -> p n c", c=P), smp_n[:, 6:14, :]).then_inc(out_kv, 16)
            act.dma_start(a["win_sample"][:, 511, :].rearrange("p (n c) -> p n c", c=P), smp_n[:, 4:6, :]).then_inc(out_kv, 16)

            own = Chain(act, act_own)

            def exps(u, s):
                act.wait_ge(mx_sb, u + 1)
                w = NCMP_P if s == 0 else None
                for t in range(2):
                    for r in range(2):
                        i = t * 2 + r
                        if s == 0:
                            v = s_p[:, 0, i * NCMP_P:(i + 1) * NCMP_P]
                        else:
                            lo = 2 * TP + r * P if t == 0 else r * TP
                            v = s_p[:, s % 2, lo:lo + (P if t == 0 else TP)]
                        nc.scalar.activation(v, v, ACT.Exp, bias=small[:, 8 * (s % 2) + i:8 * (s % 2) + i + 1],
                                             accum_out=small[:, 8 * (s % 2) + 4 + i:8 * (s % 2) + 5 + i]).then_inc(exp_sb, 1)

            def turn(u, s):
                act.wait_ge(tp_mm, u + 1)
                n = 384 if s else 256
                rows = P if s else NCMP_P
                nc.scalar.copy(pT[0:rows, 0:n], ps[0:rows, 2, 0:n]).then_inc(pt_a, 1)

            def body(j, last):
                for s in range(4):
                    if not (last and s == 3):
                        exps(j * 4 + (s + 1), (s + 1) % 4)
                    turn(j * 4 + s, s)

            exps(0, 0)
            with act.Fori(0, NPAIR - 1) as j:
                body(j, False)
            body(NPAIR - 1, True)

            def merge_copy(i):
                n = W_MRG + i
                act.wait_ge(w_used, n + 1)
                nc.scalar.copy(feat[:, T_MRG + i, :], ps[:, MRG_BANK[i], 0:T]).then_inc(proj_sb, 1)

            done = 0
            for i, v in enumerate((pc, pm, psl, pw)):
                for _ in range(EXP_AFTER[i]):
                    merge_copy(done)
                    done += 1
                act.wait_ge(dmax_sb, i + 1)
                nc.scalar.activation(v, v, ACT.Exp, bias=small[0:ROWS, 32 + i:33 + i],
                                     accum_out=small[0:ROWS, 36 + i:37 + i]).then_inc(dexp_sb, 1)
            for i in range(done, 16):
                merge_copy(i)
            for i in range(4):
                act.wait_ge(proj_sb, T_MRG + 2 + 16)
                nc.scalar.activation(feat[:, T_MRG + 4 * i:T_MRG + 4 * i + 4, :], feat[:, T_MRG + 4 * i:T_MRG + 4 * i + 4, :], ACT.Sigmoid
                                     ).then_inc(mgate_sb, 1)
            for n in range(8):
                act.wait_ge(w_used, W_OUT + n + 1)
                if n >= 2:
                    act.wait_ge(mixt_mm, n - 1)
                nc.scalar.copy(mixT[:, n % 2, :], ps[:, n % 2, 0:T]).then_inc(mixt_sb, 1)

            def deviation(n):
                tt = n % 3
                r = P if tt < 2 else NB
                act.wait_ge(var_sb, n + 1)
                nc.scalar.sqrt(stats[0:r, 15:16], stats[0:r, 14:15]).then_inc(std_sb, 1)

            for n in range(3):
                deviation(n)

            def query(n):
                act.wait_ge(w_used, W_Q + n + 1)
                if n >= 2:
                    act.wait_ge(sc_mm, n - 1)
                nc.scalar.copy(qT2[:, n % 2, :], ps[:, n % 2, 0:T]).then_inc(q_sb, 1)

            def keep_scores(n):
                act.wait_ge(sc_mm, n + 1)
                nc.scalar.copy(scores.rearrange("p (t n k) -> p t n k", t=3, n=16)[:, 0:2, n, :],
                               ps[:, 2 + n % 2, 0:2 * P].rearrange("p (t k) -> p t k", t=2)).then_inc(sc_sb, 1)
                nc.scalar.copy(scores[0:NB, (32 + n) * P:(33 + n) * P], ps[0:NB, 2 + n % 2, 2 * P:3 * P]).then_inc(sc_sb, 1)

            def expert_exps(count, c):
                r = (P, NB)[c]
                act.wait_ge(fsub_sb, count)
                nc.scalar.activation(bexp[0:r, c, :], best[0:r, c, :], ACT.Exp, bias=nbest[0:r, c:c + 1],
                                     accum_out=gsum[0:r, c:c + 1]).then_inc(gexp_sb, 1)

            def weights(g, q, weight_of, sample=False):
                act.wait_ge(u_used, g * UNROLL + UNROLL)
                nc.scalar.activation(gel[:, q, :], dots[:, q, :], ACT.Gelu).then_inc(gel_sb, 1)
                if not (isinstance(g, int) and g < GROUPS):
                    act.wait_ge(v_used, g * UNROLL + (UNROLL - GROUPS * UNROLL))
                act.wait_ge(gel_sb, g + 1)
                for s in range(UNROLL):
                    own.loose(nc.scalar.activation(wts[:, q, s:s + 1], weight_of(s), ACT.Copy, scale=gel[:, q, s:s + 1]))
                own.settle()
                for s in range(UNROLL):
                    out, src = (diag[:, q, s, 0:NB], cst[:, C_KRED:C_KRED + NB]) if sample else (diag[:, q, s, :], ident)
                    nc.scalar.activation(out, src, ACT.Copy, scale=wts[:, q, s:s + 1]).then_inc(diag_sb, 1)

            def head_group(tt, h, q):
                last = isinstance(h, int) and h == NH - 1
                if q == 0 and not (last and tt == 1):
                    expert_exps(NH + 1 if last else found(tt, h + 1), 0)
                if q == 2 and (last and tt == 0 or tt == 1 and not last):
                    expert_exps(NH + 2 if last else h * 2 + (NH + 4), 1)
                if q == 0:
                    act.wait_ge(nm_sb, found(tt, h))
                weights(h * GROUPS + (2 * TURN0[tt] + q), q,
                        lambda s: gk[:, tt, bass.ds(h * TOPK + (q * UNROLL + s), 1)])

            def heads(tt, lo, hi):
                with act.Fori(lo, hi) as h:
                    own.enter(h, GROUPS * UNROLL, lo)
                    for q in range(GROUPS):
                        head_group(tt, h, q)
                own.leave(hi - lo)

            for n in range(AHEAD):
                query(n)
                if n:
                    keep_scores(n - 1)
            expert_exps(1, 0)
            head_group(0, 0, 0)
            for g in range(17 - AHEAD):
                head_group(0, *divmod(g + 1, GROUPS))
                if AHEAD + g < 16:
                    query(AHEAD + g)
                keep_scores(AHEAD + g - 1)
            heads(0, 3, 7)
            for q in range(GROUPS):
                head_group(0, 7, q)
            for q in range(GROUPS):
                head_group(1, 0, q)
            deviation(3)
            heads(1, 1, 7)
            for q in range(GROUPS):
                head_group(1, 7, q)
            act.wait_ge(gks_in, 16 * NH)
            for q in range(2):
                weights(2 * TURN0[2] + q, q, lambda s: gk_s[:, q * UNROLL + s:q * UNROLL + s + 1], sample=True)
            deviation(4)
            deviation(5)

        @block.tensor
        def _(pe):
            mm, tp = nc.tensor.matmul, nc.tensor.transpose
            pe.wait_ge(tab_in, 32)
            pe.wait_ge(oh_in, 32)
            mm(ps[0:16, 0, 0:384], tabx[:, :], oh_rev, start=True, stop=True).then_inc(brev_mm, 1)
            for i in range(30):
                last = mm(ps[:, 7, i * 8:(i + 1) * 8], oh_c[:, i, :], tabx[:, 0:8], start=True, stop=True)
            last.then_inc(biasc_mm, 1)

            pe.wait_ge(xT_in, 16)
            pe.wait_ge(brev_sb, 1)

            def proj_body(it, tiles):
                for j in range(tiles):
                    pe.wait_ge(w_in[j], it * 16 + 16)
                    pe.wait_ge(proj_sb, it * RING + (j + 1))
                    for k in range(KD):
                        last = mm(ps[:, j % 2, 0:T], ring[:, j, k * P:(k + 1) * P], xT[:, k, :], start=(k == 0), stop=(k == KD - 1))
                    last.then_inc(w_used, 1)

            full = T_MRG // RING
            with pe.Fori(0, full) as it:
                proj_body(it, RING)
            proj_body(full, T_MRG - full * RING)
            pe.wait_ge(proj_sb, T_MRG + 2)
            pe.wait_ge(cst_in, 16)
            for g in range(12):
                if g >= 2:
                    pe.wait_ge(kvt_v if g % 2 == 0 else kvt_a, g // 2)
                n = 4 if g % 4 < 3 else 2
                for i in range(n):
                    t = KV0 + (g % 4) * 4 + i
                    if g < 8:
                        last = tp(ps[:, 2 + g % 2, i * P:(i + 1) * P], feat[:, t, (g // 4) * P:(g // 4 + 1) * P], ident)
                    else:
                        last = tp(ps[0:NB, 2 + g % 2, i * P:(i + 1) * P], feat[:, t, TP:T], ident)
                last.then_inc(kvt_mm, 1)
            pe.wait_ge(gates_sb, 1)
            for tt in range(2):
                last = tp(ps[:, 0, tt * P:(tt + 1) * P], feat[:, T_GATE, tt * P:(tt + 1) * P], ident)
            last.then_inc(kvt_mm, 1)
            pe.wait_ge(ct_in, 16 * NB * NPG)
            pe.wait_ge(kcx_sb, 2)
            pe.wait_ge(pe_in, 16)
            pe.wait_ge(biasc_sb, 1)
            for c in range(2):
                kv = kcx[:, c, :].rearrange("p (n s) -> p n s", s=16)
                for q in range(4):
                    n = W_CONV + c * 4 + q
                    pe.wait_ge(w_in[W_SLOT[n]], 16 * W_LOADS[n])
                    for i in range(8):
                        w = ring[:, W_SLOT[n], i * P:(i + 1) * P]
                        m, s = divmod(q * 8 + i, 16)
                        f, l = (q == 0 and i == 0), (q == 3 and i == 7)
                        mm(ps[:, 4 + c, 0:NB * NCMP_D].rearrange("p (b n) -> p b n", b=NB), w, ct[:, c, :, m:m + NCMP_D, s], start=f, stop=l)
                        last = mm(ps[:, 6 + c, 0:17], w, kv[:, m:m + 17, s], start=f, stop=l)
                    last.then_inc(w_used, 1)
            pe.wait_ge(comp_sb, 4)
            pe.wait_ge(kvt_v, 6)
            pe.wait_ge(kvt_a, 6)
            tp(ps[0:NCMP_P, 1, 0:P], kc_p[:, 1, 0:NCMP_P], ident)
            for b in range(NB):
                last = tp(ps[0:NCMP_D, 2 + b // 4, (b % 4) * P:(b % 4 + 1) * P], vc_dT[:, b * NCMP_D:(b + 1) * NCMP_D], ident)
            last.then_inc(vct_mm, 1)
            for m in range(2):
                for c in range(2):
                    mm(ps[0:ROWS, 4 + 2 * m + c, :], tabd[:, m, :], oh_d[:, c * 512:(c + 1) * 512], start=True, stop=True)
            for m in range(2):
                last = mm(ps[0:ROWS, 0, 256 + m:257 + m], tabd[:, m, :], cst[0:32, C_ID:C_ID + 1], start=True, stop=True)
            last.then_inc(biasd_mm, 1)
            pe.wait_ge(vct_sb, 1)
            pe.wait_ge(biasd_sb, 1)

            def keys(s, j):
                if s == 0:
                    return kc_p[:, 0, 0:NCMP_P]
                return feat[:, {1: T_KS, 2: T_KW, 3: T_KB + j}[s], 0:TP]

            def scores(u, j, s):
                if s == 0:
                    pe.wait_ge(qza_sb, j * 2 + 2)
                if s == 3:
                    pe.wait_ge(qzb_sb, j * 2 + 2)
                if u:
                    pe.wait_ge(s_sb_, u)
                k = keys(s, j)
                bank = 0
                for r in range(2):
                    q = qz[:, 1 if s == 3 else 0, r, :]
                    if s == 0:
                        for t in range(2):
                            i = t * 2 + r
                            last = mm(ps[:, bank, i * NCMP_P:(i + 1) * NCMP_P], q[:, t * P:(t + 1) * P], k, start=True, stop=True)
                    else:
                        mm(ps[:, bank, r * TP:(r + 1) * TP], q[:, P:TP], k, start=True, stop=True)
                        last = mm(ps[:, bank + 1, r * P:(r + 1) * P], q[:, 0:P], k[:, 0:P], start=True, stop=True)
                last.then_inc(qk_mm, 1)

            def values(u, j, s):
                pe.wait_ge(exp_sb, u * 4 + 4)
                buf = s_p[:, s % 2, :]
                if s == 0:
                    for t in range(2):
                        for r in range(2):
                            i = t * 2 + r
                            last = tp(ps[0:NCMP_P, 2 + r, t * P:(t + 1) * P], buf[:, i * NCMP_P:(i + 1) * NCMP_P], ident)
                else:
                    for r in range(2):
                        for c in range(2):
                            tp(ps[:, 2 + r, c * P:(c + 1) * P], buf[:, r * TP + c * P:r * TP + (c + 1) * P], ident)
                        last = tp(ps[:, 2 + r, 2 * P:3 * P], buf[:, 2 * TP + r * P:2 * TP + (r + 1) * P], ident)
                last.then_inc(tp_mm, 1)
                pe.wait_ge(pt_a, u + 1)
                pe.wait_ge(pt_v, u + 1)
                if u:
                    pe.wait_ge(o_sb, u)
                out = ps[:, 4, :]
                for r in range(2):
                    hs = slice(r * HD, (r + 1) * HD)
                    if s == 0:
                        for t in range(2):
                            last = mm(out[:, (t * 2 + r) * HD:(t * 2 + r + 1) * HD], pT[0:NCMP_P, r * 256 + t * P:r * 256 + (t + 1) * P],
                                      vc_pn[:, hs], start=True, stop=True)
                        continue
                    v = lambda c: kv_n[:, c, {1: T_VS, 2: T_VW, 3: T_VB + j}[s] - KV0, hs]
                    o1 = out[:, (2 + r) * HD:(3 + r) * HD]
                    mm(o1, pT[:, r * 384:r * 384 + P], v(0), start=True, stop=False)
                    mm(o1, pT[:, r * 384 + P:r * 384 + 2 * P], v(1), start=False, stop=True)
                    last = mm(out[:, r * HD:(r + 1) * HD], pT[:, r * 384 + 2 * P:r * 384 + 3 * P], v(0), start=True, stop=True)
                last.then_inc(pv_mm, 1)

            def decode_scores(c):
                half, b = divmod(c, NB)
                if c == 0:
                    pe.wait_ge(qbd_sb, 1)
                if c == NB:
                    pe.wait_ge(kev_sb, 1)
                pe.wait_ge(kv_in[c % 2], 64 * (c // 2 + 1))
                f, l = b == 0, b == NB - 1
                chunk = pages[:, (c % 2) * 4:(c % 2) * 4 + 4, :]
                for j in range(NPAIR):
                    last = mm(ps[0:ROWS, (5, 7)[half], :], qbd_m[:, b, j, :], chunk[:, :, j * P:(j + 1) * P], start=f and j == 0, stop=l and j == NPAIR - 1)
                mm(ps[0:ROWS, (6, 5)[half], :], qbd_a[:, b, :], chunk[:, :, 512:640], start=f, stop=l).then_inc(kv_used[c % 2], 1)

            scores(0, 0, 0)
            for u in range(4 * NPAIR):
                if u + 1 < 4 * NPAIR:
                    scores(u + 1, (u + 1) // 4, (u + 1) % 4)
                if u:
                    decode_scores(u - 1)
                values(u, u // 4, u % 4)
            decode_scores(15)
            pe.wait_ge(o_sb, 4 * NPAIR)
            for g in range(4):
                tt, c0 = divmod(g * 4, 8)
                for i in range(4):
                    last = tp(ps[:, g, i * P:(i + 1) * P],
                              o_n[:, tt, 2 * (c0 + i):2 * (c0 + i) + 2, :].rearrange("p h d -> p (h d)"), ident)
            last.then_inc(oT_mm, 1)
            pe.wait_ge(oT_v, 1)

            pe.wait_ge(winpg_in, 32)
            for b in range(NB):
                mm(ps[0:ROWS, 6, :], qbd_a[:, b, :], win_k[:, b, :], start=(b == 0), stop=(b == NB - 1))
            pe.wait_ge(oT_v, 1)
            for b in range(NB):
                last = mm(ps[0:ROWS, 0, 0:NCMP_D], qbd_a[:, b, :], kc_dk[:, b * NCMP_D:(b + 1) * NCMP_D], start=(b == 0), stop=(b == NB - 1))
            pe.wait_ge(ez_sb, 1)
            for i in range(3):
                mm(ps[0:ROWS, 1, i:i + 1], ez[:, i, :], cst[:, C_ONE:C_ONE + 1], start=True, stop=True)
            mm(ps[0:ROWS, 1, 8:11], gz[:, :], cst[0:24, C_B24:C_B24 + 3], start=True, stop=True).then_inc(sd_mm, 1)

            def merge_gate(i):
                n = W_MRG + i
                pe.wait_ge(w_in[W_SLOT[n]], 16 * W_LOADS[n])
                if i == 0:
                    pe.wait_ge(xT_in, 32)
                if i >= 2:
                    pe.wait_ge(proj_sb, T_MRG + 2 + (i - 1))
                for k in range(KD):
                    last = mm(ps[:, MRG_BANK[i], 0:T], ring[:, W_SLOT[n], k * P:(k + 1) * P], xT2[:, k, :], start=(k == 0), stop=(k == KD - 1))
                last.then_inc(w_used, 1)

            for i in range(4):
                merge_gate(i)
            pe.wait_ge(imp_rd, 1)
            mm(ps[0:ROWS, 2, 0:NCMP_D], cst[0:ROWS, C_GSUM:C_GSUM + ROWS], pc, start=True, stop=True).then_inc(imp_mm, 1)
            for i in range(4, 8):
                merge_gate(i)
            pe.wait_ge(pd_sb, 1)
            for g in range(NPG):
                tp(ps[:, 0, g * ROWS:(g + 1) * ROWS], pm[:, g * P:(g + 1) * P], cst[0:ROWS, 0:ROWS])
                tp(ps[:, 2, g * ROWS:(g + 1) * ROWS], psl[:, g * P:(g + 1) * P], cst[0:ROWS, 0:ROWS])
            for g in range(4):
                tp(ps[:, 6, g * ROWS:(g + 1) * ROWS], pw[:, g * P:(g + 1) * P], cst[0:ROWS, 0:ROWS])
            tp(ps[0:NCMP_D, 6, 256:320], pc, cst[0:ROWS, 0:ROWS]).then_inc(pdt_mm, 1)
            mm(ps[0:NB, 1, 16:40], cst[0:ROWS, C_SELB:C_SELB + 8], small[0:ROWS, 64:88], start=True, stop=True).then_inc(pnew_mm, 1)
            pe.wait_ge(proj_sb, T_MRG + 2 + 8)
            pe.wait_ge(pdt_sb, 1)
            pe.wait_ge(pnz_sb, 1)

            def columns(b):
                pe.wait_ge(od_sb, b + 1)
                mm(ps[:, 3, b * 8:b * 8 + 4], sel_n[:, b % 2, :], cst[0:NB, C_JS:C_JS + 4], start=True, stop=True)
                for j in range(NPAIR):
                    last = mm(ps[:, 3, b * 8 + 4 + j:b * 8 + 5 + j], sel_m[:, b % 2, j * P:(j + 1) * P], cst[0:NB, C_ONE:C_ONE + 1],
                              start=True, stop=True)
                last.then_inc(oc_mm, 1)

            for b in range(NB):
                rb = slice(b * 8, (b + 1) * 8)
                om, on = ps[0:NB, 4 + 2 * (b % 2), :], ps[0:NB, 5 + 2 * (b % 2), 0:P]
                if b >= 2:
                    pe.wait_ge(od_sb, b - 1)
                for g in range(NPG):
                    if g % 4 == 0:
                        pe.wait_ge(kv_in[g // 4], 64 * (NB + b + 1))
                    mm(om, pTm[:, g, rb], pages[:, g, 0:512], start=(g == 0), stop=False)
                    x = mm(on, pTs[:, g, rb], pages[:, g, 512:640], start=(g == 0), stop=False)
                    if g % 4 == 3:
                        x.then_inc(kv_used[g // 4], 1)
                for g in range(4):
                    mm(on, pTw[:, g, rb], win_v[:, b, g, :], start=False, stop=False)
                mm(on, pTc[:, rb], vc_dn[:, b, :], start=False, stop=False)
                mm(on, pnz[:, b, 8:16], smp_n[:, T_VS - KV0, :], start=False, stop=False)
                mm(on, pnz[:, b, 16:24], smp_n[:, T_VW - KV0, :], start=False, stop=True)
                mm(om, pnz[:, b, 0:8], smp_n[:, T_VB - KV0:T_VB - KV0 + 4, :].rearrange("p n c -> p (n c)"),
                   start=False, stop=True).then_inc(od_mm, 1)
                if b:
                    columns(b - 1)
            columns(NB - 1)
            pe.wait_ge(oTd_sb, 1)
            for i in range(8, 16):
                merge_gate(i)

            pe.wait_ge(proj_sb, T_MRG + 2 + 16)
            for n in range(8):
                w = W_BRANCH + n
                pe.wait_ge(w_in[W_SLOT[w]], 16 * W_LOADS[w])
                if n >= 2:
                    pe.wait_ge(m_sb, n - 1)
                for m in range(2):
                    for k in range(4):
                        last = mm(ps[:, 4 + 2 * (n % 2) + m, 0:T], ring[:, W_SLOT[w], (m * 4 + k) * P:(m * 4 + k + 1) * P], oT[:, m * 4 + k, :],
                                  start=(k == 0), stop=(k == 3))
                last.then_inc(w_used, 1)
            pe.wait_ge(m_sb, 8)

            def mix_rows(n):
                pe.wait_ge(mixt_sb, n + 1)
                if n >= 2:
                    pe.wait_ge(mix_sb, n - 1)
                for tt in range(3):
                    r = P if tt < 2 else NB
                    last = tp(ps[0:r, 2 + n % 2, tt * P:(tt + 1) * P], mixT[:, n % 2, tt * P:tt * P + r], ident)
                last.then_inc(mixt_mm, 1)

            for n in range(8):
                w = W_OUT + n
                pe.wait_ge(w_in[W_SLOT[w]], 16 * W_LOADS[w])
                if n >= 2:
                    pe.wait_ge(mixt_sb, n - 1)
                for k in range(KD):
                    last = mm(ps[:, n % 2, 0:T], ring[:, W_SLOT[w], k * P:(k + 1) * P], mT[:, k, :], start=(k == 0), stop=(k == KD - 1))
                last.then_inc(w_used, 1)
                if n:
                    mix_rows(n - 1)
            mix_rows(7)
            pe.wait_ge(mix_sb, 8)
            for tt in range(3):
                r = P if tt < 2 else NB
                pe.wait_ge(h_sb, tt + 1)
                for half in range(2):
                    for i in range(4):
                        k = half * 4 + i
                        last = tp(ps[:, 2 + 2 * tt + half if tt < 2 else 6 + half, i * P:i * P + r], x_n[0:r, tt, k * P:(k + 1) * P], ident[0:r, 0:r])
                last.then_inc(hT_mm, 1)
            pe.wait_ge(hT_sb, 4)
            pe.wait_ge(keys_in, 16)

            def key_scores(n):
                pe.wait_ge(q_sb, n + 1)
                if n >= 2:
                    pe.wait_ge(sc_sb, 2 * (n - 1))
                for tt in range(3):
                    r = P if tt < 2 else NB
                    last = mm(ps[0:r, 2 + n % 2, tt * P:(tt + 1) * P], qT2[:, n % 2, tt * P:tt * P + r], keysT[:, n, :], start=True, stop=True)
                last.then_inc(sc_mm, 1)

            def query(n):
                w = W_Q + n
                pe.wait_ge(w_in[W_SLOT[w]], 16 * W_LOADS[w])
                if n >= 2:
                    pe.wait_ge(q_sb, n - 1)
                for k in range(KD):
                    last = mm(ps[:, n % 2, 0:T], ring[:, W_SLOT[w], k * P:(k + 1) * P], xT[:, k, :], start=(k == 0), stop=(k == KD - 1))
                last.then_inc(w_used, 1)

            def residual(tt):
                for c in range(2):
                    if tt < 2:
                        mm(ps[:, 4 + 2 * tt + c, :], alpha_id, x_n[:, tt, c * 512:(c + 1) * 512], start=True, stop=False)
                    else:
                        mm(ps[0:NB, c, :], alpha_id[0:NB, 0:NB], x_n[0:NB, 2, c * 512:(c + 1) * 512], start=True, stop=False)

            def add_rows(tt, h, q):
                for s in range(UNROLL):
                    slot = (q % 2) * UNROLL + s
                    pe.wait_ge(diag_sb, h * TOPK + (8 * TURN0[tt] + q * UNROLL + s + 1))
                    pe.wait_ge(v_in[slot], h * (16 * HEAD_T) + (16 * (TURN0[tt] + q // 2) + 16))
                    stop = isinstance(h, int) and s == UNROLL - 1 and (tt == 2 and q == 1 or h == 7 and q == GROUPS - 1)
                    for c in range(2):
                        if tt < 2:
                            last = mm(ps[:, 4 + 2 * tt + c, :], diag[:, q, s, :], v_rows[:, slot, c * 512:(c + 1) * 512], start=False, stop=stop)
                        else:
                            last = mm(ps[0:NB, c, :], diag[:, q, s, 0:NB], v_rows[:, slot, c * 512:(c + 1) * 512], start=False, stop=stop)
                    last.then_inc(v_used, 1)

            for n in range(AHEAD):
                query(n)
                if n:
                    key_scores(n - 1)
            residual(0)
            residual(1)
            for g in range(3 * GROUPS):
                add_rows(0, *divmod(g, GROUPS))
                if AHEAD + g < 16:
                    query(AHEAD + g)
                if AHEAD + g <= 16:
                    key_scores(AHEAD + g - 1)
            pe.wait_ge(q_sb, 16)
            residual(2)
            for tt, first in ((0, 3), (1, 0)):
                with pe.Fori(first, 7) as h:
                    for q in range(GROUPS):
                        add_rows(tt, h, q)
                for q in range(GROUPS):
                    add_rows(tt, 7, q)
            for q in range(2):
                add_rows(2, 0, q)

        @block.vector
        def _(dve):
            own = Chain(dve, dve_own)
            v = nc.vector
            TT, TS, STT = v.tensor_tensor, v.tensor_scalar, v.scalar_tensor_tensor
            dve.wait_ge(biasc_mm, 1)
            v.tensor_copy(bc_keep[:, :], ps[:, 7, 0:240]).then_inc(biasc_sb, 1)
            own.loose(v.memset(ez[:, :, :], 0.0))
            dve.wait_ge(bscr_out, 16)
            for g in range(0, 12, 2):
                dve.wait_ge(kvt_mm, g + 1)
                n = 4
                src = ps[:, 2 + g % 2, 0:n * P].rearrange("p (n c) -> p n c", c=P)
                dst = (kv_n[:, g // 4, (g % 4) * 4:(g % 4) * 4 + n, :] if g < 8 else smp_n[:, (g % 4) * 4:(g % 4) * 4 + n, :])
                v.tensor_copy(dst, src if g < 8 else src[0:NB]).then_inc(kvt_v, 1)
            dve.wait_ge(kvt_mm, 13)
            own(v.tensor_copy(gate_n[:, :, :], ps[:, 0, 0:2 * P].rearrange("p (t c) -> p t c", t=2)[:, :, 0:24]))
            dve.wait_ge(w_used, W_MRG)
            own.loose(v.tensor_copy(kc_p[:, 0, :], ps[:, 6, 0:17]))
            own(v.tensor_copy(kc_p[:, 1, :], ps[:, 7, 0:17]))
            for c in range(2):
                TS(kc_p[:, c, 0:NCMP_P], kc_p[:, c, 0:NCMP_P], kc_p[:, c, 16:17], None, ALU.add).then_inc(comp_sb, 1)
                TS((kc_dk[:, :], vc_dT)[c], ps[:, 4 + c, 0:NB * NCMP_D], kc_p[:, c, 16:17], None, ALU.add).then_inc(comp_sb, 1)
            dve.wait_ge(vct_mm, 1)
            own.loose(v.tensor_copy(vc_pn[:, :], ps[0:NCMP_P, 1, 0:P]))
            for i in range(2):
                own.loose(v.tensor_copy(vc_dn[:, 4 * i:4 * i + 4, :].rearrange("p b c -> p (b c)"), ps[0:NCMP_D, 2 + i, :]))
            own.settle()
            v.engine_nop().then_inc(vct_sb, 1)
            dve.wait_ge(biasd_mm, 1)
            for m in range(2):
                own.loose(v.tensor_copy(biasd[:, m, 0:1024], ps[0:ROWS, 4 + 2 * m:6 + 2 * m, :].rearrange("p a b -> p (a b)")))
                own.loose(v.tensor_copy(biasd[:, m, 1024:1025], ps[0:ROWS, 0, 256 + m:257 + m]))
            own.settle()
            v.engine_nop().then_inc(biasd_sb, 1)

            for r in range(2):
                rows = slice(r * HD, (r + 1) * HD)
                def put(i):
                    return ez[rows, i, :].rearrange("p (b h) -> p h b", h=8)
                q = lambda t: feat[rows, t:t + 4, TP:T]
                own.loose(STT(put(0)[:, r:8:2, :], q(T_QB), SCALE, feat[rows, T_KB:T_KB + 4, TP:T], ALU.mult, ALU.mult))
                for i, t in ((1, T_KS), (2, T_KW)):
                    own.loose(STT(put(i)[:, 4 * r:4 * r + 4, :], q(T_QA), SCALE,
                        feat[rows, t:t + 1, TP:T].broadcast_to([HD, 4, NB]), ALU.mult, ALU.mult))
            own.loose(TT(gz[:, :].rearrange("p (b h) -> p b h", h=8), feat[0:24, T_GATE, TP:T].unsqueeze(2).broadcast_to([24, NB, 8]),
                   cst[0:24, C_M24:C_M24 + 8].unsqueeze(1).broadcast_to([24, NB, 8]), ALU.mult))
            own.settle()
            v.engine_nop().then_inc(ez_sb, 1)

            dve.wait_ge(bias_in, 16)

            def add_bias(u, j, s):
                dve.wait_ge(qk_mm, u + 1)
                if u > 1:
                    dve.wait_ge(tp_mm, u - 1)
                bank, b = 0, s % 2
                buf, mx = s_p[:, b, :], small[:, 8 * b:8 * b + 4]
                if s == 0:
                    for t in range(2):
                        own.loose(STT(buf[:, t * 30:(t + 1) * 30].rearrange("p (r n) -> p r n", r=2),
                            ps[:, bank, t * 30:(t + 1) * 30].rearrange("p (r n) -> p r n", r=2), SCALE,
                            bc_keep[:, :].rearrange("p (t n h) -> p t h n", t=2, h=8)[:, t, bass.ds(j * 2, 2), :], ALU.mult, ALU.add))
                    own.settle()
                    v.tensor_reduce(mx, buf[:, 0:60].rearrange("p (i n) -> p i n", i=4), AXX, ALU.max, negate=True).then_inc(mx_sb, 1)
                    v.engine_nop().then_inc(s_sb_, 1)
                else:
                    h0 = j * 2 + (8 if s == 3 else 0)
                    bias = bias_p[:, bass.ds(h0, 2), :]
                    own.loose(STT(buf[:, 0:512].rearrange("p (r k) -> p r k", r=2), ps[:, bank, :].rearrange("p (r k) -> p r k", r=2), SCALE,
                        bias, ALU.mult, ALU.add))
                    own.loose(STT(buf[:, 512:768].rearrange("p (r k) -> p r k", r=2), ps[:, bank + 1, 0:256].rearrange("p (r k) -> p r k", r=2), SCALE,
                        bias_p[:, bass.ds(h0, 2), P:TP], ALU.mult, ALU.add))
                    own.settle()
                    own(v.tensor_reduce(mx[:, 2:4], buf[:, 0:512].rearrange("p (i n) -> p i n", i=2), AXX, ALU.max, negate=True))
                    v.tensor_reduce(mx[:, 0:2], buf[:, 512:768].rearrange("p (i n) -> p i n", i=2), AXX, ALU.max, negate=True).then_inc(mx_sb, 1)
                    v.engine_nop().then_inc(s_sb_, 1)

            def weigh(u, j, s):
                b = s % 2
                dve.wait_ge(exp_sb, u * 4 + 4)
                if u:
                    dve.wait_ge(o_sb, u)
                sums, wt = small[:, 8 * b + 4:8 * b + 8], small[:, 16:20]
                if s == 0:
                    own(v.reciprocal(wt, sums))
                    own(TT(wt.rearrange("p (t r) -> p t r", t=2), wt.rearrange("p (t r) -> p t r", t=2),
                           cst[:, C_MASKC:C_MASKC + 2].unsqueeze(2).broadcast_to([P, 2, 2]), ALU.mult))
                else:
                    own(v.reciprocal(wt, sums))
                if s < 3:
                    own(TT(wt.rearrange("p (t r) -> p t r", t=2), wt.rearrange("p (t r) -> p t r", t=2),
                           gate_n[:, :, bass.ds(j * 6 + s, 4)][:, :, 0:4:3], ALU.mult))
                dve.wait_ge(tp_mm, u + 1)
                n = 384 if s else 256
                rows = P if s else NCMP_P
                v.tensor_copy(pT[0:rows, n:2 * n], ps[0:rows, 3, 0:n]).then_inc(pt_v, 1)
                dve.wait_ge(pv_mm, u + 1)
                out = o_n[:, :, bass.ds(j * 2 + (8 if s == 3 else 0), 2), :]
                src = ps[:, 4, 0:256].rearrange("p (t r d) -> p t r d", t=2, r=2)
                wb = wt.rearrange("p (t r) -> p t r", t=2).unsqueeze(3).broadcast_to([P, 2, 2, HD])
                if s in (0, 3):
                    TT(out, src, wb, ALU.mult).then_inc(o_sb, 1)
                else:
                    own(TT(o_part[:, :].rearrange("p (t r d) -> p t r d", t=2, r=2), src, wb, ALU.mult))
                    TT(out, out, o_part[:, :].rearrange("p (t r d) -> p t r d", t=2, r=2), ALU.add).then_inc(o_sb, 1)

            def key_half(half):
                dve.wait_ge(kv_used[1], 4 * (half + 1))
                lo = slice(half * 512, (half + 1) * 512)
                mo, se = ps[0:ROWS, (5, 7)[half], :], ps[0:ROWS, (6, 5)[half], :]
                own.loose(v.tensor_reduce(small[0:ROWS, 48 + 2 * half:50 + 2 * half], mo.rearrange("p (n k) -> p n k", k=256), AXX, ALU.add))
                own.loose(TT(half0[:, 0, :] if half == 0 else pm[:, lo], mo, biasd[:, 1, lo], ALU.add))
                own.loose(TT(half0[:, 1, :] if half == 0 else psl[:, lo], se, biasd[:, 0, lo], ALU.add))
                if half == 1:
                    own.loose(v.tensor_copy(pm[:, 0:512], half0[:, 0, :]))
                    own.loose(v.tensor_copy(psl[:, 0:512], half0[:, 1, :]))
                own.settle()
                v.engine_nop().then_inc(kev_sb, 1)

            add_bias(0, 0, 0)
            for u in range(4 * NPAIR):
                if u + 1 < 4 * NPAIR:
                    add_bias(u + 1, (u + 1) // 4, (u + 1) % 4)
                weigh(u, u // 4, u % 4)
                if u == NB:
                    key_half(0)

            dve.wait_ge(oT_mm, 1)
            dve.wait_ge(qbd_sb, 1)
            for g in range(4):
                tt, c0 = divmod(g * 4, 8)
                own.loose(v.tensor_copy(oT[:, c0:c0 + 4, tt * P:(tt + 1) * P], ps[:, g, :].rearrange("p (k t) -> p k t", k=4)))
            own.settle()
            v.engine_nop().then_inc(oT_v, 1)

            key_half(1)
            R = ROWS
            sm = small[0:R, :]
            dve.wait_ge(sd_mm, 1)
            own.loose(v.tensor_copy(sm[:, 20:23], ps[0:R, 1, 0:3]))
            own(v.tensor_copy(sm[:, 28:31], ps[0:R, 1, 8:11]))

            def drop_one(score, n, mask, tmp):
                own(v.tensor_reduce(sm[:, 44:45], score, AXX, ALU.min))
                own(TS(tmp, score, sm[:, 44:45], None, ALU.is_equal))
                own(TT(tmp, tmp, cst[0:R, C_IDX + 1:C_IDX + 1 + n], ALU.mult))
                own(v.tensor_reduce(sm[:, 45:46], tmp, AXX, ALU.max))
                own(TS(mask, cst[0:R, C_IDX + 1:C_IDX + 1 + n], sm[:, 45:46], NEG, ALU.is_equal, ALU.mult))

            own(TT(pc, ps[0:R, 0, 0:NCMP_D], biasd[:, 0, 31:1024:16], ALU.add))
            v.tensor_reduce(sm[:, 32:33], pc, AXX, ALU.max, negate=True).then_inc(dmax_sb, 1)
            drop_one(sm[:, 48:52], 4, sm[:, 52:56], sm[:, 56:60])
            own.loose(TT(pm[:, 0:1024].rearrange("p (n k) -> p n k", k=256), pm[:, 0:1024].rearrange("p (n k) -> p n k", k=256),
                   sm[:, 52:56].unsqueeze(2).broadcast_to([R, 4, 256]), ALU.add))
            own.loose(TT(pm[:, 1024:1025], sm[:, 20:21], biasd[:, 1, 1024:1025], ALU.add))
            own.settle()
            dve.wait_ge(dmax_sb, 1)
            v.tensor_reduce(sm[:, 33:34], pm, AXX, ALU.max, negate=True).then_inc(dmax_sb, 1)
            dve.wait_ge(dexp_sb, 1)
            own(v.reciprocal(sm[:, 40:41], sm[:, 36:37]))
            own(TS(pc, pc, sm[:, 40:41], None, ALU.mult))
            v.engine_nop().then_inc(imp_rd, 1)
            dve.wait_ge(imp_mm, 1)
            own(v.tensor_copy(imp[:, :], ps[0:R, 2, 0:NCMP_D]))
            own(TT(seg[:, :], imp[:, 4:60], imp[:, 3:59], ALU.add))
            own(v.tensor_reduce(blk[:, 0:14], seg[:, :].rearrange("p (n k) -> p n k", k=4), AXX, ALU.add))
            own(v.memset(blk[:, 16:32], 0.0))
            drop_one(blk[:, 0:14], 14, blk[:, 17:31], blk[:, 32:46])
            own.loose(TT(psl[:, 0:1024].rearrange("p (n k) -> p n k", k=64), psl[:, 0:1024].rearrange("p (n k) -> p n k", k=64),
                   blk[:, 16:32].unsqueeze(2).broadcast_to([R, 16, 64]), ALU.add))
            own.loose(TT(psl[:, 1024:1025], sm[:, 21:22], biasd[:, 0, 1024:1025], ALU.add))
            own.settle()
            v.tensor_reduce(sm[:, 34:35], psl, AXX, ALU.max, negate=True).then_inc(dmax_sb, 1)
            own.loose(TT(pw[:, 0:512], ps[0:R, 6, :], biasd[:, 0, 512:1024], ALU.add))
            own.loose(TT(pw[:, 512:513], sm[:, 22:23], biasd[:, 0, 1024:1025], ALU.add))
            own.settle()
            v.tensor_reduce(sm[:, 35:36], pw, AXX, ALU.max, negate=True).then_inc(dmax_sb, 1)
            dve.wait_ge(dexp_sb, 4)
            own(v.reciprocal(sm[:, 41:44], sm[:, 37:40]))
            own(TT(sm[:, 42:44], sm[:, 42:44], sm[:, 29:31], ALU.mult))
            own.loose(TS(pc, pc, sm[:, 28:29], None, ALU.mult))
            own.loose(TS(pm, pm, sm[:, 41:42], None, ALU.mult))
            own.loose(TS(psl, psl, sm[:, 42:43], None, ALU.mult))
            own.loose(TS(pw, pw, sm[:, 43:44], None, ALU.mult))
            own.settle()
            for i, p_new in enumerate((pm[:, 1024:1025], psl[:, 1024:1025], pw[:, 512:513])):
                own.loose(TS(sm[:, 64 + 8 * i:72 + 8 * i], cst[0:R, C_HM:C_HM + 8], p_new, None, ALU.mult))
            own.settle()
            v.engine_nop().then_inc(pd_sb, 1)
            dve.wait_ge(pdt_mm, 1)
            own.loose(v.tensor_copy(pTm, ps[:, 0, :].rearrange("p (g r) -> p g r", r=ROWS)))
            own.loose(v.tensor_copy(pTs, ps[:, 2, :].rearrange("p (g r) -> p g r", r=ROWS)))
            own.loose(v.tensor_copy(pTw, ps[:, 6, 0:256].rearrange("p (g r) -> p g r", r=ROWS)))
            own.loose(v.tensor_copy(pTc, ps[0:NCMP_D, 6, 256:320]))
            own.settle()
            v.engine_nop().then_inc(pdt_sb, 1)
            dve.wait_ge(pnew_mm, 1)
            own(v.tensor_copy(sm[0:NB, 96:120], ps[0:NB, 1, 16:40]))
            TT(pnz[:, :, :], sm[0:NB, 96:120].unsqueeze(1).broadcast_to([NB, NB, 24]),
               cst[0:NB, C_DIAG:C_DIAG + 8].unsqueeze(2).broadcast_to([NB, NB, 24]), ALU.mult).then_inc(pnz_sb, 1)
            for b in range(NB):
                dve.wait_ge(od_mm, b + 1)
                if b >= 2:
                    dve.wait_ge(oc_mm, b - 1)
                own(TT(sel_n[:, b % 2, :], ps[0:NB, 5 + 2 * (b % 2), 0:P], cst[0:NB, C_MN:C_MN + P], ALU.mult))
                TT(sel_m[:, b % 2, :], ps[0:NB, 4 + 2 * (b % 2), :], cst[0:NB, C_MM:C_MM + 512], ALU.mult).then_inc(od_sb, 1)
            dve.wait_ge(oc_mm, NB)
            v.tensor_copy(oT[:, :, TP:T], ps[:, 3, 0:64].rearrange("p (b k) -> p k b", k=8)).then_inc(oTd_sb, 1)

            dve.wait_ge(mgate_sb, 4)
            for n in range(8):
                dve.wait_ge(w_used, W_BRANCH + n + 1)
                bank = 4 + 2 * (n % 2)
                own.loose(TT(mT[:, n, :], ps[:, bank, 0:T], feat[:, T_MRG + n, :], ALU.mult))
                own.loose(TT(mtmp[:, 0:T], ps[:, bank + 1, 0:T], feat[:, T_MRG + 8 + n, :], ALU.mult))
                own.settle()
                TT(mT[:, n, :], mT[:, n, :], mtmp[:, 0:T], ALU.add).then_inc(m_sb, 1)
                dve.wait_ge(m_sb, n + 1)
            dve.wait_ge(x_in, 32)
            for n in range(8):
                dve.wait_ge(mixt_mm, n + 1)
                cols = slice(n * P, (n + 1) * P)
                own(STT(x_n[:, 0:2, cols], x_n[:, 0:2, cols], ALPHA, ps[:, 2 + n % 2, 0:2 * P].rearrange("p (t c) -> p t c", t=2), ALU.mult, ALU.add))
                STT(x_n[0:NB, 2, cols], x_n[0:NB, 2, cols], ALPHA, ps[0:NB, 2 + n % 2, 2 * P:3 * P], ALU.mult, ALU.add).then_inc(mix_sb, 1)
            dve.wait_ge(mix_sb, 8)
            dve.wait_ge(ln_in, 64)

            norms = [0]

            def layer_norm(tt, g, done, src=None):
                r = P if tt < 2 else NB
                xr = x_n[0:r, tt, :]
                src = xr if src is None else src
                own.loose(v.bn_stats(stats[0:r, 0:6], src[:, 0:512]))
                own.loose(v.bn_stats(stats[0:r, 6:12], src[:, 512:1024]))
                own.settle()
                own(v.bn_aggr(stats[0:r, 12:14], stats[0:r, 0:12].rearrange("p (a b) -> p a b", a=2)))
                TS(stats[0:r, 14:15], stats[0:r, 13:14], EPS, None, ALU.add).then_inc(var_sb, 1)
                dve.wait_ge(std_sb, norms[0] + 1)
                norms[0] += 1
                own(v.reciprocal(stats[0:r, 14:15], stats[0:r, 15:16]))
                own(TS(xr, src, stats[0:r, 12:13], stats[0:r, 14:15], ALU.subtract, ALU.mult))
                own(TT(xr, xr, ln_rows[0:r, g, :], ALU.mult))
                TT(xr, xr, ln_rows[0:r, g + 1, :], ALU.add).then_inc(done, 1)

            for tt in range(3):
                layer_norm(tt, 0, h_sb)
            for tt in range(3):
                r = P if tt < 2 else NB
                dve.wait_ge(hT_mm, tt + 1)
                bk = 2 + 2 * tt if tt < 2 else 6
                for half in range(2):
                    own.loose(v.tensor_copy(xT[:, half * 4:half * 4 + 4, tt * P:tt * P + r],
                        ps[:, bk + half, :].rearrange("p (k t) -> p k t", k=4)[:, :, 0:r]))
                own.settle()
                v.engine_nop().then_inc(hT_sb, 1)
            own(TS(alpha_id, ident, ALPHA, None, ALU.mult))
            v.engine_nop().then_inc(hT_sb, 1)

            def find(tt, h, c):
                r = P if tt < 2 else NB
                halves = range(2)
                carry = lambda: dve.sem_inc(dve_go, 1)
                own(v.tensor_copy(rest[0:r, :, :].rearrange("p c k -> p (c k)"), scores[0:r, bass.ds(h * 256 + tt * 2048, 256)]))
                for k in (0, 8):
                    carry()
                    for i in halves:
                        own.loose(v.max(val[0:r, i, k:k + 8], rest[0:r, i, :]))
                    own.settle()
                    carry()
                    for i in halves:
                        own.loose(v.max_index(idu[0:r, i, k:k + 8], val[0:r, i, k:k + 8], rest[0:r, i, :]))
                    own.settle()
                    if k == 0:
                        carry()
                        for i in halves:
                            own.loose(v.match_replace(rest[0:r, i, :], val[0:r, i, 0:8], rest[0:r, i, :], -3.0e38))
                        own.settle()
                own.loose(v.tensor_copy(idf[0:r], idu[0:r]))
                own(TT(cand[0:r].rearrange("p (i j) -> p i j", i=16), val[0:r, 0, :].unsqueeze(2).broadcast_to([r, 16, 16]),
                       val[0:r, 1:2, :].broadcast_to([r, 16, 16]), ALU.add))
                gv = best[0:r, c, :]
                carry()
                own(v.max(gv[:, 0:8], cand[0:r]))
                own.loose(TS(nbest[0:r, c:c + 1], gv[:, 0:1], -1.0, None, ALU.mult))
                carry()
                own(v.max_index(fpos[0:r, 0:8], gv[:, 0:8], cand[0:r]))
                carry()
                own(v.match_replace(cand[0:r], gv[:, 0:8], cand[0:r], -3.0e38))
                carry()
                own(v.max(gv[:, 8:16], cand[0:r]))
                dve.sem_inc(fsub_sb, 1)
                carry()
                own(v.max_index(fpos[0:r, 8:16], gv[:, 8:16], cand[0:r]))
                io = cst[0:r, C_IDX:C_IDX + 16].unsqueeze(1).broadcast_to([r, 16, 16])
                oh = oneh[0:r].rearrange("p (k i) -> p k i", k=16)
                for half, dst in ((0, ea), (1, eb)):
                    if half == 0:
                        own(TS(fi[0:r], fpos[0:r], 4, None, ALU.logical_shift_right))
                    else:
                        own(TS(fi[0:r], fpos[0:r], 15, None, ALU.bitwise_and))
                    own(v.tensor_copy(fif[0:r], fi[0:r]))
                    own(TT(oh, fif[0:r].unsqueeze(2).broadcast_to([r, 16, 16]), io, ALU.is_equal))
                    own(TT(oh, oh, idf[0:r, half:half + 1, :].broadcast_to([r, 16, 16]), ALU.mult))
                    own(v.tensor_reduce(dst[0:r], oh, AXX, ALU.add))
                own(STT(ea[0:r], ea[0:r], 128.0, eb[0:r], ALU.mult, ALU.add))
                own(v.tensor_copy(eidx[0:r, tt, bass.ds(h * TOPK, TOPK)], ea[0:r]))
                dve.sem_inc(e_sb, 1)

            def normalise(tt, h, c, count):
                r = P if tt < 2 else NB
                dve.wait_ge(gexp_sb, count)
                own(v.reciprocal(gsum[0:r, c:c + 1], gsum[0:r, c:c + 1]))
                own(TS(gk[0:r, tt, bass.ds(h * TOPK, TOPK)], bexp[0:r, c, :], gsum[0:r, c:c + 1], None, ALU.mult))
                dve.sem_inc(nm_sb, 1)

            def dot(g, q, turn, hrow):
                if not (isinstance(g, int) and g < GROUPS):
                    dve.wait_ge(gel_sb, g + (1 - GROUPS))
                for s in range(UNROLL):
                    slot = (q % 2) * UNROLL + s
                    dve.wait_ge(u_in[slot], turn * 16 + 16)
                    v.tensor_tensor_reduce(out=u_rows[:, slot, :], in0=u_rows[:, slot, :], in1=hrow, scale=1.0, scalar=0.0,
                                           op0=ALU.mult, op1=ALU.add, accum_out=dots[:, q, s:s + 1]).then_inc(u_used, 1)

            def head(tt, h, coming):
                for q in range(GROUPS):
                    if q % 2 == 0 and q // 2 < len(coming):
                        find(*coming[q // 2][0:3])
                    dot(h * GROUPS + (2 * TURN0[tt] + q), q, h * HEAD_T + (TURN0[tt] + q // 2), x_n[:, tt, :])
                for job in coming:
                    normalise(*job)

            def coming(tt, h):
                one = [(tt, h + 1, 0, found(tt, h + 1))]
                return one + [(2, h + 1, 1, h * 2 + (NH + 4))] if tt else one

            def heads(tt, lo, hi, per):
                with dve.Fori(lo, hi) as h:
                    own.enter(h, per, lo)
                    if tt == 0:
                        dve.wait_ge(sc_sb, h * 4 + 8)
                    head(tt, h, coming(tt, h))
                own.leave(hi - lo)

            dve.wait_ge(sc_sb, 4)
            find(0, 0, 0)
            normalise(0, 0, 0, 1)
            dve.wait_ge(sc_sb, 8)
            at = own.base + own.off
            head(0, 0, coming(0, 0))
            per = own.base + own.off - at
            heads(0, 1, 7, per)
            head(0, 7, [(1, 0, 0, NH + 1), (2, 0, 1, NH + 2)])
            at = own.base + own.off
            head(1, 0, coming(1, 0))
            per = own.base + own.off - at

            def tile_out(tt):
                dve.wait_ge(v_used, 8 * (TURN0[tt] + P // 8 if tt < 2 else TURNS))
                src = ps[0:NB, 0:2, :] if tt == 2 else ps[:, 4 + 2 * tt:6 + 2 * tt, :]
                layer_norm(tt, 2, y_sb, src.rearrange("p a b -> p (a b)"))

            tile_out(0)
            heads(1, 1, 7, per)
            head(1, 7, [])
            dve.wait_ge(hrep_in, 16)
            for q in range(2):
                dot(2 * TURN0[2] + q, q, TURN0[2], h_rep)
            tile_out(1)
            tile_out(2)


OUT_SHAPES = {
    "y_prompt": (TP, D), "y_sample": (NB, D), "nsa_prompt": (TP, 512), "moba_prompt": (TP, 1024),
    "win_prompt": (TP, 256), "nsa_sample": (NB, 512), "moba_sample": (NB, 1024), "win_sample": (NB, 512, 256),
}
OUT_NAMES = list(OUT_SHAPES)


def bucket(np, n):
    n = np.asarray(n)
    nf = np.maximum(n, 1).astype(np.float32)
    large = 16 + (np.log(nf / np.float32(16)) / math.log(1024 / 16) * 16).astype(np.int32)
    return np.where(n < 16, n, np.minimum(large, 31))


def shape_constants(np):
    def one_hot(dist):
        flat = np.asarray(dist).reshape(-1)
        oh = np.zeros((33, flat.size), np.float32)
        rows = np.where(flat < 0, 32, bucket(np, np.maximum(flat, 0)))
        oh[rows, np.arange(flat.size)] = 1.0
        return oh

    t = np.arange(P)
    rev = one_hot(255 - np.arange(384))
    ends = 16 * np.arange(NCMP_P) + 31
    dist_c = np.stack([[(tt * P + t) - e for e in ends] for tt in range(2)])
    onehot = np.concatenate([rev, one_hot(dist_c), one_hot(PAST - np.arange(PAST))], axis=1)
    c = np.zeros((P, NCONST), np.float32)
    r = np.arange(ROWS)
    c[:, C_ID:C_ID + P] = np.eye(P)
    c[:, C_ONE:C_ONE + P] = 1
    c[:, C_MASKC:C_MASKC + 2] = (dist_c[:, 0] >= 0).T
    c[:ROWS, C_HM:C_HM + 8] = (r % 8)[:, None] == np.arange(8)
    c[:ROWS, C_GSUM:C_GSUM + ROWS] = (r // 4)[:, None] == (r // 4)
    c[:ROWS, C_SELB:C_SELB + 8] = (r // 8)[:, None] == np.arange(8)
    c[:, C_IDX:C_IDX + 16] = np.arange(16)
    c[:8, C_DIAG:C_DIAG + 8] = np.eye(8)
    c[:8, C_MM:C_MM + 512] = np.arange(8)[:, None] == np.arange(512) // 64
    c[:8, C_MN:C_MN + P] = (np.arange(8) // 4)[:, None] == np.arange(P) // 64
    c[:8, C_JS:C_JS + 4] = (np.arange(8) % 4)[:, None] == np.arange(4)
    q = np.arange(24)
    c[:24, C_M24:C_M24 + 8] = (q // 6 + 4 * (q // 3 % 2))[:, None] == np.arange(8)
    c[:24, C_B24:C_B24 + 3] = (q % 3)[:, None] == np.arange(3)
    c[:, C_KRED:C_KRED + 8] = (np.arange(P) // 16)[:, None] == np.arange(8)
    return onehot, c


def kernel(**inputs):
    import numpy as np
    import concourse.bacc as bacc
    from concourse.bass_utils import run_bass_kernel_spmd as run

    i = {k: np.asarray(v) for k, v in inputs.items()}
    pair = [h for j in range(4) for h in (j, j + 4)]
    w = i["w_in"][0]
    cols = lambda lo, n: w[:, lo:lo + n]
    wq_a = cols(0, 512).reshape(D, 8, 64)[:, pair].reshape(D, 512)
    gate = cols(1280, 24).reshape(D, 8, 3)[:, pair].reshape(D, 24)
    gate = np.concatenate([gate, np.zeros((D, P - 24), np.float32)], axis=1)
    w_feat = np.concatenate([wq_a, cols(1304, 512), cols(512, 512), cols(1024, 256), cols(1816, 1024), gate, cols(2840, 2048)], axis=1)

    def tiles(m):
        k, n = m.shape
        return m.reshape(k // P, P, n // P, P).transpose(2, 1, 0, 3).reshape(n // P, P, k)

    cw = i["nsa_cmp_w"][0]
    conv = np.zeros((2, 4, P, 8, P), np.float32)
    cw8 = cw.reshape(2, 4, 8, 64, 64)
    for g in range(2):
        conv[:, :, g * 64:(g + 1) * 64, :, g * 64:(g + 1) * 64] = cw8.transpose(0, 1, 3, 2, 4)
    wa = i["w_branch_a"][0].reshape(8, 64, D)[pair].reshape(512, D)
    branch = np.concatenate([wa, i["w_branch_b"][0]], axis=0)
    wall = np.concatenate([tiles(w_feat)[:T_MRG], conv.reshape(8, P, D), tiles(w_feat)[T_MRG:], tiles(branch), tiles(i["w_out"][0]), tiles(i["peer_wq"][0])], axis=0)

    x_all = np.concatenate([i["x_prompt"][0], i["x_sample"][:, 0]], axis=0)
    nsa = i["cache_nsa"][0]
    moba = i["cache_moba"][0]
    pool = nsa.shape[0]
    col = lambda m: m.reshape(pool, PAGE, P).transpose(0, 2, 1)
    pack_cmp = np.stack([col(nsa[:, :, 0]), col(nsa[:, :, 1])], axis=2)
    k_m = moba[:, :, 0].reshape(pool, PAGE, 4, P).transpose(0, 3, 2, 1).reshape(pool, P, 512)
    pack_k = np.concatenate([k_m, col(nsa[:, :, 2])], axis=2)
    pack_v = np.concatenate([moba[:, :, 1].reshape(pool, PAGE, 512), nsa[:, :, 3].reshape(pool, PAGE, P)], axis=2)
    win = i["state_nsa_win"][0]
    win_kT = win[:, :, 0].reshape(NB, 512, P).transpose(0, 2, 1)
    win_vr = win[:, :, 1].reshape(NB, 4, P, P).transpose(0, 2, 1, 3).reshape(NB, P, 512)
    pe = i["nsa_cmp_pe"][0].transpose(2, 0, 1)
    rb = i["rel_bias"]
    rb_p = rb[:, pair + list(range(8, 16))]
    tab_ext = np.concatenate([rb_p, np.full((1, 16), NEG, np.float32)], axis=0)
    tab_dec = np.stack([np.tile(rb[:, 0:8], (1, NB)), np.tile(rb[:, 8:16], (1, NB))], axis=1)
    onehot, consts = shape_constants(np)
    keysT = i["peer_keys"][0].reshape(16, P, P).transpose(2, 0, 1)
    arrays = {
        "tab_ext": tab_ext, "tab_dec": tab_dec, "onehot": onehot, "consts": consts,
        "xT": x_all.T.reshape(KD, P, T).transpose(1, 0, 2).reshape(P, KD * T),
        "x_prompt": i["x_prompt"][0], "x_sample": i["x_sample"][:, 0], "wall": wall,
        "win_state": win.reshape(NB, 512, 256), "page_table": i["page_table"].reshape(1, NB * NPG),
        "pack_cmp": pack_cmp, "pack_kv": np.stack([pack_k, pack_v]), "win_kT": win_kT, "win_vr": win_vr,
        "peT": np.concatenate([pe, pe], axis=0), "keysT": keysT,
        "ln1_g": i["ln1_g"], "ln1_b": i["ln1_b"], "ln2_g": i["ln2_g"], "ln2_b": i["ln2_b"],
        "peer_u": i["peer_u"][0], "peer_v": i["peer_v"][0],
    }
    nc = bacc.Bacc("TRN2", target_bir_lowering=False, num_devices=1)
    feeds, aps = {}, {}
    for name, v in arrays.items():
        v = np.ascontiguousarray(v)
        feeds[name] = v
        aps[name] = nc.dram_tensor(name, v.shape, mybir.dt.from_np(v.dtype), kind="ExternalInput").ap()
    for name, shape in OUT_SHAPES.items():
        aps[name] = nc.dram_tensor(name, shape, F32, kind="ExternalOutput").ap()
    hybrid_layer(nc, aps)
    r = run(nc, [feeds], core_ids=[0]).results[0]
    return (
        r["y_prompt"].reshape(1, TP, D), r["y_sample"].reshape(NB, 1, D),
        r["nsa_prompt"].reshape(1, 1, TP, 4, 2, 64), r["moba_prompt"].reshape(1, 1, TP, 2, 8, 64),
        r["win_prompt"].reshape(1, 1, TP, 2, 2, 64), r["nsa_sample"].reshape(1, NB, 1, 4, 2, 64),
        r["moba_sample"].reshape(1, NB, 1, 2, 8, 64), r["win_sample"].reshape(1, NB, 512, 2, 2, 64),
    )
```

```python
import math
from contextlib import ExitStack

import concourse.bass as bass
from concourse import mybir

F32 = mybir.dt.float32
U32 = mybir.dt.uint32
I32 = mybir.dt.int32
ALU = mybir.AluOpType
ACT = mybir.ActivationFunctionType
AXX = mybir.AxisListType.X

P = 128
D = 1024
KD = D // P
TP = 256
NB = 8
T = TP + NB
HD = 64
NPAIR = 4
PAST = 1024
PAGE = 128
NPG = PAST // PAGE
NCMP_P = TP // 16 - 1
NCMP_D = PAST // 16 - 1
NEG = -1e30
SCALE = HD ** -0.5
ALPHA = 2.0 ** 0.25
EPS = 1e-5
ROWS = NB * 8
TOPK = 16
NH = 8

T_QA, T_QB, T_KC, T_VC, T_KS, T_VS, T_KW, T_VW, T_KB, T_VB, T_GATE, T_MRG = 0, 4, 8, 9, 10, 11, 12, 13, 14, 18, 22, 23
NT_IN = T_MRG + 16
KV0 = T_KC
NKV = T_GATE - T_KC
W_CONV = T_MRG
W_MRG = W_CONV + 2
W_BRANCH = W_MRG + 16
W_OUT = W_BRANCH + 8
W_Q = W_OUT + 8
NW = W_Q + 16
RING = 8
PGRING = 3
PGW = 640
PE_COLS = 1 * P
UNROLL = 4
GROUPS = 4
HEAD_T = 2
TURN0 = (0, P // 8, P // 4)
TURNS = P // 4 + 1
AHEAD = 16 + 2 - 3 * GROUPS

C_ID = 0
C_ONE = C_ID + P
C_MASKC = C_ONE + P
C_HM = C_MASKC + 2
C_GSUM = C_HM + 8
C_SELB = C_GSUM + ROWS
C_IDX = C_SELB + 8
C_DIAG = C_IDX + 16
C_MM = C_DIAG + 8
C_MN = C_MM + 512
C_JS = C_MN + P
C_M24 = C_JS + 4
C_B24 = C_M24 + 8
C_KRED = C_B24 + 3
NCONST = C_KRED + 8


def ring_slots():
    slots, before, loads, last, count = [], [], [], {}, {}
    for n in range(NW):
        slot = n % RING if n < W_MRG else (n - W_MRG) % PGRING if n < W_BRANCH else (n - W_BRANCH + PGRING) % RING
        if n >= W_BRANCH and n - W_BRANCH < RING and slot >= PGRING:
            last[slot] = None
        slots.append(slot)
        before.append(last.get(slot))
        last[slot] = n
        count[slot] = count.get(slot, 0) + 1
        loads.append(count[slot])
    return slots, before, loads


W_SLOT, W_BEFORE, W_LOADS = ring_slots()


def found(tt, h):
    return h + 1 if tt == 0 else h * 2 + (NH + 1)


class Chain:

    def __init__(self, eng, sem):
        self.eng, self.sem, self.base, self.off = eng, sem, 0, 0

    def __call__(self, ins):
        self.off += 1
        ins.then_inc(self.sem, 1)
        self.eng.wait_ge(self.sem, self.base + self.off)

    def loose(self, ins):
        self.off += 1
        ins.then_inc(self.sem, 1)

    def settle(self):
        self.eng.wait_ge(self.sem, self.base + self.off)

    def enter(self, i, per, first=0):
        self.start, self.per = self.base + self.off, per
        self.base, self.off = i * per + (self.start - first * per), 0

    def leave(self, turns):
        assert self.off == self.per, (self.off, self.per)
        self.base, self.off = 0, self.start + turns * self.per


def hybrid_layer(nc, a):
    ctx = ExitStack()
    with ctx:
        def sb(name, shape, dt=F32):
            return ctx.enter_context(nc.sbuf_tensor(name, shape, dt))

        def sem(name):
            return ctx.enter_context(nc.semaphore(name))

        cst = sb("cst", [P, NCONST])
        x_n = sb("x_n", [P, 3, D])
        xT_r = sb("xT_r", [P, KD * T])
        feat_r = sb("feat_r", [P, NT_IN * T])
        kv_n = sb("kv_n", [P, 2, NKV, P])
        ring = sb("ring", [P, RING, D])
        big = sb("big", [P, 16384])
        pg_r = sb("pg_r", [P, NPG * PGW])
        ps = ctx.enter_context(nc.psum_tensor("ps", [P, 8, 512], F32))
        tabx = sb("tabx", [33, 16])
        tabd = sb("tabd", [32, 2, ROWS])
        kc_p = sb("kc_p", [P, 2, 17])
        vc_pn = sb("vc_pn", [NCMP_P, P])
        gate_n = sb("gate_n", [P, 2, 24])
        ptab = sb("ptab", [1, NB * NPG], I32)
        small = sb("small", [P, 128])

        ident = cst[:, C_ID:C_ID + P]
        feat = feat_r[:, :].rearrange("p (n t) -> p n t", t=T)
        xT = xT_r[:, :].rearrange("p (k t) -> p k t", t=T)
        ct = big[:, :].rearrange("p (a c g n i) -> p a c g n i", c=2, g=2, n=8, i=8)
        bias_p = pg_r[:, 0:4096].rearrange("p (h k) -> p h k", h=16)
        pages = ring[:, PGRING:RING, :].rearrange("p a b -> p (a b)").rearrange("p (g c) -> p g c", g=NPG)
        xT2 = pg_r[:, 0:KD * T].rearrange("p (k t) -> p k t", t=T)

        o_n = big[:, 0:2048].rearrange("p (t h d) -> p t h d", t=2, h=16)
        qz = big[:, 2048:3072].rearrange("p (m r t) -> p m r t", m=2, r=2)
        s_p = big[:, 3072:4608].rearrange("p (r c) -> p r c", r=2)
        pT = big[:, 4608:5376]
        biasd = big[0:ROWS, 5376:7426].rearrange("p (m k) -> p m k", m=2)
        win_k = big[:, 7426:11522].rearrange("p (b k) -> p b k", b=NB)
        win_v = big[:, 11522:15618].rearrange("p (b c d) -> p b c d", b=NB, c=4)
        VD = NPAIR * P - PE_COLS
        vprod = big[:, 7426:7426 + 4 * VD].rearrange("p (g c) -> p g c", g=4)
        vtwo = big[:, 8962:8962 + 2 * VD].rearrange("p (g c) -> p g c", g=2)
        vacc = big[:, 9730:9730 + 3 * VD].rearrange("p (r c) -> p r c", r=3)
        pm = big[0:ROWS, 0:1025]
        psl = big[0:ROWS, 1025:2050]
        half0 = pg_r[0:ROWS, 4096:5120].rearrange("p (n k) -> p n k", k=512)
        pw = big[0:ROWS, 2050:2563]
        pc = big[0:ROWS, 2563:2626]
        pTm = big[:, 2626:3138].rearrange("p (g r) -> p g r", r=ROWS)
        pTs = big[:, 3138:3650].rearrange("p (g r) -> p g r", r=ROWS)
        pTw = big[:, 3650:3906].rearrange("p (g r) -> p g r", r=ROWS)
        pTc = big[0:NCMP_D, 3906:3970]
        sel_m = big[0:NB, 3970:4994].rearrange("p (r c) -> p r c", r=2)
        sel_n = big[0:NB, 4994:5250].rearrange("p (r c) -> p r c", r=2)
        mT = big[:, 0:KD * T].rearrange("p (k t) -> p k t", t=T)
        mixT = big[:, 2640:2640 + 2 * T].rearrange("p (r t) -> p r t", r=2)
        oT = feat_r[:, 0:KD * T].rearrange("p (k t) -> p k t", t=T)
        kc_dk = sb("kc_dk", [P, NB * NCMP_D])
        bc_keep = sb("bc_keep", [P, 240])
        x_flat = x_n[:, :, :].rearrange("p t d -> p (t d)")
        brev = x_flat[0:16, 0:384]
        smp_n = x_flat[0:NB, 0:NKV * P].rearrange("p (n c) -> p n c", c=P)
        vc_dn = x_flat[0:NCMP_D, NKV * P:NKV * P + NB * P].rearrange("p (b c) -> p b c", b=NB)
        o_part = big[:, 15618:15874]
        imp, seg, blk = big[0:ROWS, 15874:15937], big[0:ROWS, 15937:15993], big[0:ROWS, 15993:16041]
        mtmp = big[:, 2112:2112 + T]
        stats = sb("stats", [P, 16])
        stats1 = sb("stats1", [P, 3, 12])
        mean_var = sb("mean_var", [P, 3, 2])
        dev1 = sb("dev1", [P, 2, 3])
        lnT = sb("lnT", [P, 2, KD])
        vc_dT = xT_r[:, 0:NB * NCMP_D]
        kcx = xT_r[:, 576:1152].rearrange("p (c g k) -> p c g k", c=2, g=2)
        other = x_flat[:, NKV * P:NKV * P + 2 * NB * NCMP_D].rearrange("p (c b n) -> p c b n", c=2, b=NB)
        other_p = x_flat[:, 2816:2850].rearrange("p (c n) -> p c n", c=2)
        qbd_m = xT_r[:, 0:2048].rearrange("p (b j r) -> p b j r", b=NB, j=NPAIR)
        qa_r = sb("qa_r", [P, NB * ROWS])
        qbd_a = qa_r[:, :].rearrange("p (b r) -> p b r", b=NB)
        ez = sb("ez", [P, 3, ROWS])
        gz = sb("gz", [24, ROWS])
        pnz = sb("pnz", [NB, NB, 24])

        scores = feat_r[:, 0:6144]
        keysT = feat_r[:, 6144:8192].rearrange("p (n k) -> p n k", n=16)
        h_rep = feat_r[:, 8192:9216]
        kv_flat = kv_n[:, :, :, :].rearrange("p t n c -> p (t n c)")
        diag = kv_flat[:, 0:2048].rearrange("p (g s k) -> p g s k", g=GROUPS, s=UNROLL)
        qT2 = kv_flat[:, 2048:2048 + 2 * T].rearrange("p (r t) -> p r t", r=2)
        rest = kv_flat[:, 2576:2832].rearrange("p (c k) -> p c k", c=2)
        cand = kv_flat[:, 2832:3088]
        oneh = kv_flat[:, 3088:3344]
        val = kv_flat[:, 3344:3376].rearrange("p (c k) -> p c k", c=2)
        idu = kv_flat[:, 3376:3408].bitcast(U32).rearrange("p (c k) -> p c k", c=2)
        idf = kv_flat[:, 3408:3440].rearrange("p (c k) -> p c k", c=2)
        fpos = kv_flat[:, 3440:3456].bitcast(U32)
        fi = kv_flat[:, 3456:3472].bitcast(U32)
        fif = kv_flat[:, 3472:3488]
        ea = kv_flat[:, 3488:3504]
        eb = kv_flat[:, 3504:3520]
        best = kv_flat[:, 3520:3552].rearrange("p (c k) -> p c k", c=2)
        bexp = kv_flat[:, 3552:3584].rearrange("p (c k) -> p c k", c=2)
        gsum = sb("gsum", [P, 2])
        nbest = sb("nbest", [P, 2])
        alpha_id = qa_r[:, 0:P]
        ln_rows = pg_r[:, 0:4096].rearrange("p (n d) -> p n d", n=4)
        gk = sb("gk", [P, 3, P])
        eidx = sb("eidx", [P, 3, P], U32)
        idx_u = sb("idx_u", [P, 2, UNROLL], U32)
        idx_v = sb("idx_v", [P, 2, UNROLL], U32)
        dots = sb("dots", [P, GROUPS, UNROLL])
        gel = sb("gel", [P, GROUPS, UNROLL])
        wts = sb("wts", [P, GROUPS, UNROLL])
        gk_s = sb("gk_s", [P, 8])
        eidx_s = sb("eidx_s", [P, 8], U32)
        u_rows = big[:, 0:8192].rearrange("p (s d) -> p s d", s=8)
        v_rows = big[:, 8192:16384].rearrange("p (s d) -> p s d", s=8)

        bias_scr = nc.dram_tensor("bias_scr", (16, P, 384), F32).ap()
        h_scr = nc.dram_tensor("h_scr", (NB, D), F32).ap()
        g_scr = nc.dram_tensor("g_scr", (NB, P), F32).ap()
        e_scr = nc.dram_tensor("e_scr", (NB, P), U32).ap()

        cst_in, tab_in, oh_in, pt_in, xT_in, x_in = (sem(n) for n in ("cst_in", "tab_in", "oh_in", "pt_in", "xT_in", "x_in"))
        pe_in = sem("pe_in")
        w_in = [sem(f"w_in{i}") for i in range(RING)]
        w_used = sem("w_used")
        brev_mm, brev_sb, bscr_out, bias_in = (
            sem(n) for n in ("brev_mm", "brev_sb", "bscr_out", "bias_in"))
        proj_sb, gates_sb = sem("proj_sb"), sem("gates_sb")
        kvt_mm, kvt_v, kvt_a = sem("kvt_mm"), sem("kvt_v"), sem("kvt_a")
        ct_in, kcx_sb, comp_sb, vct_mm, vct_sb = (
            sem(n) for n in ("ct_in", "kcx_sb", "comp_sb", "vct_mm", "vct_sb"))
        qza_sb, qzb_sb, qk_mm, s_sb_, mx_sb, exp_sb, tp_mm, pt_v, pt_a, pv_mm, o_sb = (
            sem(n) for n in ("qza_sb", "qzb_sb", "qk_mm", "s_sb", "mx_sb", "exp_sb", "tp_mm", "pt_v", "pt_a", "pv_mm", "o_sb"))
        qz_zero = sem("qz_zero")
        oT_mm, oT_v = sem("oT_mm"), sem("oT_v")
        winpg_in = sem("winpg_in")
        kv_in = [sem("kv_in0"), sem("kv_in1")]
        kv_used = [sem("kv_used0"), sem("kv_used1")]
        vp_in, vp_used, vd_used = ([sem(f"{nm}{q}") for q in range(4)] for nm in ("vp_in", "vp_used", "vd_used"))
        biasd_mm, biasd_sb, qbd_sb, ez_sb, sd_mm = (
            sem(n) for n in ("biasd_mm", "biasd_sb", "qbd_sb", "ez_sb", "sd_mm"))
        dmax_sb, dexp_sb, imp_rd, imp_mm, pd_sb, pdt_mm, pdt_sb, pnew_mm, pnz_sb = (
            sem(n) for n in ("dmax_sb", "dexp_sb", "imp_rd", "imp_mm", "pd_sb", "pdt_mm", "pdt_sb", "pnew_mm", "pnz_sb"))
        od_mm, od_sb, oc_mm, oTd_sb = (sem(n) for n in ("od_mm", "od_sb", "oc_mm", "oTd_sb"))
        m_sb, mix_sb, ln_in, h_sb, hT_mm, hT_sb = (
            sem(n) for n in ("m_sb", "mix_sb", "ln_in", "h_sb", "hT_mm", "hT_sb"))
        keys_in, q_sb, sc_mm, sc_sb = (sem(n) for n in ("keys_in", "q_sb", "sc_mm", "sc_sb"))
        fsub_sb, gexp_sb, e_sb, hs_out, gs_out, es_out, hrep_in, gks_in, eis_in = (
            sem(n) for n in ("fsub_sb", "gexp_sb", "e_sb", "hs_out", "gs_out", "es_out", "hrep_in", "gks_in", "eis_in"))
        idx_st, idx_go = sem("idx_st"), sem("idx_go")
        u_in = [sem(f"u_in{i}") for i in range(8)]
        v_in = [sem(f"v_in{i}") for i in range(8)]
        u_used, v_used, gel_sb = sem("u_used"), sem("v_used"), sem("gel_sb")
        diag_sb, nm_sb, y_sb, dve_go = sem("diag_sb"), sem("nm_sb"), sem("y_sb"), sem("dve_go")
        nrm_sb, csh_sb, sp_go, pool_go = sem("nrm_sb"), sem("csh_sb"), sem("sp_go"), sem("pool_go")
        var_sb, std_sb = sem("var_sb"), sem("std_sb")
        mgate_sb, mixt_mm, mixt_sb, kev_sb = (sem(n) for n in ("mgate_sb", "mixt_mm", "mixt_sb", "kev_sb"))
        MRG_BANK = [(3, 4)[i % 2] if i < 8 else i % 2 for i in range(16)]
        EXP_AFTER = (1, 2, 2, 2)
        out_w, out_kv, out_y = sem("out_w"), sem("out_kv"), sem("out_y")
        dve_own, pool_own, act_own = sem("dve_own"), sem("pool_own"), sem("act_own")

        oh_rev = feat_r[0:33, 0:384]
        oh_d = pg_r[0:32, 4096:4096 + PAST]
        block = ctx.enter_context(nc.Block())

        def kind_of(s):
            return ("cmp", "sel", "win", "moba")[s]

        def load_values(eng, places, go):
            for half in range(2):
                eng.wait_ge(kv_used[half], NB)
            with eng.Fori(0, NB) as b:
                for q in places:
                    page = [eng.value_load(ptab[0:1, bass.ds(b * NPG + (2 * q + g), 1)], min_val=0, max_val=79) for g in range(2)]
                    eng.wait_ge(vd_used[q], b + 1)
                    eng.sem_inc(go, 1)
                    eng.wait_ge(vp_used[q], b + 1)
                    eng.sem_inc(go, 1)
                    for g in range(2):
                        eng.dma_start(pages[:, 2 * q + g:2 * q + g + 1, :],
                                      a["pack_kv"][1, bass.ds(page[g], 1), :, :].rearrange("a p c -> p a c")).then_inc(vp_in[q], 16)

        @block.sync
        def _(sp):
            sp.dma_start(tabx[:, :], a["tab_ext"]).then_inc(tab_in, 16)
            sp.dma_start(tabd[:, :, :], a["tab_dec"]).then_inc(tab_in, 16)
            sp.dma_start(oh_rev, a["onehot"][:, 0:384]).then_inc(oh_in, 16)
            sp.dma_start(xT_r[:, :], a["xT"]).then_inc(xT_in, 16)
            sp.dma_start(oh_d, a["onehot"][0:32, 384:384 + PAST]).then_inc(oh_in, 16)
            sp.dma_start(cst[:, :], a["consts"]).then_inc(cst_in, 16)

            def weight(n):
                if W_BEFORE[n] is not None:
                    sp.wait_ge(w_used, W_BEFORE[n] + 1)
                sp.dma_start(ring[:, W_SLOT[n], :], a["wall"][n]).then_inc(w_in[W_SLOT[n]], 16)

            for n in range(RING):
                weight(n)
            sp.dma_start(a["win_sample"][:, 0:511, :], a["win_state"][:, 1:512, :]).then_inc(out_w, 16)
            turns = W_MRG // RING
            with sp.Fori(1, turns) as it:
                for j in range(RING):
                    sp.wait_ge(w_used, it * RING + (j + 1 - RING))
                    sp.dma_start(ring[:, j:j + 1, :], a["wall"][bass.ds(it * RING + j, 1), :, :].rearrange("a p c -> p a c")
                                 ).then_inc(w_in[j], 16)
            for n in range(turns * RING, W_MRG + PGRING):
                weight(n)
            sp.wait_ge(pt_in, 16)
            sp.wait_ge(w_used, W_MRG)

            def load_chunk(which, b, first_page, buf, uses):
                if uses is not None:
                    sp.wait_ge(kv_used[buf], uses)
                for g in range(4):
                    page = sp.value_load(ptab[0:1, bass.ds(b * NPG + (first_page + g), 1)], min_val=0, max_val=79)
                    sp.dma_start(pages[:, buf * 4 + g:buf * 4 + g + 1, :],
                                 a["pack_kv"][which, bass.ds(page, 1), :, :].rearrange("a p c -> p a c")).then_inc(kv_in[buf], 16)

            for half in range(2):
                if half == 0:
                    for b in range(2):
                        load_chunk(0, b, 0, b, None)
                with sp.Fori(1 - half, NB // 2) as i:
                    for r in range(2):
                        load_chunk(0, i * 2 + r, 4 * half, r, i + NB // 2 * half)
            sp.wait_ge(s_sb_, 4 * NPAIR)
            sp.dma_start(pg_r[:, 0:KD * T], a["xT"]).then_inc(xT_in, 16)
            for n in range(W_MRG + PGRING, W_MRG + 8):
                weight(n)
            load_values(sp, (0, 2), sp_go)
            for n in range(W_MRG + 8, W_BRANCH):
                weight(n)
            sp.wait_ge(od_mm, NB)
            for q in range(4):
                sp.wait_ge(vd_used[q], NB + 1)
            for n in range(W_BRANCH, W_OUT):
                weight(n)
            sp.wait_ge(out_kv, 16 * 9)
            sp.dma_start(x_n[:, 0:2, :], a["x_prompt"].rearrange("(t p) d -> p t d", p=P)).then_inc(x_in, 16)
            sp.dma_start(x_n[0:NB, 2, :], a["x_sample"]).then_inc(x_in, 16)
            for i, nm in enumerate(("ln1_g", "ln1_b", "ln2_g", "ln2_b")):
                sp.wait_ge(w_used, W_BRANCH)
                sp.dma_start(ln_rows[:, i, :], a[nm].broadcast_to([P, D])).then_inc(ln_in, 16)
            sp.dma_start(lnT[:, :, :], a["ln1_T"]).then_inc(ln_in, 16)
            for n in range(W_OUT, W_Q):
                weight(n)
            sp.wait_ge(m_sb, 8)
            sp.dma_start(keysT, a["keysT"]).then_inc(keys_in, 16)
            for n in range(W_Q, NW):
                weight(n)
            sp.wait_ge(h_sb, 3)
            sp.dma_start(h_scr, x_n[0:NB, 2, :]).then_inc(hs_out, 16)
            sp.wait_ge(hs_out, 16)
            sp.dma_start(h_rep, h_scr.unsqueeze(1).broadcast_to([NB, TOPK, D])).then_inc(hrep_in, 16)
            sp.wait_ge(y_sb, 1)
            sp.dma_start(a["y_prompt"][0:P, :], x_n[:, 0, :]).then_inc(out_y, 16)
            sp.wait_ge(nm_sb, 3 * NH)
            sp.dma_start(g_scr, gk[0:NB, 2, :]).then_inc(gs_out, 16)
            sp.dma_start(e_scr, eidx[0:NB, 2, :]).then_inc(es_out, 16)
            sp.wait_ge(gs_out, 16)
            sp.wait_ge(es_out, 16)
            with nc.allow_non_contiguous_dma(reason="a small re-layout"):
                for h in range(NH):
                    sp.dma_start(gk_s[:, h:h + 1], g_scr.rearrange("n (h k) -> n k h", h=NH)[:, :, h:h + 1]).then_inc(gks_in, 16)
                    sp.dma_start(eidx_s[:, h:h + 1], e_scr.rearrange("n (h k) -> n k h", h=NH)[:, :, h:h + 1]).then_inc(eis_in, 16)
            sp.wait_ge(y_sb, 2)
            sp.dma_start(a["y_prompt"][P:TP, :], x_n[:, 1, :]).then_inc(out_y, 16)
            sp.wait_ge(y_sb, 3)
            sp.dma_start(a["y_sample"], x_n[0:NB, 2, :]).then_inc(out_y, 16)
            sp.wait_ge(out_y, 48)
            sp.wait_ge(out_w, 16)
            sp.wait_ge(out_kv, 16 * 9)

        @block.gpsimd
        def _(pool):
            own = Chain(pool, pool_own)
            pool.dma_start(ptab[:, :], a["page_table"]).then_inc(pt_in, 16)
            pool.wait_ge(pt_in, 16)
            with pool.Fori(0, NB * NPG) as g:
                page = pool.value_load(ptab[0:1, bass.ds(g, 1)], min_val=0, max_val=79)
                pool.dma_start(big[:, :].rearrange("p (g k) -> p g k", k=2 * PAGE)[:, bass.ds(g, 1), :],
                               a["pack_cmp"][bass.ds(page, 1), :, :].rearrange("a p k -> p a k")).then_inc(ct_in, 16)
            pool.wait_ge(brev_sb, 1)
            pool.dma_start(bias_scr, brev[:, :].unsqueeze(1).broadcast_to([16, P, 384])).then_inc(bscr_out, 16)
            pool.wait_ge(bscr_out, 16)
            pool.dma_start(bias_p, bass.AP(tensor=bias_scr.tensor, offset=127, ap=[[383, P], [P * 384, 16], [1, TP]])
                           ).then_inc(bias_in, 16)
            pool.wait_ge(w_used, T_MRG)
            pool.dma_start(kcx[:, :, :, TP // 2:], a["peT"]).then_inc(pe_in, 16)
            pool.wait_ge(w_used, W_MRG)
            pool.memset(qz[:, :, :, :], 0.0).then_inc(qz_zero, 1)
            pool.dma_start(win_k, a["win_kT"].rearrange("b p k -> p b k")).then_inc(winpg_in, 16)
            pool.dma_start(win_v, a["win_vr"].rearrange("b p c -> p b c")).then_inc(winpg_in, 16)
            pool.wait_ge(qz_zero, 1)

            def stage_q(j, first):
                for m, tile in ((0, T_QA), (1, T_QB)):
                    done = (qza_sb, qzb_sb)[m]
                    if not first:
                        pool.wait_ge(qk_mm, j * 4 + (m - 1))
                    for r in range(2):
                        pool.tensor_copy(qz[r * HD:(r + 1) * HD, m:m + 1, r, :],
                                         feat[r * HD:(r + 1) * HD, bass.ds(j + tile, 1), 0:TP]).then_inc(done, 1)

            pool.wait_ge(proj_sb, T_MRG + 2)
            stage_q(0, True)
            pool.wait_ge(vct_sb, 1)
            pool.wait_ge(qza_sb, 2)
            pool.wait_ge(qzb_sb, 2)
            own(pool.memset(xT_r[:, :], 0.0))
            own(pool.memset(qa_r[:, :], 0.0))
            qm = xT_r[:, 0:2048]
            for r in range(2):
                rows = slice(r * HD, (r + 1) * HD)
                for j in range(NPAIR):
                    st = j * 66 + r
                    own(pool.tensor_scalar(qm[rows, st:st + 264 * 7 + 1:264], feat[rows, T_QB + j, TP:T], SCALE, None, ALU.mult))
                    st = j + 4 * r
                    own(pool.tensor_scalar(qa_r[rows, st:st + 72 * 7 + 1:72], feat[rows, T_QA + j, TP:T], SCALE, None, ALU.mult))
            own.settle()
            pool.engine_nop().then_inc(qbd_sb, 1)
            with pool.Fori(1, NPAIR) as j:
                stage_q(j, False)

            load_values(pool, (1, 3), pool_go)

            def fetch(kind, half, turn, idx_ap, count):
                if not (isinstance(turn, int) and turn == 0):
                    pool.wait_ge((u_used, v_used)[kind], turn * 8 + (4 * half - 4))
                    pool.sem_inc(idx_go, 1)
                staged = (idx_u, idx_v)[kind]
                pool.tensor_copy(staged[:, half, :], idx_ap).then_inc(idx_st, 1)
                pool.wait_ge(idx_st, count)
                pool.sem_inc(idx_go, 1)
                table, slots, landed = ((a["peer_u"], u_rows, u_in), (a["peer_v"], v_rows, v_in))[kind]
                for s in range(UNROLL):
                    slot = half * UNROLL + s
                    off = bass.IndirectOffsetOnAxis(ap=staged[:, half, s:s + 1], axis=0)
                    pool.indirect_dma_start(slots[:, slot, :], None, table, off).then_inc(landed[slot], 16)

            def fetch_turn(turn, at, src, before):
                zero = isinstance(turn, int) and turn == 0
                c = 1 if zero else turn * 4
                fetch(0, 0, turn, src(at), c)
                if not zero:
                    fetch(1, 1, turn + (-1), before, c + 1)
                fetch(0, 1, turn, src(at + UNROLL), 2 if zero else c + 2)
                fetch(1, 0, turn, src(at), 3 if zero else c + 3)

            before = None
            for tt in range(2):
                src = lambda at, tt=tt: eidx[:, tt, bass.ds(at, UNROLL)]

                def rows_of_head(h, peeled):
                    pool.wait_ge(e_sb, found(tt, h))
                    pool.sem_inc(idx_go, 1)
                    for i in range(HEAD_T):
                        at = h * TOPK + i * 8
                        fetch_turn(h * HEAD_T + (TURN0[tt] + i), at, src, before if peeled and i == 0 else src(at + (-UNROLL)))

                rows_of_head(0, True)
                with pool.Fori(1, NH) as h:
                    rows_of_head(h, False)
                before = src(P - UNROLL)
            pool.wait_ge(eis_in, 16 * NH)
            fetch_turn(TURN0[2], 0, lambda at: eidx_s[:, bass.ds(at, UNROLL)], before)
            before = eidx_s[:, UNROLL:2 * UNROLL]
            fetch(1, 1, TURNS - 1, before, 4 * TURNS)

        @block.scalar
        def _(act):
            act.wait_ge(brev_mm, 1)
            nc.scalar.copy(brev[:, :], ps[0:16, 0, 0:384]).then_inc(brev_sb, 1)
            act.sem_inc(proj_sb, 2)
            with act.Fori(0, T_MRG // 2) as i:
                for j in range(2):
                    act.wait_ge(w_used, i * 2 + (j + 1))
                    nc.scalar.copy(feat[:, bass.ds(i * 2 + j, 1), :], ps[:, j:j + 1, 0:T]).then_inc(proj_sb, 1)
            act.wait_ge(w_used, T_MRG)
            nc.scalar.copy(feat[:, T_GATE, :], ps[:, 0, 0:T]).then_inc(proj_sb, 1)
            act.wait_ge(proj_sb, T_MRG + 2)
            for c in range(2):
                for g in range(2):
                    for r in range(2):
                        nc.scalar.copy(kcx[r * HD:(r + 1) * HD, c, g, 0:TP // 2],
                                       feat[g * HD:(g + 1) * HD, T_KC + c, r:TP:2]).then_inc(kcx_sb, 1)
            nc.scalar.activation(feat[:, T_GATE, :], feat[:, T_GATE, :], ACT.Sigmoid).then_inc(gates_sb, 1)
            act.wait_ge(bscr_out, 16)
            for g in range(1, 12, 2):
                act.wait_ge(kvt_mm, g + 1)
                n = 4 if g % 4 < 3 else 2
                src = ps[:, 2 + g % 2, 0:n * P].rearrange("p (n c) -> p n c", c=P)
                dst = (kv_n[:, g // 4, (g % 4) * 4:(g % 4) * 4 + n, :] if g < 8
                       else smp_n[:, (g % 4) * 4:(g % 4) * 4 + n, :])
                nc.scalar.copy(dst, src if g < 8 else src[0:NB]).then_inc(kvt_a, 1)
            act.wait_ge(kvt_a, 6)
            act.wait_ge(kvt_v, 6)
            for tt in range(2):
                r = slice(tt * P, (tt + 1) * P)
                for nm, lo, hi in (("nsa_prompt", 0, 4), ("win_prompt", 4, 6), ("moba_prompt", 6, 14)):
                    act.dma_start(a[nm][r, :].rearrange("p (n c) -> p n c", c=P), kv_n[:, tt, lo:hi, :]).then_inc(out_kv, 16)
            act.dma_start(a["nsa_sample"].rearrange("p (n c) -> p n c", c=P), smp_n[:, 0:4, :]).then_inc(out_kv, 16)
            act.dma_start(a["moba_sample"].rearrange("p (n c) -> p n c", c=P), smp_n[:, 6:14, :]).then_inc(out_kv, 16)
            act.dma_start(a["win_sample"][:, 511, :].rearrange("p (n c) -> p n c", c=P), smp_n[:, 4:6, :]).then_inc(out_kv, 16)

            own = Chain(act, act_own)

            for c in range(2):
                act.wait_ge(w_used, W_CONV + c + 1)
                for g in range(2):
                    src, dst = slice((1 - g) * HD, (2 - g) * HD), slice(g * HD, (g + 1) * HD)
                    lo = 1 - g
                    nc.scalar.copy(other_p[dst, c, :], ps[src, 1 + c, 18 * g + lo:18 * g + lo + 17]).then_inc(csh_sb, 1)
                    nc.scalar.copy(other[dst, c, :, :], ps[src, 4 + 2 * c + g, :].rearrange("p (b n) -> p b n", b=NB)[:, :, lo:lo + NCMP_D]
                                   ).then_inc(csh_sb, 1)

            def exps(u, s):
                act.wait_ge(mx_sb, u + 1)
                w = NCMP_P if s == 0 else None
                for t in range(2):
                    for r in range(2):
                        i = t * 2 + r
                        if s == 0:
                            v = s_p[:, 0, i * NCMP_P:(i + 1) * NCMP_P]
                        else:
                            lo = 2 * TP + r * P if t == 0 else r * TP
                            v = s_p[:, s % 2, lo:lo + (P if t == 0 else TP)]
                        nc.scalar.activation(v, v, ACT.Exp, bias=small[:, 8 * (s % 2) + i:8 * (s % 2) + i + 1],
                                             accum_out=small[:, 8 * (s % 2) + 4 + i:8 * (s % 2) + 5 + i]).then_inc(exp_sb, 1)

            def turn(u, s):
                act.wait_ge(tp_mm, u + 1)
                n = 384 if s else 256
                rows = P if s else NCMP_P
                nc.scalar.copy(pT[0:rows, 0:n], ps[0:rows, 2, 0:n]).then_inc(pt_a, 1)

            def body(j, last):
                for s in range(4):
                    if not (last and s == 3):
                        exps(j * 4 + (s + 1), (s + 1) % 4)
                    turn(j * 4 + s, s)

            exps(0, 0)
            with act.Fori(0, NPAIR - 1) as j:
                body(j, False)
            body(NPAIR - 1, True)

            def merge_copy(i):
                n = W_MRG + i
                act.wait_ge(w_used, n + 1)
                if i < 8:
                    nc.scalar.copy(feat[:, T_MRG + i, :], ps[:, MRG_BANK[i], 0:T]).then_inc(proj_sb, 1)
                else:
                    nc.scalar.activation(feat[:, T_MRG + i, :], ps[:, MRG_BANK[i], 0:T], ACT.Sigmoid).then_inc(proj_sb, 1)

            done = 0
            for i, v in enumerate((pc, pm, psl, pw)):
                for _ in range(EXP_AFTER[i]):
                    merge_copy(done)
                    done += 1
                act.wait_ge(dmax_sb, i + 1)
                nc.scalar.activation(v, v, ACT.Exp, bias=small[0:ROWS, 32 + i:33 + i],
                                     accum_out=small[0:ROWS, 36 + i:37 + i]).then_inc(dexp_sb, 1)
            for i in range(done, 8):
                merge_copy(i)
            for i in range(2):
                act.wait_ge(proj_sb, T_MRG + 2 + 8)
                nc.scalar.activation(feat[:, T_MRG + 4 * i:T_MRG + 4 * i + 4, :], feat[:, T_MRG + 4 * i:T_MRG + 4 * i + 4, :], ACT.Sigmoid
                                     ).then_inc(mgate_sb, 1)
            for i in range(8, 16):
                merge_copy(i)
            for n in range(8):
                act.wait_ge(w_used, W_OUT + n + 1)
                if n >= 2:
                    act.wait_ge(mixt_mm, n - 1)
                nc.scalar.copy(mixT[:, n % 2, :], ps[:, n % 2, 0:T]).then_inc(mixt_sb, 1)

            def deviation(n):
                tt = n
                r = P if tt < 2 else NB
                act.wait_ge(var_sb, n + 2)
                nc.scalar.sqrt(stats[0:r, 15:16], stats[0:r, 14:15]).then_inc(std_sb, 1)

            act.wait_ge(var_sb, 1)
            nc.scalar.sqrt(dev1[:, 0, :], dev1[:, 1, :]).then_inc(std_sb, 1)
            act.wait_ge(ln_in, 80)
            for tt in (0, 2):
                act.wait_ge(hT_mm, tt + 1)
                r = P if tt < 2 else NB
                for k in range(KD):
                    nc.scalar.activation(xT[:, k, tt * P:tt * P + r], ps[:, (2, 4, 6)[tt] + k // 4, (k % 4) * P:(k % 4) * P + r], ACT.Identity,
                                         bias=lnT[:, 1, k:k + 1], scale=lnT[:, 0, k:k + 1]).then_inc(hT_sb, 1)

            def query(n):
                act.wait_ge(w_used, W_Q + n + 1)
                if n >= 2:
                    act.wait_ge(sc_mm, n - 1)
                nc.scalar.copy(qT2[:, n % 2, :], ps[:, n % 2, 0:T]).then_inc(q_sb, 1)

            def keep_scores(n):
                act.wait_ge(sc_mm, n + 1)
                nc.scalar.copy(scores.rearrange("p (t n k) -> p t n k", t=3, n=16)[:, 0:2, n, :],
                               ps[:, 2 + n % 2, 0:2 * P].rearrange("p (t k) -> p t k", t=2)).then_inc(sc_sb, 1)
                nc.scalar.copy(scores[0:NB, (32 + n) * P:(33 + n) * P], ps[0:NB, 2 + n % 2, 2 * P:3 * P]).then_inc(sc_sb, 1)

            def expert_exps(count, c):
                r = (P, NB)[c]
                act.wait_ge(fsub_sb, count)
                nc.scalar.activation(bexp[0:r, c, :], best[0:r, c, :], ACT.Exp, bias=nbest[0:r, c:c + 1],
                                     accum_out=gsum[0:r, c:c + 1]).then_inc(gexp_sb, 1)

            def weights(g, q, weight_of, sample=False):
                act.wait_ge(u_used, g * UNROLL + UNROLL)
                nc.scalar.activation(gel[:, q, :], dots[:, q, :], ACT.Gelu).then_inc(gel_sb, 1)
                if not (isinstance(g, int) and g < GROUPS):
                    act.wait_ge(v_used, g * UNROLL + (UNROLL - GROUPS * UNROLL))
                act.wait_ge(gel_sb, g + 1)
                for s in range(UNROLL):
                    own.loose(nc.scalar.activation(wts[:, q, s:s + 1], weight_of(s), ACT.Copy, scale=gel[:, q, s:s + 1]))
                own.settle()
                for s in range(UNROLL):
                    out, src = (diag[:, q, s, 0:NB], cst[:, C_KRED:C_KRED + NB]) if sample else (diag[:, q, s, :], ident)
                    nc.scalar.activation(out, src, ACT.Copy, scale=wts[:, q, s:s + 1]).then_inc(diag_sb, 1)

            def head_group(tt, h, q):
                last = isinstance(h, int) and h == NH - 1
                if q == (1 if tt == 0 and isinstance(h, int) and h == 0 else 0) and not (last and tt == 1):
                    expert_exps(NH + 1 if last else found(tt, h + 1), 0)
                if q == 2 and (last and tt == 0 or tt == 1 and not last):
                    expert_exps(NH + 2 if last else h * 2 + (NH + 4), 1)
                if q == 0:
                    act.wait_ge(nm_sb, found(tt, h))
                weights(h * GROUPS + (2 * TURN0[tt] + q), q,
                        lambda s: gk[:, tt, bass.ds(h * TOPK + (q * UNROLL + s), 1)])

            def heads(tt, lo, hi):
                with act.Fori(lo, hi) as h:
                    own.enter(h, GROUPS * UNROLL, lo)
                    for q in range(GROUPS):
                        head_group(tt, h, q)
                own.leave(hi - lo)

            query(0)
            query(1)
            keep_scores(0)
            keep_scores(1)
            for n in range(2, AHEAD):
                query(n)
                if n > 2:
                    keep_scores(n - 1)
            expert_exps(1, 0)
            head_group(0, 0, 0)
            for g in range(17 - AHEAD):
                head_group(0, *divmod(g + 1, GROUPS))
                if AHEAD + g < 16:
                    query(AHEAD + g)
                keep_scores(AHEAD + g - 1)
            heads(0, 3, 7)
            for q in range(GROUPS):
                head_group(0, 7, q)
            for q in range(GROUPS):
                head_group(1, 0, q)
            deviation(0)
            heads(1, 1, 7)
            for q in range(GROUPS):
                head_group(1, 7, q)
            act.wait_ge(gks_in, 16 * NH)
            for q in range(2):
                weights(2 * TURN0[2] + q, q, lambda s: gk_s[:, q * UNROLL + s:q * UNROLL + s + 1], sample=True)
            deviation(1)
            deviation(2)

        @block.tensor
        def _(pe):
            mm, tp = nc.tensor.matmul, nc.tensor.transpose
            pe.wait_ge(tab_in, 32)
            pe.wait_ge(oh_in, 32)
            mm(ps[0:16, 0, 0:384], tabx[:, :], oh_rev, start=True, stop=True).then_inc(brev_mm, 1)

            pe.wait_ge(xT_in, 16)
            pe.wait_ge(brev_sb, 1)

            def proj_body(it, tiles):
                for j in range(tiles):
                    pe.wait_ge(w_in[j], it * 16 + 16)
                    pe.wait_ge(proj_sb, it * RING + (j + 1))
                    for k in range(KD):
                        last = mm(ps[:, j % 2, 0:T], ring[:, j, k * P:(k + 1) * P], xT[:, k, :], start=(k == 0), stop=(k == KD - 1))
                    last.then_inc(w_used, 1)

            full = T_MRG // RING
            with pe.Fori(0, full) as it:
                proj_body(it, RING)
            proj_body(full, T_MRG - full * RING)
            pe.wait_ge(proj_sb, T_MRG + 2)
            pe.wait_ge(cst_in, 16)
            for g in range(12):
                if g >= 2:
                    pe.wait_ge(kvt_v if g % 2 == 0 else kvt_a, g // 2)
                n = 4 if g % 4 < 3 else 2
                for i in range(n):
                    t = KV0 + (g % 4) * 4 + i
                    if g < 8:
                        last = tp(ps[:, 2 + g % 2, i * P:(i + 1) * P], feat[:, t, (g // 4) * P:(g // 4 + 1) * P], ident)
                    else:
                        last = tp(ps[0:NB, 2 + g % 2, i * P:(i + 1) * P], feat[:, t, TP:T], ident)
                last.then_inc(kvt_mm, 1)
            pe.wait_ge(gates_sb, 1)
            for tt in range(2):
                last = tp(ps[:, 0, tt * P:(tt + 1) * P], feat[:, T_GATE, tt * P:(tt + 1) * P], ident)
            last.then_inc(kvt_mm, 1)
            pe.wait_ge(ct_in, 16 * NB * NPG)
            pe.wait_ge(kcx_sb, 8)
            pe.wait_ge(pe_in, 16)
            for c in range(2):
                n = W_CONV + c
                pe.wait_ge(w_in[W_SLOT[n]], 16 * W_LOADS[n])
                if c:
                    pe.wait_ge(kvt_v, 6)
                for i in range(8):
                    w = ring[:, W_SLOT[n], i * P:(i + 1) * P]
                    for g in range(2):
                        mm(ps[:, 4 + 2 * c + g, :].rearrange("p (a n) -> p a n", n=8), w, ct[:, :, c, g, :, i], start=(i == 0), stop=(i == 7))
                    last = mm(ps[:, 1 + c, 0:36].rearrange("p (g n) -> p g n", g=2), w,
                              kcx[:, c, :, :].rearrange("p g (n i) -> p g n i", i=8)[:, :, :, i], start=(i == 0), stop=(i == 7))
                last.then_inc(w_used, 1)
            pe.wait_ge(comp_sb, 6)
            pe.wait_ge(kvt_v, 6)
            pe.wait_ge(kvt_a, 6)
            tp(ps[0:NCMP_P, 1, 0:P], kc_p[:, 1, 0:NCMP_P], ident)
            for b in range(NB):
                last = tp(ps[0:NCMP_D, 2 + b // 4, (b % 4) * P:(b % 4 + 1) * P], vc_dT[:, b * NCMP_D:(b + 1) * NCMP_D], ident)
            last.then_inc(vct_mm, 1)

            def keys(s, j):
                if s == 0:
                    return kc_p[:, 0, 0:NCMP_P]
                return feat[:, {1: T_KS, 2: T_KW, 3: T_KB + j}[s], 0:TP]

            def scores(u, j, s):
                if s == 0:
                    pe.wait_ge(qza_sb, j * 2 + 2)
                if s == 3:
                    pe.wait_ge(qzb_sb, j * 2 + 2)
                if u:
                    pe.wait_ge(s_sb_, u)
                k = keys(s, j)
                bank = 0
                for r in range(2):
                    q = qz[:, 1 if s == 3 else 0, r, :]
                    if s == 0:
                        for t in range(2):
                            i = t * 2 + r
                            last = mm(ps[:, bank, i * NCMP_P:(i + 1) * NCMP_P], q[:, t * P:(t + 1) * P], k, start=True, stop=True)
                    else:
                        mm(ps[:, bank, r * TP:(r + 1) * TP], q[:, P:TP], k, start=True, stop=True)
                        last = mm(ps[:, bank + 1, r * P:(r + 1) * P], q[:, 0:P], k[:, 0:P], start=True, stop=True)
                last.then_inc(qk_mm, 1)

            def values(u, j, s):
                pe.wait_ge(exp_sb, u * 4 + 4)
                buf = s_p[:, s % 2, :]
                if s == 0:
                    for t in range(2):
                        for r in range(2):
                            i = t * 2 + r
                            last = tp(ps[0:NCMP_P, 2 + r, t * P:(t + 1) * P], buf[:, i * NCMP_P:(i + 1) * NCMP_P], ident)
                else:
                    for r in range(2):
                        for c in range(2):
                            tp(ps[:, 2 + r, c * P:(c + 1) * P], buf[:, r * TP + c * P:r * TP + (c + 1) * P], ident)
                        last = tp(ps[:, 2 + r, 2 * P:3 * P], buf[:, 2 * TP + r * P:2 * TP + (r + 1) * P], ident)
                last.then_inc(tp_mm, 1)
                pe.wait_ge(pt_a, u + 1)
                pe.wait_ge(pt_v, u + 1)
                if u:
                    pe.wait_ge(o_sb, u)
                out = ps[:, 4, :]
                for r in range(2):
                    hs = slice(r * HD, (r + 1) * HD)
                    if s == 0:
                        for t in range(2):
                            last = mm(out[:, (t * 2 + r) * HD:(t * 2 + r + 1) * HD], pT[0:NCMP_P, r * 256 + t * P:r * 256 + (t + 1) * P],
                                      vc_pn[:, hs], start=True, stop=True)
                        continue
                    v = lambda c: kv_n[:, c, {1: T_VS, 2: T_VW, 3: T_VB + j}[s] - KV0, hs]
                    o1 = out[:, (2 + r) * HD:(3 + r) * HD]
                    mm(o1, pT[:, r * 384:r * 384 + P], v(0), start=True, stop=False)
                    mm(o1, pT[:, r * 384 + P:r * 384 + 2 * P], v(1), start=False, stop=True)
                    last = mm(out[:, r * HD:(r + 1) * HD], pT[:, r * 384 + 2 * P:r * 384 + 3 * P], v(0), start=True, stop=True)
                last.then_inc(pv_mm, 1)

            def decode_scores(c):
                half, b = divmod(c, NB)
                if c == 0:
                    pe.wait_ge(qbd_sb, 1)
                if c == NB:
                    pe.wait_ge(kev_sb, 1)
                pe.wait_ge(kv_in[c % 2], 64 * (c // 2 + 1))
                f, l = b == 0, b == NB - 1
                chunk = pages[:, (c % 2) * 4:(c % 2) * 4 + 4, :]
                for j in range(NPAIR):
                    last = mm(ps[0:ROWS, (5, 7)[half], :], qbd_m[:, b, j, :], chunk[:, :, j * P:(j + 1) * P], start=f and j == 0, stop=l and j == NPAIR - 1)
                mm(ps[0:ROWS, (6, 5)[half], :], qbd_a[:, b, :], chunk[:, :, 512:640], start=f, stop=l).then_inc(kv_used[c % 2], 1)

            scores(0, 0, 0)
            for m in range(2):
                for c in range(2):
                    mm(ps[0:ROWS, 4 + 2 * m + c, :], tabd[:, m, :], oh_d[:, c * 512:(c + 1) * 512], start=True, stop=True)
            pe.wait_ge(vct_sb, 1)
            for m in range(2):
                last = mm(ps[0:ROWS, 3, 0 + m:1 + m], tabd[:, m, :], cst[0:32, C_ID:C_ID + 1], start=True, stop=True)
            last.then_inc(biasd_mm, 1)
            for u in range(4 * NPAIR):
                if u + 1 < 4 * NPAIR:
                    scores(u + 1, (u + 1) // 4, (u + 1) % 4)
                if u == 0:
                    pe.wait_ge(biasd_sb, 1)
                if u:
                    decode_scores(u - 1)
                values(u, u // 4, u % 4)
            decode_scores(15)
            pe.wait_ge(o_sb, 4 * NPAIR)
            for g in range(4):
                tt, c0 = divmod(g * 4, 8)
                for i in range(4):
                    last = tp(ps[:, g, i * P:(i + 1) * P],
                              o_n[:, tt, 2 * (c0 + i):2 * (c0 + i) + 2, :].rearrange("p h d -> p (h d)"), ident)
            last.then_inc(oT_mm, 1)
            pe.wait_ge(oT_v, 1)

            pe.wait_ge(winpg_in, 32)
            for b in range(NB):
                mm(ps[0:ROWS, 6, :], qbd_a[:, b, :], win_k[:, b, :], start=(b == 0), stop=(b == NB - 1))
            pe.wait_ge(oT_v, 1)
            for b in range(NB):
                last = mm(ps[0:ROWS, 0, 0:NCMP_D], qbd_a[:, b, :], kc_dk[:, b * NCMP_D:(b + 1) * NCMP_D], start=(b == 0), stop=(b == NB - 1))
            pe.wait_ge(ez_sb, 1)
            for i in range(3):
                mm(ps[0:ROWS, 1, i:i + 1], ez[:, i, :], cst[:, C_ONE:C_ONE + 1], start=True, stop=True)
            mm(ps[0:ROWS, 1, 8:11], gz[:, :], cst[0:24, C_B24:C_B24 + 3], start=True, stop=True).then_inc(sd_mm, 1)

            def merge_gate(i):
                n = W_MRG + i
                pe.wait_ge(w_in[W_SLOT[n]], 16 * W_LOADS[n])
                if i == 0:
                    pe.wait_ge(xT_in, 32)
                if i >= 2:
                    pe.wait_ge(proj_sb, T_MRG + 2 + (i - 1))
                for k in range(KD):
                    last = mm(ps[:, MRG_BANK[i], 0:T], ring[:, W_SLOT[n], k * P:(k + 1) * P], xT2[:, k, :], start=(k == 0), stop=(k == KD - 1))
                last.then_inc(w_used, 1)

            for i in range(4):
                merge_gate(i)
            pe.wait_ge(imp_rd, 1)
            mm(ps[0:ROWS, 2, 0:NCMP_D], cst[0:ROWS, C_GSUM:C_GSUM + ROWS], pc, start=True, stop=True).then_inc(imp_mm, 1)
            for i in range(4, 8):
                merge_gate(i)
            pe.wait_ge(pd_sb, 1)
            for g in range(NPG):
                tp(ps[:, 0, g * ROWS:(g + 1) * ROWS], pm[:, g * P:(g + 1) * P], cst[0:ROWS, 0:ROWS])
                tp(ps[:, 2, g * ROWS:(g + 1) * ROWS], psl[:, g * P:(g + 1) * P], cst[0:ROWS, 0:ROWS])
            for g in range(4):
                tp(ps[:, 6, g * ROWS:(g + 1) * ROWS], pw[:, g * P:(g + 1) * P], cst[0:ROWS, 0:ROWS])
            tp(ps[0:NCMP_D, 6, 256:320], pc, cst[0:ROWS, 0:ROWS]).then_inc(pdt_mm, 1)
            mm(ps[0:NB, 1, 16:40], cst[0:ROWS, C_SELB:C_SELB + 8], small[0:ROWS, 64:88], start=True, stop=True).then_inc(pnew_mm, 1)
            pe.wait_ge(proj_sb, T_MRG + 2 + 8)
            pe.wait_ge(pdt_sb, 1)
            pe.wait_ge(pnz_sb, 1)

            def columns(b):
                pe.wait_ge(od_sb, b + 1)
                mm(ps[:, 3, b * 8:b * 8 + 4], sel_n[:, b % 2, :], cst[0:NB, C_JS:C_JS + 4], start=True, stop=True)
                for j in range(NPAIR):
                    col, dve_part = ps[:, 3, b * 8 + 4 + j:b * 8 + 5 + j], j * P - PE_COLS
                    last = mm(col, sel_m[:, b % 2, j * P:(j + 1) * P], cst[0:NB, C_ONE:C_ONE + 1], start=True, stop=dve_part < 0)
                    if dve_part >= 0:
                        last = mm(col, vacc[:, b % 2, dve_part:dve_part + P], cst[:, C_ONE:C_ONE + 1], start=False, stop=True)
                last.then_inc(oc_mm, 1)

            for b in range(NB):
                rb = slice(b * 8, (b + 1) * 8)
                om, on = ps[0:NB, 4 + 2 * (b % 2), :], ps[0:NB, 5 + 2 * (b % 2), 0:P]
                if b >= 2:
                    pe.wait_ge(od_sb, b - 1)
                for g in range(NPG):
                    if g % 2 == 0:
                        pe.wait_ge(vp_in[g // 2], 32 * (b + 1))
                    mm(om[:, 0:PE_COLS], pTm[:, g, rb], pages[:, g, 0:PE_COLS], start=(g == 0), stop=False)
                    x = mm(on, pTs[:, g, rb], pages[:, g, 512:640], start=(g == 0), stop=False)
                    if g % 2 == 1:
                        x.then_inc(vp_used[g // 2], 1)
                for g in range(4):
                    mm(on, pTw[:, g, rb], win_v[:, b, g, :], start=False, stop=False)
                mm(on, pTc[:, rb], vc_dn[:, b, :], start=False, stop=False)
                mm(on, pnz[:, b, 8:16], smp_n[:, T_VS - KV0, :], start=False, stop=False)
                mm(on, pnz[:, b, 16:24], smp_n[:, T_VW - KV0, :], start=False, stop=True)
                new = smp_n[:, T_VB - KV0:T_VB - KV0 + 4, :].rearrange("p n c -> p (n c)")
                mm(om[:, 0:PE_COLS], pnz[:, b, 0:8], new[:, 0:PE_COLS], start=False, stop=True)
                mm(om[:, PE_COLS:], pnz[:, b, 0:8], new[:, PE_COLS:], start=True, stop=True).then_inc(od_mm, 1)
                if b:
                    columns(b - 1)
            columns(NB - 1)
            for i in range(8, 16):
                merge_gate(i)
            pe.wait_ge(oTd_sb, 1)

            pe.wait_ge(proj_sb, T_MRG + 2 + 16)
            for n in range(8):
                w = W_BRANCH + n
                pe.wait_ge(w_in[W_SLOT[w]], 16 * W_LOADS[w])
                if n >= 2:
                    pe.wait_ge(m_sb, n - 1)
                for m in range(2):
                    for k in range(4):
                        last = mm(ps[:, 4 + 2 * (n % 2) + m, 0:T], ring[:, W_SLOT[w], (m * 4 + k) * P:(m * 4 + k + 1) * P], oT[:, m * 4 + k, :],
                                  start=(k == 0), stop=(k == 3))
                last.then_inc(w_used, 1)
            pe.wait_ge(m_sb, 8)

            def mix_rows(n):
                pe.wait_ge(mixt_sb, n + 1)
                if n >= 2:
                    pe.wait_ge(mix_sb, n - 1)
                for tt in range(3):
                    r = P if tt < 2 else NB
                    last = tp(ps[0:r, 2 + n % 2, tt * P:(tt + 1) * P], mixT[:, n % 2, tt * P:tt * P + r], ident)
                last.then_inc(mixt_mm, 1)

            for n in range(8):
                w = W_OUT + n
                pe.wait_ge(w_in[W_SLOT[w]], 16 * W_LOADS[w])
                if n >= 2:
                    pe.wait_ge(mixt_sb, n - 1)
                for k in range(KD):
                    last = mm(ps[:, n % 2, 0:T], ring[:, W_SLOT[w], k * P:(k + 1) * P], mT[:, k, :], start=(k == 0), stop=(k == KD - 1))
                last.then_inc(w_used, 1)
                if n:
                    mix_rows(n - 1)
            mix_rows(7)
            pe.wait_ge(mix_sb, 8)
            for tt in range(3):
                r = P if tt < 2 else NB
                pe.wait_ge(nrm_sb, tt + 1)
                for half in range(2):
                    for i in range(4):
                        k = half * 4 + i
                        last = tp(ps[:, 2 + 2 * tt + half if tt < 2 else 6 + half, i * P:i * P + r], x_n[0:r, tt, k * P:(k + 1) * P], ident[0:r, 0:r])
                last.then_inc(hT_mm, 1)
            pe.wait_ge(hT_sb, 3 * KD)
            pe.wait_ge(keys_in, 16)

            def key_scores(n):
                pe.wait_ge(q_sb, n + 1)
                if n >= 2:
                    pe.wait_ge(sc_sb, 2 * (n - 1))
                for tt in range(3):
                    r = P if tt < 2 else NB
                    last = mm(ps[0:r, 2 + n % 2, tt * P:(tt + 1) * P], qT2[:, n % 2, tt * P:tt * P + r], keysT[:, n, :], start=True, stop=True)
                last.then_inc(sc_mm, 1)

            def query(n):
                w = W_Q + n
                pe.wait_ge(w_in[W_SLOT[w]], 16 * W_LOADS[w])
                if n >= 2:
                    pe.wait_ge(q_sb, n - 1)
                for k in range(KD):
                    last = mm(ps[:, n % 2, 0:T], ring[:, W_SLOT[w], k * P:(k + 1) * P], xT[:, k, :], start=(k == 0), stop=(k == KD - 1))
                last.then_inc(w_used, 1)

            def residual(tt):
                for c in range(2):
                    if tt < 2:
                        mm(ps[:, 4 + 2 * tt + c, :], alpha_id, x_n[:, tt, c * 512:(c + 1) * 512], start=True, stop=False)
                    else:
                        mm(ps[0:NB, c, :], alpha_id[0:NB, 0:NB], x_n[0:NB, 2, c * 512:(c + 1) * 512], start=True, stop=False)

            def add_rows(tt, h, q):
                for s in range(UNROLL):
                    slot = (q % 2) * UNROLL + s
                    pe.wait_ge(diag_sb, h * TOPK + (8 * TURN0[tt] + q * UNROLL + s + 1))
                    pe.wait_ge(v_in[slot], h * (16 * HEAD_T) + (16 * (TURN0[tt] + q // 2) + 16))
                    stop = isinstance(h, int) and s == UNROLL - 1 and (tt == 2 and q == 1 or h == 7 and q == GROUPS - 1)
                    for c in range(2):
                        if tt < 2:
                            last = mm(ps[:, 4 + 2 * tt + c, :], diag[:, q, s, :], v_rows[:, slot, c * 512:(c + 1) * 512], start=False, stop=stop)
                        else:
                            last = mm(ps[0:NB, c, :], diag[:, q, s, 0:NB], v_rows[:, slot, c * 512:(c + 1) * 512], start=False, stop=stop)
                    last.then_inc(v_used, 1)

            query(0)
            query(1)
            key_scores(0)
            key_scores(1)
            for n in range(2, AHEAD):
                query(n)
                if n > 2:
                    key_scores(n - 1)
            pe.wait_ge(h_sb, 4)
            residual(0)
            residual(1)
            for g in range(3 * GROUPS):
                add_rows(0, *divmod(g, GROUPS))
                if AHEAD + g < 16:
                    query(AHEAD + g)
                if AHEAD + g <= 16:
                    key_scores(AHEAD + g - 1)
            pe.wait_ge(q_sb, 16)
            residual(2)
            for tt, first in ((0, 3), (1, 0)):
                with pe.Fori(first, 7) as h:
                    for q in range(GROUPS):
                        add_rows(tt, h, q)
                for q in range(GROUPS):
                    add_rows(tt, 7, q)
            for q in range(2):
                add_rows(2, 0, q)

        @block.vector
        def _(dve):
            own = Chain(dve, dve_own)
            v = nc.vector
            TT, TS, STT = v.tensor_tensor, v.tensor_scalar, v.scalar_tensor_tensor
            for q in range(4):
                dve.sem_inc(vd_used[q], 1)
                dve.sem_inc(vp_used[q], 1)
            own.loose(v.memset(ez[:, :, :], 0.0))
            dve.wait_ge(bscr_out, 16)
            for g in range(0, 12, 2):
                dve.wait_ge(kvt_mm, g + 1)
                n = 4
                src = ps[:, 2 + g % 2, 0:n * P].rearrange("p (n c) -> p n c", c=P)
                dst = (kv_n[:, g // 4, (g % 4) * 4:(g % 4) * 4 + n, :] if g < 8 else smp_n[:, (g % 4) * 4:(g % 4) * 4 + n, :])
                v.tensor_copy(dst, src if g < 8 else src[0:NB]).then_inc(kvt_v, 1)
            dve.wait_ge(kvt_mm, 13)
            own(v.tensor_copy(gate_n[:, :, :], ps[:, 0, 0:2 * P].rearrange("p (t c) -> p t c", t=2)[:, :, 0:24]))
            dve.wait_ge(bias_in, 16)
            own(v.memset(bc_keep[:, 0:NCMP_P * 8], NEG))
            blocks = bc_keep[:, :].rearrange("p (t n h) -> p t h n", t=2, h=8)
            own.loose(v.tensor_copy(blocks[:, 0, :, 0:7], bias_p[:, 0:8, P + 31:TP:16]))
            own(v.tensor_copy(blocks[:, 1, :, :], bias_p[:, 0:8, 31:TP:16]))
            for r in range(2):
                rows = slice(r * HD, (r + 1) * HD)
                def put(i):
                    return ez[rows, i, :].rearrange("p (b h) -> p h b", h=8)
                q = lambda t: feat[rows, t:t + 4, TP:T]
                own.loose(STT(put(0)[:, r:8:2, :], q(T_QB), SCALE, feat[rows, T_KB:T_KB + 4, TP:T], ALU.mult, ALU.mult))
                for i, t in ((1, T_KS), (2, T_KW)):
                    own.loose(STT(put(i)[:, 4 * r:4 * r + 4, :], q(T_QA), SCALE,
                        feat[rows, t:t + 1, TP:T].broadcast_to([HD, 4, NB]), ALU.mult, ALU.mult))
            own.loose(TT(gz[:, :].rearrange("p (b h) -> p b h", h=8), feat[0:24, T_GATE, TP:T].unsqueeze(2).broadcast_to([24, NB, 8]),
                   cst[0:24, C_M24:C_M24 + 8].unsqueeze(1).broadcast_to([24, NB, 8]), ALU.mult))
            own.settle()
            v.engine_nop().then_inc(ez_sb, 1)

            for c in range(2):
                dve.wait_ge(csh_sb, 4 * (c + 1))
                half = [slice(g * HD, (g + 1) * HD) for g in range(2)]
                for g in range(2):
                    own.loose(TT(kc_p[half[g], c, :], ps[half[g], 1 + c, 19 * g:19 * g + 17], other_p[half[g], c, :], ALU.add))
                own.settle()
                for g in range(2):
                    dst = (kc_dk[:, :], vc_dT)[c].rearrange("p (b n) -> p b n", b=NB)
                    STT(dst[half[g]], ps[half[g], 4 + 2 * c + g, :].rearrange("p (b n) -> p b n", b=NB)[:, :, g:g + NCMP_D],
                        kc_p[half[g], c, 16:17], other[half[g], c, :, :], ALU.add, ALU.add).then_inc(comp_sb, 1)
                own(TS(kc_p[:, c, 0:NCMP_P], kc_p[:, c, 0:NCMP_P], kc_p[:, c, 16:17], None, ALU.add))
                v.engine_nop().then_inc(comp_sb, 1)
            dve.wait_ge(vct_mm, 1)
            own.loose(v.tensor_copy(vc_pn[:, :], ps[0:NCMP_P, 1, 0:P]))
            for i in range(2):
                own.loose(v.tensor_copy(vc_dn[:, 4 * i:4 * i + 4, :].rearrange("p b c -> p (b c)"), ps[0:NCMP_D, 2 + i, :]))
            own.settle()
            v.engine_nop().then_inc(vct_sb, 1)
            dve.wait_ge(bias_in, 16)

            def add_bias(u, j, s):
                dve.wait_ge(qk_mm, u + 1)
                if u > 1:
                    dve.wait_ge(tp_mm, u - 1)
                bank, b = 0, s % 2
                buf, mx = s_p[:, b, :], small[:, 8 * b:8 * b + 4]
                if s == 0:
                    for t in range(2):
                        own.loose(STT(buf[:, t * 30:(t + 1) * 30].rearrange("p (r n) -> p r n", r=2),
                            ps[:, bank, t * 30:(t + 1) * 30].rearrange("p (r n) -> p r n", r=2), SCALE,
                            bc_keep[:, :].rearrange("p (t n h) -> p t h n", t=2, h=8)[:, t, bass.ds(j * 2, 2), :], ALU.mult, ALU.add))
                    own.settle()
                    v.tensor_reduce(mx, buf[:, 0:60].rearrange("p (i n) -> p i n", i=4), AXX, ALU.max, negate=True).then_inc(mx_sb, 1)
                    v.engine_nop().then_inc(s_sb_, 1)
                else:
                    h0 = j * 2 + (8 if s == 3 else 0)
                    bias = bias_p[:, bass.ds(h0, 2), :]
                    own.loose(STT(buf[:, 0:512].rearrange("p (r k) -> p r k", r=2), ps[:, bank, :].rearrange("p (r k) -> p r k", r=2), SCALE,
                        bias, ALU.mult, ALU.add))
                    own.loose(STT(buf[:, 512:768].rearrange("p (r k) -> p r k", r=2), ps[:, bank + 1, 0:256].rearrange("p (r k) -> p r k", r=2), SCALE,
                        bias_p[:, bass.ds(h0, 2), P:TP], ALU.mult, ALU.add))
                    own.settle()
                    own(v.tensor_reduce(mx[:, 2:4], buf[:, 0:512].rearrange("p (i n) -> p i n", i=2), AXX, ALU.max, negate=True))
                    v.tensor_reduce(mx[:, 0:2], buf[:, 512:768].rearrange("p (i n) -> p i n", i=2), AXX, ALU.max, negate=True).then_inc(mx_sb, 1)
                    v.engine_nop().then_inc(s_sb_, 1)

            def weigh(u, j, s):
                b = s % 2
                dve.wait_ge(exp_sb, u * 4 + 4)
                if u:
                    dve.wait_ge(o_sb, u)
                sums, wt = small[:, 8 * b + 4:8 * b + 8], small[:, 16:20]
                if s == 0:
                    own(v.reciprocal(wt, sums))
                    own(TT(wt.rearrange("p (t r) -> p t r", t=2), wt.rearrange("p (t r) -> p t r", t=2),
                           cst[:, C_MASKC:C_MASKC + 2].unsqueeze(2).broadcast_to([P, 2, 2]), ALU.mult))
                else:
                    own(v.reciprocal(wt, sums))
                if s < 3:
                    own(TT(wt.rearrange("p (t r) -> p t r", t=2), wt.rearrange("p (t r) -> p t r", t=2),
                           gate_n[:, :, bass.ds(j * 6 + s, 4)][:, :, 0:4:3], ALU.mult))
                dve.wait_ge(tp_mm, u + 1)
                n = 384 if s else 256
                rows = P if s else NCMP_P
                v.tensor_copy(pT[0:rows, n:2 * n], ps[0:rows, 3, 0:n]).then_inc(pt_v, 1)
                dve.wait_ge(pv_mm, u + 1)
                out = o_n[:, :, bass.ds(j * 2 + (8 if s == 3 else 0), 2), :]
                src = ps[:, 4, 0:256].rearrange("p (t r d) -> p t r d", t=2, r=2)
                wb = wt.rearrange("p (t r) -> p t r", t=2).unsqueeze(3).broadcast_to([P, 2, 2, HD])
                if s in (0, 3):
                    TT(out, src, wb, ALU.mult).then_inc(o_sb, 1)
                else:
                    own(TT(o_part[:, :].rearrange("p (t r d) -> p t r d", t=2, r=2), src, wb, ALU.mult))
                    TT(out, out, o_part[:, :].rearrange("p (t r d) -> p t r d", t=2, r=2), ALU.add).then_inc(o_sb, 1)

            def key_half(half):
                dve.wait_ge(kv_used[1], 4 * (half + 1))
                lo = slice(half * 512, (half + 1) * 512)
                mo, se = ps[0:ROWS, (5, 7)[half], :], ps[0:ROWS, (6, 5)[half], :]
                own.loose(v.tensor_reduce(small[0:ROWS, 48 + 2 * half:50 + 2 * half], mo.rearrange("p (n k) -> p n k", k=256), AXX, ALU.add))
                own.loose(TT(half0[:, 0, :] if half == 0 else pm[:, lo], mo, biasd[:, 1, lo], ALU.add))
                own.loose(TT(half0[:, 1, :] if half == 0 else psl[:, lo], se, biasd[:, 0, lo], ALU.add))
                if half == 1:
                    own.loose(v.tensor_copy(pm[:, 0:512], half0[:, 0, :]))
                    own.loose(v.tensor_copy(psl[:, 0:512], half0[:, 1, :]))
                own.settle()
                v.engine_nop().then_inc(kev_sb, 1)

            add_bias(0, 0, 0)
            dve.wait_ge(biasd_mm, 1)
            for m in range(2):
                own.loose(v.tensor_copy(biasd[:, m, 0:1024], ps[0:ROWS, 4 + 2 * m:6 + 2 * m, :].rearrange("p a b -> p (a b)")))
                own.loose(v.tensor_copy(biasd[:, m, 1024:1025], ps[0:ROWS, 3, m:m + 1]))
            own.settle()
            v.engine_nop().then_inc(biasd_sb, 1)
            for u in range(4 * NPAIR):
                if u + 1 < 4 * NPAIR:
                    add_bias(u + 1, (u + 1) // 4, (u + 1) % 4)
                weigh(u, u // 4, u % 4)
                if u == NB:
                    key_half(0)

            dve.wait_ge(oT_mm, 1)
            dve.wait_ge(qbd_sb, 1)
            for g in range(4):
                tt, c0 = divmod(g * 4, 8)
                own.loose(v.tensor_copy(oT[:, c0:c0 + 4, tt * P:(tt + 1) * P], ps[:, g, :].rearrange("p (k t) -> p k t", k=4)))
            own.settle()
            v.engine_nop().then_inc(oT_v, 1)

            key_half(1)
            R = ROWS
            sm = small[0:R, :]
            dve.wait_ge(sd_mm, 1)
            own.loose(v.tensor_copy(sm[:, 20:23], ps[0:R, 1, 0:3]))
            own(v.tensor_copy(sm[:, 28:31], ps[0:R, 1, 8:11]))

            def drop_one(score, n, mask, tmp):
                own(v.tensor_reduce(sm[:, 44:45], score, AXX, ALU.min))
                own(TS(tmp, score, sm[:, 44:45], None, ALU.is_equal))
                own(TT(tmp, tmp, cst[0:R, C_IDX + 1:C_IDX + 1 + n], ALU.mult))
                own(v.tensor_reduce(sm[:, 45:46], tmp, AXX, ALU.max))
                own(TS(mask, cst[0:R, C_IDX + 1:C_IDX + 1 + n], sm[:, 45:46], NEG, ALU.is_equal, ALU.mult))

            own(TT(pc, ps[0:R, 0, 0:NCMP_D], biasd[:, 0, 31:1024:16], ALU.add))
            v.tensor_reduce(sm[:, 32:33], pc, AXX, ALU.max, negate=True).then_inc(dmax_sb, 1)
            drop_one(sm[:, 48:52], 4, sm[:, 52:56], sm[:, 56:60])
            own.loose(TT(pm[:, 0:1024].rearrange("p (n k) -> p n k", k=256), pm[:, 0:1024].rearrange("p (n k) -> p n k", k=256),
                   sm[:, 52:56].unsqueeze(2).broadcast_to([R, 4, 256]), ALU.add))
            own.loose(TT(pm[:, 1024:1025], sm[:, 20:21], biasd[:, 1, 1024:1025], ALU.add))
            own.settle()
            dve.wait_ge(dmax_sb, 1)
            v.tensor_reduce(sm[:, 33:34], pm, AXX, ALU.max, negate=True).then_inc(dmax_sb, 1)
            dve.wait_ge(dexp_sb, 1)
            own(v.reciprocal(sm[:, 40:41], sm[:, 36:37]))
            own(TS(pc, pc, sm[:, 40:41], None, ALU.mult))
            v.engine_nop().then_inc(imp_rd, 1)
            dve.wait_ge(imp_mm, 1)
            own(v.tensor_copy(imp[:, :], ps[0:R, 2, 0:NCMP_D]))
            own(TT(seg[:, :], imp[:, 4:60], imp[:, 3:59], ALU.add))
            own(v.tensor_reduce(blk[:, 0:14], seg[:, :].rearrange("p (n k) -> p n k", k=4), AXX, ALU.add))
            own(v.memset(blk[:, 16:32], 0.0))
            drop_one(blk[:, 0:14], 14, blk[:, 17:31], blk[:, 32:46])
            own.loose(TT(psl[:, 0:1024].rearrange("p (n k) -> p n k", k=64), psl[:, 0:1024].rearrange("p (n k) -> p n k", k=64),
                   blk[:, 16:32].unsqueeze(2).broadcast_to([R, 16, 64]), ALU.add))
            own.loose(TT(psl[:, 1024:1025], sm[:, 21:22], biasd[:, 0, 1024:1025], ALU.add))
            own.settle()
            v.tensor_reduce(sm[:, 34:35], psl, AXX, ALU.max, negate=True).then_inc(dmax_sb, 1)
            own.loose(TT(pw[:, 0:512], ps[0:R, 6, :], biasd[:, 0, 512:1024], ALU.add))
            own.loose(TT(pw[:, 512:513], sm[:, 22:23], biasd[:, 0, 1024:1025], ALU.add))
            own.settle()
            v.tensor_reduce(sm[:, 35:36], pw, AXX, ALU.max, negate=True).then_inc(dmax_sb, 1)
            dve.wait_ge(dexp_sb, 4)
            own(v.reciprocal(sm[:, 41:44], sm[:, 37:40]))
            own(TT(sm[:, 42:44], sm[:, 42:44], sm[:, 29:31], ALU.mult))
            own.loose(TS(pc, pc, sm[:, 28:29], None, ALU.mult))
            own.loose(TS(pm, pm, sm[:, 41:42], None, ALU.mult))
            own.loose(TS(psl, psl, sm[:, 42:43], None, ALU.mult))
            own.loose(TS(pw, pw, sm[:, 43:44], None, ALU.mult))
            own.settle()
            for i, p_new in enumerate((pm[:, 1024:1025], psl[:, 1024:1025], pw[:, 512:513])):
                own.loose(TS(sm[:, 64 + 8 * i:72 + 8 * i], cst[0:R, C_HM:C_HM + 8], p_new, None, ALU.mult))
            own.settle()
            v.engine_nop().then_inc(pd_sb, 1)
            dve.wait_ge(pdt_mm, 1)
            own.loose(v.tensor_copy(pTm, ps[:, 0, :].rearrange("p (g r) -> p g r", r=ROWS)))
            own.loose(v.tensor_copy(pTs, ps[:, 2, :].rearrange("p (g r) -> p g r", r=ROWS)))
            own.loose(v.tensor_copy(pTw, ps[:, 6, 0:256].rearrange("p (g r) -> p g r", r=ROWS)))
            own.loose(v.tensor_copy(pTc, ps[0:NCMP_D, 6, 256:320]))
            own.settle()
            v.engine_nop().then_inc(pdt_sb, 1)
            dve.wait_ge(pnew_mm, 1)
            own(v.tensor_copy(sm[0:NB, 96:120], ps[0:NB, 1, 16:40]))
            TT(pnz[:, :, :], sm[0:NB, 96:120].unsqueeze(1).broadcast_to([NB, NB, 24]),
               cst[0:NB, C_DIAG:C_DIAG + 8].unsqueeze(2).broadcast_to([NB, NB, 24]), ALU.mult).then_inc(pnz_sb, 1)
            first_head = PE_COLS // HD

            def weigh_pages(b):
                for half in range(2):
                    for q in (2 * half, 2 * half + 1):
                        dve.wait_ge(vp_in[q], 32 * (b + 1))
                        TT(vprod[:, 2 * (q % 2):2 * (q % 2) + 2, :].rearrange("p g (h d) -> p g h d", d=HD),
                           pages[:, 2 * q:2 * q + 2, PE_COLS:512].rearrange("p g (h d) -> p g h d", d=HD),
                           pTm[:, 2 * q:2 * q + 2, b * 8 + first_head:b * 8 + 8].unsqueeze(3).broadcast_to([P, 2, 8 - first_head, HD]),
                           ALU.mult).then_inc(vd_used[q], 1)
                    for q in (2 * half, 2 * half + 1):
                        dve.wait_ge(vd_used[q], b + 2)
                    own(TT(vtwo[:, :, :], vprod[:, 0:2, :], vprod[:, 2:4, :], ALU.add))
                    if half == 0 and b >= 2:
                        dve.wait_ge(oc_mm, b - 1)
                    if half == 0 and b:
                        own_columns(b - 1)
                    own(TT(vacc[:, 2 if half else b % 2, :], vtwo[:, 0, :], vtwo[:, 1, :], ALU.add))
                own(TT(vacc[:, b % 2, :], vacc[:, b % 2, :], vacc[:, 2, :], ALU.add))

            def own_columns(b):
                dve.wait_ge(od_mm, b + 1)
                if b >= 2:
                    dve.wait_ge(oc_mm, b - 1)
                own(TT(sel_n[:, b % 2, :], ps[0:NB, 5 + 2 * (b % 2), 0:P], cst[0:NB, C_MN:C_MN + P], ALU.mult))
                TT(sel_m[:, b % 2, :], ps[0:NB, 4 + 2 * (b % 2), :], cst[0:NB, C_MM:C_MM + 512], ALU.mult).then_inc(od_sb, 1)

            for b in range(NB):
                weigh_pages(b)
            own_columns(NB - 1)
            dve.wait_ge(oc_mm, NB)
            v.tensor_copy(oT[:, :, TP:T], ps[:, 3, 0:64].rearrange("p (b k) -> p k b", k=8)).then_inc(oTd_sb, 1)

            dve.wait_ge(mgate_sb, 2)
            dve.wait_ge(proj_sb, T_MRG + 2 + 16)
            for n in range(8):
                dve.wait_ge(w_used, W_BRANCH + n + 1)
                bank = 4 + 2 * (n % 2)
                own.loose(TT(mT[:, n, :], ps[:, bank, 0:T], feat[:, T_MRG + n, :], ALU.mult))
                own.loose(TT(mtmp[:, 0:T], ps[:, bank + 1, 0:T], feat[:, T_MRG + 8 + n, :], ALU.mult))
                own.settle()
                TT(mT[:, n, :], mT[:, n, :], mtmp[:, 0:T], ALU.add).then_inc(m_sb, 1)
                dve.wait_ge(m_sb, n + 1)
            own(v.memset(mean_var[:, :, :], 1.0))

            def half_stats(half):
                for tt in range(3):
                    r = P if tt < 2 else NB
                    own.loose(v.bn_stats(stats1[0:r, tt, 6 * half:6 * half + 6], x_n[0:r, tt, half * 512:(half + 1) * 512]))

            dve.wait_ge(x_in, 32)
            for n in range(8):
                dve.wait_ge(mixt_mm, n + 1)
                cols = slice(n * P, (n + 1) * P)
                own(STT(x_n[:, 0:2, cols], x_n[:, 0:2, cols], ALPHA, ps[:, 2 + n % 2, 0:2 * P].rearrange("p (t c) -> p t c", t=2), ALU.mult, ALU.add))
                STT(x_n[0:NB, 2, cols], x_n[0:NB, 2, cols], ALPHA, ps[0:NB, 2 + n % 2, 2 * P:3 * P], ALU.mult, ALU.add).then_inc(mix_sb, 1)
                if n % 4 == 3:
                    dve.wait_ge(mix_sb, n + 1)
                    half_stats(n // 4)
            own.settle()
            for tt in range(3):
                r = P if tt < 2 else NB
                own.loose(v.bn_aggr(mean_var[0:r, tt, :], stats1[0:r, tt, :].rearrange("p (a b) -> p a b", a=2)))
            own.settle()
            TS(dev1[:, 1, :], mean_var[:, :, 1], EPS, None, ALU.add).then_inc(var_sb, 1)
            dve.wait_ge(std_sb, 1)
            own(v.reciprocal(dev1[:, 1, :], dev1[:, 0, :]))
            for tt in range(3):
                r = P if tt < 2 else NB
                TS(x_n[0:r, tt, :], x_n[0:r, tt, :], mean_var[0:r, tt, 0:1], dev1[0:r, 1, tt:tt + 1], ALU.subtract, ALU.mult).then_inc(nrm_sb, 1)
            dve.wait_ge(ln_in, 80)
            dve.wait_ge(hT_mm, 2)
            for k in range(KD):
                TS(xT[:, k, P:TP], ps[:, 4 + k // 4, (k % 4) * P:(k % 4 + 1) * P], lnT[:, 0, k:k + 1], lnT[:, 1, k:k + 1], ALU.mult, ALU.add).then_inc(hT_sb, 1)
            dve.wait_ge(nrm_sb, 3)
            dve.wait_ge(hT_mm, 3)
            for i, op in ((0, ALU.mult), (1, ALU.add)):
                for tt in range(3):
                    r = P if tt < 2 else NB
                    x = TT(x_n[0:r, tt, :], x_n[0:r, tt, :], ln_rows[0:r, i, :], op)
                    if i == 0:
                        own.loose(x)
                    else:
                        x.then_inc(h_sb, 1)
                if i == 0:
                    own.settle()
            own(TS(alpha_id, ident, ALPHA, None, ALU.mult))
            v.engine_nop().then_inc(h_sb, 1)
            dve.wait_ge(h_sb, 4)

            norms = [1]

            def layer_norm(tt, g, done, src=None):
                r = P if tt < 2 else NB
                xr = x_n[0:r, tt, :]
                src = xr if src is None else src
                own.loose(v.bn_stats(stats[0:r, 0:6], src[:, 0:512]))
                own.loose(v.bn_stats(stats[0:r, 6:12], src[:, 512:1024]))
                own.settle()
                own(v.bn_aggr(stats[0:r, 12:14], stats[0:r, 0:12].rearrange("p (a b) -> p a b", a=2)))
                TS(stats[0:r, 14:15], stats[0:r, 13:14], EPS, None, ALU.add).then_inc(var_sb, 1)
                dve.wait_ge(std_sb, norms[0] + 1)
                norms[0] += 1
                own(v.reciprocal(stats[0:r, 14:15], stats[0:r, 15:16]))
                own(TS(xr, src, stats[0:r, 12:13], stats[0:r, 14:15], ALU.subtract, ALU.mult))
                own(TT(xr, xr, ln_rows[0:r, g, :], ALU.mult))
                TT(xr, xr, ln_rows[0:r, g + 1, :], ALU.add).then_inc(done, 1)

            def find(tt, h, c):
                r = P if tt < 2 else NB
                halves = range(2)
                carry = lambda: dve.sem_inc(dve_go, 1)
                own(v.tensor_copy(rest[0:r, :, :].rearrange("p c k -> p (c k)"), scores[0:r, bass.ds(h * 256 + tt * 2048, 256)]))
                for k in (0, 8):
                    carry()
                    for i in halves:
                        own.loose(v.max(val[0:r, i, k:k + 8], rest[0:r, i, :]))
                    own.settle()
                    carry()
                    for i in halves:
                        own.loose(v.max_index(idu[0:r, i, k:k + 8], val[0:r, i, k:k + 8], rest[0:r, i, :]))
                    own.settle()
                    if k == 0:
                        carry()
                        for i in halves:
                            own.loose(v.match_replace(rest[0:r, i, :], val[0:r, i, 0:8], rest[0:r, i, :], -3.0e38))
                        own.settle()
                own.loose(v.tensor_copy(idf[0:r], idu[0:r]))
                own(TT(cand[0:r].rearrange("p (i j) -> p i j", i=16), val[0:r, 0, :].unsqueeze(2).broadcast_to([r, 16, 16]),
                       val[0:r, 1:2, :].broadcast_to([r, 16, 16]), ALU.add))
                gv = best[0:r, c, :]
                carry()
                own(v.max(gv[:, 0:8], cand[0:r]))
                own.loose(TS(nbest[0:r, c:c + 1], gv[:, 0:1], -1.0, None, ALU.mult))
                carry()
                own(v.max_index(fpos[0:r, 0:8], gv[:, 0:8], cand[0:r]))
                carry()
                own(v.match_replace(cand[0:r], gv[:, 0:8], cand[0:r], -3.0e38))
                carry()
                own(v.max(gv[:, 8:16], cand[0:r]))
                dve.sem_inc(fsub_sb, 1)
                carry()
                own(v.max_index(fpos[0:r, 8:16], gv[:, 8:16], cand[0:r]))
                io = cst[0:r, C_IDX:C_IDX + 16].unsqueeze(1).broadcast_to([r, 16, 16])
                oh = oneh[0:r].rearrange("p (k i) -> p k i", k=16)
                for half, dst in ((0, ea), (1, eb)):
                    if half == 0:
                        own(TS(fi[0:r], fpos[0:r], 4, None, ALU.logical_shift_right))
                    else:
                        own(TS(fi[0:r], fpos[0:r], 15, None, ALU.bitwise_and))
                    own(v.tensor_copy(fif[0:r], fi[0:r]))
                    own(TT(oh, fif[0:r].unsqueeze(2).broadcast_to([r, 16, 16]), io, ALU.is_equal))
                    own(TT(oh, oh, idf[0:r, half:half + 1, :].broadcast_to([r, 16, 16]), ALU.mult))
                    own(v.tensor_reduce(dst[0:r], oh, AXX, ALU.add))
                own(STT(ea[0:r], ea[0:r], 128.0, eb[0:r], ALU.mult, ALU.add))
                own(v.tensor_copy(eidx[0:r, tt, bass.ds(h * TOPK, TOPK)], ea[0:r]))
                dve.sem_inc(e_sb, 1)

            def normalise(tt, h, c, count):
                r = P if tt < 2 else NB
                dve.wait_ge(gexp_sb, count)
                own(v.reciprocal(gsum[0:r, c:c + 1], gsum[0:r, c:c + 1]))
                own(TS(gk[0:r, tt, bass.ds(h * TOPK, TOPK)], bexp[0:r, c, :], gsum[0:r, c:c + 1], None, ALU.mult))
                dve.sem_inc(nm_sb, 1)

            def dot(g, q, turn, hrow):
                if not (isinstance(g, int) and g < GROUPS):
                    dve.wait_ge(gel_sb, g + (1 - GROUPS))
                for s in range(UNROLL):
                    slot = (q % 2) * UNROLL + s
                    dve.wait_ge(u_in[slot], turn * 16 + 16)
                    v.tensor_tensor_reduce(out=u_rows[:, slot, :], in0=u_rows[:, slot, :], in1=hrow, scale=1.0, scalar=0.0,
                                           op0=ALU.mult, op1=ALU.add, accum_out=dots[:, q, s:s + 1]).then_inc(u_used, 1)

            def head(tt, h, coming, late=0):
                for q in range(GROUPS):
                    if q % 2 == late and q // 2 < len(coming):
                        find(*coming[q // 2][0:3])
                    dot(h * GROUPS + (2 * TURN0[tt] + q), q, h * HEAD_T + (TURN0[tt] + q // 2), x_n[:, tt, :])
                for job in coming:
                    normalise(*job)

            def coming(tt, h):
                one = [(tt, h + 1, 0, found(tt, h + 1))]
                return one + [(2, h + 1, 1, h * 2 + (NH + 4))] if tt else one

            def heads(tt, lo, hi, per):
                with dve.Fori(lo, hi) as h:
                    own.enter(h, per, lo)
                    if tt == 0:
                        dve.wait_ge(sc_sb, h * 4 + 8)
                    head(tt, h, coming(tt, h))
                own.leave(hi - lo)

            dve.wait_ge(sc_sb, 4)
            find(0, 0, 0)
            normalise(0, 0, 0, 1)
            dve.wait_ge(sc_sb, 8)
            at = own.base + own.off
            head(0, 0, coming(0, 0), late=1)
            per = own.base + own.off - at
            heads(0, 1, 7, per)
            head(0, 7, [(1, 0, 0, NH + 1), (2, 0, 1, NH + 2)])
            at = own.base + own.off
            head(1, 0, coming(1, 0))
            per = own.base + own.off - at

            def tile_out(tt):
                dve.wait_ge(v_used, 8 * (TURN0[tt] + P // 8 if tt < 2 else TURNS))
                src = ps[0:NB, 0:2, :] if tt == 2 else ps[:, 4 + 2 * tt:6 + 2 * tt, :]
                layer_norm(tt, 2, y_sb, src.rearrange("p a b -> p (a b)"))

            tile_out(0)
            heads(1, 1, 7, per)
            head(1, 7, [])
            dve.wait_ge(hrep_in, 16)
            for q in range(2):
                dot(2 * TURN0[2] + q, q, TURN0[2], h_rep)
            tile_out(1)
            tile_out(2)


OUT_SHAPES = {
    "y_prompt": (TP, D), "y_sample": (NB, D), "nsa_prompt": (TP, 512), "moba_prompt": (TP, 1024),
    "win_prompt": (TP, 256), "nsa_sample": (NB, 512), "moba_sample": (NB, 1024), "win_sample": (NB, 512, 256),
}
OUT_NAMES = list(OUT_SHAPES)


def bucket(np, n):
    n = np.asarray(n)
    nf = np.maximum(n, 1).astype(np.float32)
    large = 16 + (np.log(nf / np.float32(16)) / math.log(1024 / 16) * 16).astype(np.int32)
    return np.where(n < 16, n, np.minimum(large, 31))


def shape_constants(np):
    def one_hot(dist):
        flat = np.asarray(dist).reshape(-1)
        oh = np.zeros((33, flat.size), np.float32)
        rows = np.where(flat < 0, 32, bucket(np, np.maximum(flat, 0)))
        oh[rows, np.arange(flat.size)] = 1.0
        return oh

    t = np.arange(P)
    rev = one_hot(255 - np.arange(384))
    ends = 16 * np.arange(NCMP_P) + 31
    dist_c = np.stack([[(tt * P + t) - e for e in ends] for tt in range(2)])
    onehot = np.concatenate([rev, one_hot(PAST - np.arange(PAST))], axis=1)
    c = np.zeros((P, NCONST), np.float32)
    r = np.arange(ROWS)
    c[:, C_ID:C_ID + P] = np.eye(P)
    c[:, C_ONE:C_ONE + P] = 1
    c[:, C_MASKC:C_MASKC + 2] = (dist_c[:, 0] >= 0).T
    c[:ROWS, C_HM:C_HM + 8] = (r % 8)[:, None] == np.arange(8)
    c[:ROWS, C_GSUM:C_GSUM + ROWS] = (r // 4)[:, None] == (r // 4)
    c[:ROWS, C_SELB:C_SELB + 8] = (r // 8)[:, None] == np.arange(8)
    c[:, C_IDX:C_IDX + 16] = np.arange(16)
    c[:8, C_DIAG:C_DIAG + 8] = np.eye(8)
    c[:8, C_MM:C_MM + 512] = np.arange(8)[:, None] == np.arange(512) // 64
    c[:8, C_MN:C_MN + P] = (np.arange(8) // 4)[:, None] == np.arange(P) // 64
    c[:8, C_JS:C_JS + 4] = (np.arange(8) % 4)[:, None] == np.arange(4)
    q = np.arange(24)
    c[:24, C_M24:C_M24 + 8] = (q // 6 + 4 * (q // 3 % 2))[:, None] == np.arange(8)
    c[:24, C_B24:C_B24 + 3] = (q % 3)[:, None] == np.arange(3)
    c[:, C_KRED:C_KRED + 8] = (np.arange(P) // 16)[:, None] == np.arange(8)
    return onehot, c


def kernel(**inputs):
    import numpy as np
    import concourse.bacc as bacc
    from concourse.bass_utils import run_bass_kernel_spmd as run

    i = {k: np.asarray(v) for k, v in inputs.items()}
    pair = [h for j in range(4) for h in (j, j + 4)]
    w = i["w_in"][0]
    cols = lambda lo, n: w[:, lo:lo + n]
    wq_a = cols(0, 512).reshape(D, 8, 64)[:, pair].reshape(D, 512)
    gate = cols(1280, 24).reshape(D, 8, 3)[:, pair].reshape(D, 24)
    gate = np.concatenate([gate, np.zeros((D, P - 24), np.float32)], axis=1)
    w_feat = np.concatenate([wq_a, cols(1304, 512), cols(512, 512), cols(1024, 256), cols(1816, 1024), gate, cols(2840, 2048)], axis=1)

    def tiles(m):
        k, n = m.shape
        return m.reshape(k // P, P, n // P, P).transpose(2, 1, 0, 3).reshape(n // P, P, k)

    cw = i["nsa_cmp_w"][0]
    conv = cw.reshape(2, 2, 8, 2, HD, HD).transpose(0, 3, 4, 2, 1, 5)
    wa = i["w_branch_a"][0].reshape(8, 64, D)[pair].reshape(512, D)
    branch = np.concatenate([wa, i["w_branch_b"][0]], axis=0)
    wall = np.concatenate([tiles(w_feat)[:T_MRG], conv.reshape(2, P, D), tiles(w_feat)[T_MRG:], tiles(branch), tiles(i["w_out"][0]), tiles(i["peer_wq"][0])], axis=0)

    x_all = np.concatenate([i["x_prompt"][0], i["x_sample"][:, 0]], axis=0)
    nsa = i["cache_nsa"][0]
    moba = i["cache_moba"][0]
    pool = nsa.shape[0]
    col = lambda m: m.reshape(pool, PAGE, P).transpose(0, 2, 1)
    pack_cmp = nsa[:, :, 0:2].reshape(pool, HD, 2, 2, 2, HD).transpose(0, 2, 5, 3, 4, 1).reshape(pool, P, 2 * PAGE)
    k_m = moba[:, :, 0].reshape(pool, PAGE, 4, P).transpose(0, 3, 2, 1).reshape(pool, P, 512)
    pack_k = np.concatenate([k_m, col(nsa[:, :, 2])], axis=2)
    pack_v = np.concatenate([moba[:, :, 1].reshape(pool, PAGE, 512), nsa[:, :, 3].reshape(pool, PAGE, P)], axis=2)
    win = i["state_nsa_win"][0]
    win_kT = win[:, :, 0].reshape(NB, 512, P).transpose(0, 2, 1)
    win_vr = win[:, :, 1].reshape(NB, 4, P, P).transpose(0, 2, 1, 3).reshape(NB, P, 512)
    pe = i["nsa_cmp_pe"][0].reshape(2, 16, 2, HD).transpose(2, 3, 0, 1).reshape(P, 2, 1, 16)
    rb = i["rel_bias"]
    rb_p = rb[:, pair + list(range(8, 16))]
    tab_ext = np.concatenate([rb_p, np.full((1, 16), NEG, np.float32)], axis=0)
    tab_dec = np.stack([np.tile(rb[:, 0:8], (1, NB)), np.tile(rb[:, 8:16], (1, NB))], axis=1)
    onehot, consts = shape_constants(np)
    keysT = i["peer_keys"][0].reshape(16, P, P).transpose(2, 0, 1)
    arrays = {
        "tab_ext": tab_ext, "tab_dec": tab_dec, "onehot": onehot, "consts": consts,
        "xT": x_all.T.reshape(KD, P, T).transpose(1, 0, 2).reshape(P, KD * T),
        "x_prompt": i["x_prompt"][0], "x_sample": i["x_sample"][:, 0], "wall": wall,
        "win_state": win.reshape(NB, 512, 256), "page_table": i["page_table"].reshape(1, NB * NPG),
        "pack_cmp": pack_cmp, "pack_kv": np.stack([pack_k, pack_v]), "win_kT": win_kT, "win_vr": win_vr,
        "peT": np.concatenate([pe, pe], axis=2), "keysT": keysT,
        "ln1_g": i["ln1_g"], "ln1_b": i["ln1_b"], "ln2_g": i["ln2_g"], "ln2_b": i["ln2_b"],
        "ln1_T": np.stack([i["ln1_g"].reshape(KD, P).T, i["ln1_b"].reshape(KD, P).T], axis=1),
        "peer_u": i["peer_u"][0], "peer_v": i["peer_v"][0],
    }
    nc = bacc.Bacc("TRN2", target_bir_lowering=False, num_devices=1)
    feeds, aps = {}, {}
    for name, v in arrays.items():
        v = np.ascontiguousarray(v)
        feeds[name] = v
        aps[name] = nc.dram_tensor(name, v.shape, mybir.dt.from_np(v.dtype), kind="ExternalInput").ap()
    for name, shape in OUT_SHAPES.items():
        aps[name] = nc.dram_tensor(name, shape, F32, kind="ExternalOutput").ap()
    hybrid_layer(nc, aps)
    r = run(nc, [feeds], core_ids=[0]).results[0]
    return (
        r["y_prompt"].reshape(1, TP, D), r["y_sample"].reshape(NB, 1, D),
        r["nsa_prompt"].reshape(1, 1, TP, 4, 2, 64), r["moba_prompt"].reshape(1, 1, TP, 2, 8, 64),
        r["win_prompt"].reshape(1, 1, TP, 2, 2, 64), r["nsa_sample"].reshape(1, NB, 1, 4, 2, 64),
        r["moba_sample"].reshape(1, NB, 1, 2, 8, 64), r["win_sample"].reshape(1, NB, 512, 2, 2, 64),
    )
```
